# Optimizing a Trainium2 kernel written in Bass

```python
import math
import jax, jax.numpy as jnp
from jax import lax
import numpy as np

D_MODEL = 1024
BATCH = 1
SEQ = 1024
DEPTH = 2

EPS = 1e-6
PLE_DIM = 256
D_FF = 4 * D_MODEL
N_EVEN = (DEPTH + 1) // 2
N_ODD = DEPTH // 2

S5_WIDTH = D_MODEL // 2
S5_GROUP = 16
S5_GROUPS = S5_WIDTH // S5_GROUP
S5_STATE = 64

HG_WIDTH = D_MODEL // 2
HG_HEADS = 4
HG_DK = HG_WIDTH // HG_HEADS
HG_DV = HG_WIDTH // HG_HEADS
HG_CHUNK = 64

EVEN_IN = S5_WIDTH + 4 * HG_WIDTH

N_Q_HEADS = 16
N_KV_HEADS = 4
HEAD_DIM = D_MODEL // N_Q_HEADS
Q_PER_KV = N_Q_HEADS // N_KV_HEADS
WINDOW = 128
ATT_BLOCK = WINDOW
ODD_IN = (N_Q_HEADS + 2 * N_KV_HEADS) * HEAD_DIM

kernel_name = "hybrid_s5_hgrn2_swa_sink_trunk"

def rms_norm(x, g):
    xf = x.astype(jnp.float32)
    y = xf * lax.rsqrt(jnp.mean(xf * xf, axis=-1, keepdims=True) + EPS)
    return (y * g.astype(jnp.float32)).astype(x.dtype)

def s5_mixer(u, lam_re, lam_im, log_dt, b_re, b_im, c_re, c_im, d_skip, w_glu, b_glu):
    f32 = jnp.float32
    bsz, L, _ = u.shape
    uf = u.astype(f32).reshape(bsz, L, S5_GROUPS, S5_GROUP)
    lr = jnp.minimum(lam_re.astype(f32), -1e-4)
    li = lam_im.astype(f32)
    dt = jnp.exp(log_dt.astype(f32))[:, None]
    mag = jnp.exp(lr * dt)
    ar = mag * jnp.cos(li * dt)
    ai = mag * jnp.sin(li * dt)
    den = lr * lr + li * li
    xr = ar - 1.0
    zr = (xr * lr + ai * li) / den
    zi = (ai * lr - xr * li) / den
    br = b_re.astype(f32)
    bi = b_im.astype(f32)
    bbar_re = zr[..., None] * br - zi[..., None] * bi
    bbar_im = zr[..., None] * bi + zi[..., None] * br
    bu_re = jnp.einsum('blgh,gph->blgp', uf, bbar_re)
    bu_im = jnp.einsum('blgh,gph->blgp', uf, bbar_im)
    a_re = jnp.broadcast_to(ar, bu_re.shape)
    a_im = jnp.broadcast_to(ai, bu_im.shape)

    def combine(e1, e2):
        ar1, ai1, br1, bi1 = e1
        ar2, ai2, br2, bi2 = e2
        return (ar2 * ar1 - ai2 * ai1,
                ar2 * ai1 + ai2 * ar1,
                ar2 * br1 - ai2 * bi1 + br2,
                ar2 * bi1 + ai2 * br1 + bi2)

    _, _, s_re, s_im = lax.associative_scan(combine, (a_re, a_im, bu_re, bu_im), axis=1)
    y = (jnp.einsum('blgp,ghp->blgh', s_re, c_re.astype(f32))
         - jnp.einsum('blgp,ghp->blgh', s_im, c_im.astype(f32))
         + d_skip.astype(f32) * uf)
    z = jax.nn.gelu(y.reshape(bsz, L, S5_WIDTH))
    out = z * jax.nn.sigmoid(z @ w_glu.astype(f32) + b_glu.astype(f32))
    return out.astype(u.dtype)

def hgrn2_mixer(q, f_logit, inp, g, lb, head_norm):
    f32 = jnp.float32
    bsz, L, _ = q.shape
    nc = L // HG_CHUNK
    lbf = lb.astype(f32)
    zf = f_logit.astype(f32)
    log_f = jnp.logaddexp(jnp.log(jnp.maximum(lbf, 1e-30)),
                          jnp.log1p(-lbf) + jax.nn.log_sigmoid(zf))
    k = (1.0 - lbf) * jax.nn.sigmoid(-zf)

    def to_chunks(t, d):
        return t.astype(f32).reshape(bsz, nc, HG_CHUNK, HG_HEADS, d).transpose(1, 0, 3, 2, 4)

    qc = to_chunks(q, HG_DK)
    kc = to_chunks(k, HG_DK)
    vc = to_chunks(inp, HG_DV)
    gc = to_chunks(log_f, HG_DK)
    causal = jnp.tril(jnp.ones((HG_CHUNK, HG_CHUNK), dtype=bool))

    def step(S, xs):
        q_c, k_c, v_c, g_c = xs
        b = jnp.cumsum(g_c, axis=2)
        o_inter = jnp.einsum('bhtk,bhkv->bhtv', q_c * jnp.exp(b), S)
        diff = b[:, :, :, None, :] - b[:, :, None, :, :]
        decay = jnp.exp(jnp.where(causal[None, None, :, :, None], diff, -jnp.inf))
        att = jnp.einsum('bhtk,bhtsk,bhsk->bhts', q_c, decay, k_c)
        o = o_inter + jnp.einsum('bhts,bhsv->bhtv', att, v_c)
        b_last = b[:, :, -1:, :]
        S_new = (jnp.exp(b_last[:, :, 0, :])[..., None] * S
                 + jnp.einsum('bhsk,bhsv->bhkv', k_c * jnp.exp(b_last - b), v_c))
        return S_new, o

    S0 = jnp.zeros((bsz, HG_HEADS, HG_DK, HG_DV), f32)
    _, o = lax.scan(step, S0, (qc, kc, vc, gc))
    o = o.transpose(1, 0, 3, 2, 4).reshape(bsz, L, HG_HEADS, HG_DV)
    o = o * lax.rsqrt(jnp.mean(o * o, axis=-1, keepdims=True) + EPS) * head_norm.astype(f32)
    o = o.reshape(bsz, L, HG_WIDTH) * jax.nn.silu(g.astype(f32))
    return o.astype(q.dtype)

def swa_sink_attention(q, k, v, sinks):
    f32 = jnp.float32
    bsz, L = q.shape[0], q.shape[1]
    nb = L // ATT_BLOCK
    qb = q.reshape(bsz, nb, ATT_BLOCK, N_KV_HEADS, Q_PER_KV, HEAD_DIM)

    def window_blocks(t):
        tp = jnp.pad(t, ((0, 0), (ATT_BLOCK, 0), (0, 0), (0, 0)))
        tb = tp.reshape(bsz, nb + 1, ATT_BLOCK, N_KV_HEADS, HEAD_DIM)
        return jnp.concatenate([tb[:, :-1], tb[:, 1:]], axis=2)

    kw = window_blocks(k)
    vw = window_blocks(v)
    scale = 1.0 / math.sqrt(HEAD_DIM)
    scores = jnp.einsum('bntkgd,bnskd->bnkgts', qb, kw).astype(f32) * scale
    t_loc = jnp.arange(ATT_BLOCK)[:, None] + ATT_BLOCK
    s_loc = jnp.arange(2 * ATT_BLOCK)[None, :]
    dist = t_loc - s_loc
    valid = (dist >= 0) & (dist < WINDOW)
    key_pos = jnp.arange(nb)[:, None] * ATT_BLOCK + jnp.arange(2 * ATT_BLOCK)[None, :] - ATT_BLOCK
    valid = valid[None, :, :] & (key_pos >= 0)[:, None, :]
    slopes = jnp.exp2(-8.0 * jnp.arange(1, N_Q_HEADS + 1, dtype=f32) / N_Q_HEADS)
    slopes = slopes.reshape(N_KV_HEADS, Q_PER_KV)
    scores = scores - slopes[:, :, None, None] * dist.astype(f32)
    scores = jnp.where(valid[None, :, None, None, :, :], scores, -jnp.inf)
    sink = sinks.astype(f32).reshape(N_KV_HEADS, Q_PER_KV)[None, None, :, :, None, None]
    m = jnp.maximum(jnp.max(scores, axis=-1, keepdims=True), sink)
    pr = jnp.exp(scores - m)
    pr = pr / (jnp.sum(pr, axis=-1, keepdims=True) + jnp.exp(sink - m))
    out = jnp.einsum('bnkgts,bnskd->bntkgd', pr.astype(v.dtype), vw)
    return out.reshape(bsz, L, N_Q_HEADS * HEAD_DIM)

def setup_inputs(seed: int = 0) -> dict:
    key = jax.random.key(seed)
    ks = jax.random.split(key, 32)
    f32 = jnp.float32

    def nrm(k, shape, scale):
        return jax.random.normal(k, shape, f32) * scale

    def gain(k, shape):
        return 1.0 + 0.02 * jax.random.normal(k, shape, f32)

    lam_im0 = jnp.pi * jnp.arange(S5_STATE, dtype=f32)
    return {
        "x": jax.random.normal(ks[0], (BATCH, SEQ, D_MODEL), f32),
        "p": jax.random.normal(ks[1], (DEPTH, BATCH, SEQ, PLE_DIM), f32),
        "mix_norm": gain(ks[2], (DEPTH, D_MODEL)),
        "mlp_norm": gain(ks[3], (DEPTH, D_MODEL)),
        "ple_norm": gain(ks[4], (DEPTH, D_MODEL)),
        "final_norm": gain(ks[5], (D_MODEL,)),
        "w_in_even": nrm(ks[6], (N_EVEN, D_MODEL, EVEN_IN), D_MODEL ** -0.5),
        "w_out_even": nrm(ks[7], (N_EVEN, S5_WIDTH + HG_WIDTH, D_MODEL), (S5_WIDTH + HG_WIDTH) ** -0.5),
        "s5_lam_re": -0.5 + 0.01 * jax.random.normal(ks[8], (N_EVEN, S5_GROUPS, S5_STATE), f32),
        "s5_lam_im": lam_im0 + 0.01 * jax.random.normal(ks[9], (N_EVEN, S5_GROUPS, S5_STATE), f32),
        "s5_log_dt": jax.random.uniform(ks[10], (N_EVEN, S5_GROUPS), f32,
                                        minval=math.log(1e-3), maxval=math.log(1e-1)),
        "s5_b_re": nrm(ks[11], (N_EVEN, S5_GROUPS, S5_STATE, S5_GROUP), (2 * S5_GROUP) ** -0.5),
        "s5_b_im": nrm(ks[12], (N_EVEN, S5_GROUPS, S5_STATE, S5_GROUP), (2 * S5_GROUP) ** -0.5),
        "s5_c_re": nrm(ks[13], (N_EVEN, S5_GROUPS, S5_GROUP, S5_STATE), S5_STATE ** -0.5),
        "s5_c_im": nrm(ks[14], (N_EVEN, S5_GROUPS, S5_GROUP, S5_STATE), S5_STATE ** -0.5),
        "s5_d": nrm(ks[15], (N_EVEN, S5_GROUPS, S5_GROUP), 1.0),
        "s5_w_glu": nrm(ks[16], (N_EVEN, S5_WIDTH, S5_WIDTH), S5_WIDTH ** -0.5),
        "s5_b_glu": nrm(ks[17], (N_EVEN, S5_WIDTH), 0.01),
        "hgrn_lb_logits": nrm(ks[18], (N_EVEN, HG_WIDTH), 1.0),
        "hgrn_norm": gain(ks[19], (N_EVEN, HG_HEADS, HG_DV)),
        "w_qkv_odd": nrm(ks[20], (N_ODD, D_MODEL, ODD_IN), D_MODEL ** -0.5),
        "w_o_odd": nrm(ks[21], (N_ODD, N_Q_HEADS * HEAD_DIM, D_MODEL), (N_Q_HEADS * HEAD_DIM) ** -0.5),
        "attn_sinks": nrm(ks[22], (N_ODD, N_Q_HEADS), 0.5),
        "w_mlp_in": nrm(ks[23], (DEPTH, D_MODEL, D_FF), D_MODEL ** -0.5),
        "w_mlp_out": nrm(ks[24], (DEPTH, D_FF, D_MODEL), D_FF ** -0.5),
        "w_ple_up": nrm(ks[25], (DEPTH, PLE_DIM, D_MODEL), PLE_DIM ** -0.5),
        "w_ple_gate": nrm(ks[26], (DEPTH, D_MODEL, D_MODEL), D_MODEL ** -0.5),
    }

def reference(x, p, mix_norm, mlp_norm, ple_norm, final_norm, w_in_even, w_out_even,
              s5_lam_re, s5_lam_im, s5_log_dt, s5_b_re, s5_b_im, s5_c_re, s5_c_im, s5_d,
              s5_w_glu, s5_b_glu, hgrn_lb_logits, hgrn_norm, w_qkv_odd, w_o_odd, attn_sinks,
              w_mlp_in, w_mlp_out, w_ple_up, w_ple_gate):
    bsz, L, _ = x.shape
    lb_sm = jax.nn.softmax(hgrn_lb_logits.astype(jnp.float32), axis=0)
    lower_bounds = jnp.cumsum(lb_sm, axis=0) - lb_sm[0:1]
    h = x
    for i in range(DEPTH):
        j = i // 2
        hn = rms_norm(h, mix_norm[i])
        if i % 2 == 0:
            proj = hn @ w_in_even[j]
            u, q_b, f_b, i_b, g_b = jnp.split(
                proj, [S5_WIDTH, S5_WIDTH + HG_WIDTH, S5_WIDTH + 2 * HG_WIDTH,
                       S5_WIDTH + 3 * HG_WIDTH], axis=-1)
            y_a = s5_mixer(u, s5_lam_re[j], s5_lam_im[j], s5_log_dt[j], s5_b_re[j], s5_b_im[j],
                           s5_c_re[j], s5_c_im[j], s5_d[j], s5_w_glu[j], s5_b_glu[j])
            y_b = hgrn2_mixer(q_b, f_b, i_b, g_b, lower_bounds[j], hgrn_norm[j])
            h = h + jnp.concatenate([y_a, y_b], axis=-1) @ w_out_even[j]
        else:
            proj = hn @ w_qkv_odd[j]
            nq = N_Q_HEADS * HEAD_DIM
            nkv = N_KV_HEADS * HEAD_DIM
            q = proj[..., :nq].reshape(bsz, L, N_Q_HEADS, HEAD_DIM)
            k = proj[..., nq:nq + nkv].reshape(bsz, L, N_KV_HEADS, HEAD_DIM)
            v = proj[..., nq + nkv:].reshape(bsz, L, N_KV_HEADS, HEAD_DIM)
            h = h + swa_sink_attention(q, k, v, attn_sinks[j]) @ w_o_odd[j]
        hn = rms_norm(h, mlp_norm[i])
        h = h + jnp.square(jax.nn.relu(hn @ w_mlp_in[i])) @ w_mlp_out[i]
        hn = rms_norm(h, ple_norm[i])
        h = h + (p[i] @ w_ple_up[i]) * jax.nn.sigmoid(hn @ w_ple_gate[i])
    return rms_norm(h, final_norm)


_drawn_inputs = setup_inputs


def setup_inputs(seed=0):
    import zlib

    import numpy as np

    out = dict(_drawn_inputs(seed))
    spreads = {}
    factors = {'mlp_norm': 2.781,
     'ple_norm': 64.0,
     'final_norm': 7.346,
     's5_lam_re': 64.0,
     's5_lam_im': 23.16,
     's5_log_dt': 24.032,
     's5_b_re': 32.536,
     's5_b_im': 32.552,
     's5_c_re': 32.472,
     's5_c_im': 32.624,
     's5_b_glu': 64.0,
     'hgrn_norm': 7.271,
     'attn_sinks': 16.102}
    for name, (base, spread) in spreads.items():
        noise = np.random.default_rng([zlib.crc32(name.encode()), seed]).standard_normal(out[name].shape)
        drawn = base * np.exp(spread * noise) if base else spread * noise
        out[name] = __import__('jax').numpy.asarray(drawn.astype(out[name].dtype))
    for name, factor in factors.items():
        out[name] = (out[name] * factor).astype(out[name].dtype)
    return out
```

```python
from contextlib import ExitStack, contextmanager

import numpy as np

import concourse.bass as bass
from concourse import mybir

F32, F32R = mybir.dt.float32, mybir.dt.float32r
ALU, ACT = mybir.AluOpType, mybir.ActivationFunctionType
X = mybir.AxisListType.X

P = 128
D, T, FF, PLE = 1024, 1024, 4096, 256
KT = D // P
NB = T // P
HALF = 512
EPS = 1e-6
S5W, GRP, STATES = 512, 16, 64
GROUPS, PAIRS = 32, 16
L = 8
CH = T // L
HEADS = 4
LEVELS = [64, 32, 16, 8, 4, 2, 1]
HG_STEPS, AT_STEPS = 22, 36
QH, KVH, HD = 16, 4, 64
FAR = 1.0e32
CREDIT = 1
TWO_PI = 6.283185307179586
MAGIC = 12582912.0

SLAB = dict(u=0, heads=4, glu=20, out=22, mlp0=30, gate0=94, up0=102, qkv=104, wo=116, mlp1=124, gate1=188, up1=196)
UNIT = dict(u=0, heads=4, glu=20, out=24, mlp0=32, gate0=96, up0=104, qkv=112, wo=124, mlp1=132, gate1=196, up1=204)
ROW = dict(mix=0, mlp=16, ple=32, final=48, head_norm=56, b_glu=60, lb=64, d=68, lam_re=72, lam_im=88)
N_ROWS = 104


class Own:

    def __init__(self, eng, sem):
        self.eng, self.sem, self.n, self.taken = eng, sem, 0, 0

    def __call__(self, ins):
        ins.then_inc(self.sem, 1)
        self.n = self.n + 1
        self.taken += 1
        self.eng.wait_ge(self.sem, self.n)

    @contextmanager
    def loop(self, count, steps):
        base, outer = self.n, self.taken
        with self.eng.Fori(0, count) as i:
            self.n, self.taken = i * steps + base, 0
            yield i
        assert self.taken == steps, (self.taken, steps)
        self.n, self.taken = base + count * steps, outer + count * steps


def build(nc, a, out):
    ctx = ExitStack()
    base = 16512

    def at(name, shape, dt, offset):
        return nc.alloc_sbuf_tensor_at(name, shape, dt, offset=offset)

    K = 1024
    H_AT, XAH_AT, XAL_AT, XBH_AT, XBL_AT = (base + i * 32 * K for i in range(5))
    RAW_AT = base + 160 * K
    W_AT = RAW_AT + 8 * K
    MISC_AT = W_AT + 16 * K

    H = at("residual", [P, KT, T], F32, H_AT)
    XAh, XAl = at("x_hi", [P, KT, T], F32R, XAH_AT), at("x_lo", [P, KT, T], F32R, XAL_AT)
    XBh, XBl = at("mid_hi", [P, KT, T], F32R, XBH_AT), at("mid_lo", [P, KT, T], F32R, XBL_AT)
    RAW = at("w_raw", [P, 2, KT * P], F32, RAW_AT)
    WH, WL = at("w_hi", [P, 2, KT * P], F32R, W_AT), at("w_lo", [P, 2, KT * P], F32R, W_AT + 8 * K)
    RSTD = at("rstd", [P, T], F32, MISC_AT)
    ST = [at(f"stage{i}", [P, T], F32, MISC_AT + (1 + i) * 4 * K) for i in range(4)]
    SUMSQ, SQ = ST[3], ST[2]
    small_at = [MISC_AT + 20 * K]

    def small(name, shape):
        n = -(-int(np.prod(shape[1:])) * 4 // 32) * 32
        o = small_at[0]
        small_at[0] += n
        assert small_at[0] <= 229368, small_at[0]
        return at(name, shape, F32, o)

    ident, ones = small("identity", [P, P]), small("ones", [P, P])
    COLS = small("vectors", [P, N_ROWS])
    dist = small("distance", [P, 2 * P])
    sink, slope = small("sinks", [P, QH]), small("neg_slopes", [P, QH])
    log_dt = small("s5_log_dt", [P, GROUPS])
    keep, floor_ = small("one_minus_lb", [P, HEADS]), small("lb_floor", [P, HEADS])
    sm = small("softmax_stats", [P, 8, 4])
    phase = small("s5_phase", [P, 6, PAIRS])

    def col(name, i):
        return COLS[:, ROW[name] + i:ROW[name] + i + 1]

    U = at("s5_u", [P, GROUPS, CH], F32, H_AT)
    TOEP = at("s5_toeplitz", [P, GROUPS, P], F32, H_AT + 16 * K)
    EW = at("s5_end_weights", [P, PAIRS, 2, P], F32, XBH_AT)
    YS = at("s5_y_chunks", [P, GROUPS, CH], F32, XBH_AT)
    BA = at("s5_ba", [P, 2, PAIRS, L, GRP], F32, XBH_AT + 16 * K)
    GK = at("s5_kernel", [GRP, GROUPS, P], F32, XBH_AT + 16 * K)
    CR = at("s5_state", [P, 2, PAIRS, CH], F32, XBH_AT + 16 * K)
    ROT = at("s5_rotation", [P, 2, PAIRS, CH], F32, XBL_AT)
    CA = at("s5_ca", [P, 2, PAIRS, L, GRP], F32, XBL_AT + 16 * K)
    CROW = at("s5_c_rows", [P, 2, 2, P], F32, XBL_AT)
    BRAW = at("s5_b", [P, 2, PAIRS, GRP], F32, XBL_AT + 2 * K)
    BB = at("s5_bbar", [P, 2, PAIRS, GRP], F32, XBL_AT + 4 * K)
    C0 = at("s5_c", [P, 2, PAIRS, GRP], F32, XBL_AT + 6 * K)
    PW = at("s5_powers", [P, 2, PAIRS, L + 1], F32, XBL_AT + 8 * K)
    PR = at("s5_params", [P, 28, PAIRS], F32, XBL_AT + 10 * K)
    PT1 = at("s5_tmp", [P, 1024], F32, XBL_AT + 12 * K)
    YT = at("s5_y", [P, 4, T], F32, H_AT)
    UT = at("s5_ut", [P, 4, T], F32, H_AT + 16 * K)

    XS = at("x_tokens", [P, NB, D], F32, XBH_AT)
    ROWS = at("vector_rows", [N_ROWS, P], F32, MISC_AT + 4 * K)

    hg = XAH_AT
    FQIG = at("hg_fqig", [P, 4, T], F32, hg)
    LVL = at("hg_levels", [P, 7, T], F32, hg + 16 * K)
    BC = at("hg_cumulative", [P, T], F32, hg + 44 * K)
    KK = at("hg_k", [P, T], F32, hg + 48 * K)
    QB = at("hg_q_decayed", [P, T], F32, hg + 52 * K)
    KD = at("hg_k_decayed", [P, T], F32, hg + 56 * K)
    OUTH = at("hg_out", [P, T], F32, hg + 60 * K)
    MASK = at("hg_masks", [P, 8, P], F32, H_AT + 16 * K)
    MP = at("hg_masked", [P, 2, 8, P], F32, H_AT + 20 * K)
    VT = at("hg_v_tokens", [P, 2, P], F32, H_AT + 28 * K)
    KDT = at("hg_kd_tokens", [P, 2, P], F32, H_AT + 29 * K)
    AT = at("hg_att", [P, 2, P], F32, H_AT + 30 * K)
    SS = at("hg_state", [P, P], F32, H_AT + 31 * K)
    TA = at("hg_tmp_a", [P, T], F32, H_AT + 0)
    TB = at("hg_tmp_b", [P, T], F32, H_AT + 4 * K)
    TC = at("hg_tmp_c", [P, T], F32, H_AT + 8 * K)
    TD = at("hg_tmp_d", [P, T], F32, H_AT + 12 * K)

    AQ = at("at_q", [P, 2, T], F32, XAH_AT)
    AK = at("at_k", [P, T], F32, XAH_AT + 8 * K)
    AV = at("at_v", [HD, T], F32, XAH_AT + 12 * K)
    AVT = at("at_v_tokens", [P, NB, HD], F32, XAH_AT + 16 * K)
    BIAS = at("at_bias", [P, 4, 2 * P], F32, XAH_AT + 18 * K)
    SC = at("at_scores", [P, 2, 4, 2 * P], F32, XAH_AT + 22 * K)
    PT = at("at_probs_t", [P, 2, 2, 4, P], F32, XAL_AT)

    PTh, PTl = at("p_hi", [P, 2, T], F32R, XBH_AT), at("p_lo", [P, 2, T], F32R, XBH_AT + 8 * K)
    PIN = at("p_tokens", [P, NB, PLE], F32, XBH_AT + 16 * K)
    GATE = at("gate", [P, KT, T], F32, XBL_AT)
    OT = at("out_tokens", [P, 2, D], F32, XBL_AT)

    def dram(name, shape):
        return nc.dram_tensor(name, shape, F32, kind="Internal").ap()

    h_dram = dram("residual_dram", [D, T])
    u_dram = dram("u_dram", [S5W, T])
    y_dram = dram("y_dram", [S5W, T])
    fqig_dram = dram("fqig_dram", [HEADS * 4 * P, T])
    qkv_dram = dram("qkv_dram", [12 * P, T])

    with ctx:
        PS = ctx.enter_context(nc.psum_tensor("ps", [P, 8, HALF], F32))
        ACC = [PS[:, 0:2, :], PS[:, 2:4, :]]

        def flat(ap):
            return ap.rearrange("p a b -> p (a b)")

        def sem(name):
            return ctx.enter_context(nc.semaphore(name))

        names = """acc_done acc_free acc_free_act w_hi_done w_ready x_hi_done x_ready mid_hi_done mid_ready
        h_ready sq_done sq_used sumsq_ready ss_done ss_read rcp_done rstd_done relu_sq_done
        consts_ready rows_loaded cols_done cols_ready sinks_loaded x_tr_done x_tr_dve x_tr_act
        dve_step act_step pool_step act_passed pool_passed pe_passed h_spilled h_restored
        s5_raw_loaded s5_c_tr s5_dve s5_act s5_ba_ready s5_ca_ready s5_ew_tr s5_ew_copied s5_g_done s5_g_copied
        s5_t_zeroed s5_t_loaded s5_u_loaded s5_end_done s5_end_read s5_states_ready s5_y_done s5_y_copied s5_y_stored
        s5_yt_loaded lb_in lb_exp glu_tanh_in glu_tanh glu_zz glu_sig masks_ready
        hg_loaded hg_dve hg_act hg_pool hg_tr hg_tr_copied hg_lvl_done hg_lvl_read hg_att hg_o_done hg_o_copied
        hg_ds_done hg_state hg_y_ready
        hg_ss hg_ss_read hg_head_done dist_ready slopes_ready
        at_q_loaded at_vt_done at_vt_copied at_qk_done at_scored at_max at_exp at_den at_norm at_pt_done at_pt_copied at_o_done at_o_hi at_o_done_lo
        p_loaded p_tr p_hi p_ready gate_done fin_ready fin_tr fin_copied""".split()
        S = {n: sem(n) for n in names}
        w_loaded = [sem(f"w_loaded{i}") for i in range(2)]
        spilled = [sem(f"spilled{i}") for i in range(2)]
        x_loaded = [sem(f"x_loaded{i}") for i in range(NB)]
        out_stored = [sem(f"out_stored{i}") for i in range(2)]

        def free_of(u):
            if 4 <= u < 20:
                return S["acc_free_act"], u - 3
            return S["acc_free"], (u + 1 if u < 4 else u - 15)

        block = ctx.enter_context(nc.Block())

        @block.sync
        def _(sp):
            def load(b, need, src):
                if need is not None:
                    sp.wait_ge(S["w_ready"], need)
                dst = RAW[:, b, :].rearrange("p (k n) -> p k n", n=src.shape[-1])
                sp.dma_start(dst, src).then_inc(w_loaded[b], 16)

            def cols(w, c):
                return w[:, c].rearrange("(k p) n -> p k n", p=P)

            def run(s0, n, w, c0=0):
                with sp.Fori(0, n // 2) as i:
                    for b in range(2):
                        load(b, i * 2 + (s0 + b - 1), cols(w, bass.ds(i * 2 * P + (c0 + b * P), P)))

            def mlp(s0, i):
                w_in, w_out = a["w_mlp_in"][i], a["w_mlp_out"][i]
                with sp.Fori(0, 4) as c:
                    with sp.Fori(0, 4) as m:
                        for b in range(2):
                            load(b, c * 16 + m * 2 + (s0 + b - 1), cols(w_in, bass.ds(c * 1024 + m * 256 + b * P, P)))
                    with sp.Fori(0, 4) as m:
                        for b in range(2):
                            src = w_out[bass.ds(c * 1024, 1024), bass.ds(m * 256 + b * P, P)]
                            load(b, c * 16 + m * 2 + (s0 + 8 + b - 1), src.rearrange("(k p) n -> p k n", p=P))

            def ple_up(s0, i):
                for s in range(2):
                    src = a["w_ple_up"][i][:, s * HALF:(s + 1) * HALF].rearrange("(k p) n -> p k n", p=P)
                    load(s, s0 + s - 1, src)

            w_in = a["w_in_even"][0]
            for t in range(NB):
                sp.dma_start(XS[:, t, :], a["x"][0, t * P:(t + 1) * P, :]).then_inc(x_loaded[t], 16)
                if t in (1, 3):
                    b = (t - 1) // 2
                    load(b, None, cols(w_in, slice(b * P, (b + 1) * P)))
            for s in range(2, 4):
                load(s % 2, s - 1, cols(w_in, slice(s * P, (s + 1) * P)))
            with sp.Fori(0, HEADS) as hd:
                for j, c0 in enumerate((2 * S5W, S5W, 3 * S5W, 4 * S5W)):
                    load(j % 2, hd * 4 + (4 + j - 1), cols(w_in, bass.ds(hd * P + c0, P)))
            for s in range(2):
                src = a["s5_w_glu"][0][:, s * 256:(s + 1) * 256].rearrange("(k p) n -> p k n", p=P)
                load(s, 20 + s - 1, src)
            w = a["w_out_even"][0]
            for b in range(2):
                load(b, 22 + b - 1, cols(w, slice(b * P, (b + 1) * P)))
            for b in range(2):
                sp.wait_ge(spilled[b], 16 * 10)
            sp.wait_ge(S["acc_done"], 20)
            sp.dma_start(FQIG[:, :, :], fqig_dram[0:4 * P, :].rearrange("(j p) t -> p j t", p=P)).then_inc(S["hg_loaded"], 16)
            with sp.Fori(1, HEADS) as hd:
                sp.wait_ge(S["hg_head_done"], hd)
                src = fqig_dram[bass.ds(hd * 4 * P, 4 * P), :].rearrange("(j p) t -> p j t", p=P)
                sp.dma_start(FQIG[:, :, :], src).then_inc(S["hg_loaded"], 16)
            sp.wait_ge(S["hg_head_done"], HEADS)
            sp.wait_ge(S["h_spilled"], 16)
            sp.dma_start(H[:, :, :], h_dram.rearrange("(k p) t -> p k t", p=P)).then_inc(S["h_restored"], 16)
            with sp.Fori(1, 4) as i:
                for b in range(2):
                    load(b, i * 2 + (22 + b - 1), cols(w, bass.ds(i * 256 + b * P, P)))
            mlp(SLAB["mlp0"], 0)
            run(SLAB["gate0"], 8, a["w_ple_gate"][0])
            ple_up(SLAB["up0"], 0)
            run(SLAB["qkv"], 12, a["w_qkv_odd"][0])
            w = a["w_o_odd"][0]
            for b in range(2):
                load(b, SLAB["wo"] + b - 1, cols(w, slice(b * P, (b + 1) * P)))
            with sp.Fori(0, KVH) as g:
                for b in range(2):
                    sp.wait_ge(spilled[b], 16 * 16)
                sp.wait_ge(S["at_vt_done"], g + CREDIT)
                sp.wait_ge(S["at_qk_done"], g * NB + CREDIT)
                sp.dma_start(AQ[:, :, :], qkv_dram[bass.ds(g * 256, 256), :].rearrange("(j p) t -> p j t", p=P)).then_inc(S["at_q_loaded"], 16)
                for r in range(2):
                    sp.dma_start(AK[r * HD:(r + 1) * HD, :], qkv_dram[bass.ds(g * HD + 1024, HD), :]).then_inc(S["at_q_loaded"], 16)
                sp.dma_start(AV[:, :], qkv_dram[bass.ds(g * HD + 1280, HD), :]).then_inc(S["at_q_loaded"], 16)
            with sp.Fori(1, 4) as i:
                for b in range(2):
                    load(b, i * 2 + (SLAB["wo"] + b - 1), cols(w, bass.ds(i * 256 + b * P, P)))
            mlp(SLAB["mlp1"], 1)
            run(SLAB["gate1"], 8, a["w_ple_gate"][1])
            ple_up(SLAB["up1"], 1)
            for n in range(NB):
                sp.wait_ge(S["fin_copied"], n + 1)
                sp.dma_start(out[0, n * P:(n + 1) * P, :], OT[:, n % 2, :]).then_inc(out_stored[n % 2], 16)
            for b in range(2):
                sp.wait_ge(out_stored[b], 16 * NB // 2)

        @block.gpsimd
        def _(pool):
            own = Own(pool, S["pool_step"])

            own(pool.memset(ident[:, :], 1.0))
            own(pool.affine_select(out=ident[:, :], in_=ident[:, :], compare_op=ALU.is_equal, fill=0.0,
                                   base=0, pattern=[[-1, P]], channel_multiplier=1))
            pool.memset(ones[:, :], 1.0).then_inc(S["consts_ready"], 1)
            own(pool.iota(dist[:, :], [[-1, 2 * P]], base=P, channel_multiplier=1, allow_small_or_imprecise_dtypes=True))
            own(pool.affine_select(out=dist[:, :], in_=dist[:, :], compare_op=ALU.is_ge, fill=FAR,
                                   base=P, pattern=[[-1, 2 * P]], channel_multiplier=1))
            pool.affine_select(out=dist[:, :], in_=dist[:, :], compare_op=ALU.is_ge, fill=FAR,
                               base=-1, pattern=[[1, 2 * P]], channel_multiplier=-1).then_inc(S["dist_ready"], 1)
            for h in range(QH):
                ins = pool.memset(slope[:, h:h + 1], -2.0 ** (-8.0 * (h + 1) / QH))
            ins.then_inc(S["slopes_ready"], 1)

            def split(b, s, visit, used):
                pool.wait_ge(w_loaded[b], visit)
                if used is not None:
                    pool.wait_ge(S["acc_done"], used)
                pool.nop().then_inc(S["pool_passed"], 1)
                pool.tensor_copy(WH[:, b, :], RAW[:, b, :]).then_inc(S["w_hi_done"], 1)
                pool.wait_ge(S["w_hi_done"], s)
                pool.tensor_tensor(WL[:, b, :], RAW[:, b, :], WH[:, b, :].bitcast(F32), ALU.subtract).then_inc(S["w_ready"], 1)

            def one(s, used):
                split(s % 2, s + 1, 16 * (s // 2 + 1), used)

            def run(s0, u0, n):
                with pool.Fori(0, n // 2) as i:
                    for b in range(2):
                        split(b, i * 2 + (s0 + b + 1), i * 16 + 16 * (s0 // 2 + 1), i * 2 + (u0 + b - 1))

            for s in range(2):
                one(s, None)
            for s in range(2, 4):
                one(s, s - 1)
            run(4, 4, 16)
            one(20, 19)
            one(21, 20)
            pool.wait_ge(S["glu_zz"], 4)
            own(pool.memset(MASK[:, :, :], 1.0))
            for l, w in enumerate(LEVELS):
                m = MASK[:, l, :]
                n = P // (2 * w)
                own(pool.affine_select(out=m, in_=m, compare_op=ALU.is_ge, fill=0.0, base=0,
                                       pattern=[[-2 * w, n], [0, 2 * w]], channel_multiplier=1))
                own(pool.affine_select(out=m, in_=m, compare_op=ALU.is_ge, fill=0.0, base=w - 1,
                                       pattern=[[2 * w, n], [0, 2 * w]], channel_multiplier=-1))
                own(pool.affine_select(out=m, in_=m, compare_op=ALU.is_ge, fill=0.0, base=-w,
                                       pattern=[[0, n], [1, 2 * w]], channel_multiplier=0))
            pool.affine_select(out=MASK[:, 7, :], in_=MASK[:, 7, :], compare_op=ALU.is_equal, fill=0.0,
                               base=0, pattern=[[-1, P]], channel_multiplier=1).then_inc(S["masks_ready"], 1)
            one(22, 22)
            one(23, 24)
            with pool.Fori(0, HEADS) as hd:
                for l, w in enumerate(LEVELS):
                    v = LVL[:, l, :].rearrange("p (n two w) -> p n two w", two=2, w=w)
                    k = KK[:, :].rearrange("p (n two w) -> p n two w", two=2, w=w)
                    q = FQIG[:, 1, :].rearrange("p (n two w) -> p n two w", two=2, w=w)
                    pool.wait_ge(S["hg_act"], hd * 14 + (5 + l))
                    pool.tensor_tensor(v[:, :, 0, :], v[:, :, 0, :], k[:, :, 0, :], ALU.mult)
                    pool.tensor_tensor(v[:, :, 1, :], v[:, :, 1, :], q[:, :, 1, :], ALU.mult).then_inc(S["hg_pool"], 1)
            with pool.Fori(0, 3) as i:
                for b in range(2):
                    split(b, i * 2 + (24 + b + 1), i * 16 + 16 * 13, i * 2 + (26 + b - 1))
            run(SLAB["mlp0"], UNIT["mlp0"], 64)
            run(SLAB["gate0"], UNIT["gate0"], 8)

            def ups(name, nxt, n_next):
                s, u = SLAB[name], UNIT[name]
                one(s, u - 1)
                one(s + 1, u)
                if nxt:
                    s, u = SLAB[nxt], UNIT[nxt]
                    one(s, u - 4)
                    one(s + 1, u)
                    with pool.Fori(1, n_next // 2) as i:
                        for b in range(2):
                            split(b, i * 2 + (s + b + 1), i * 16 + 16 * (s // 2 + 1), i * 2 + (u + b - 1))

            ups("up0", "qkv", 12)
            for s in range(SLAB["wo"], SLAB["wo"] + 2):
                one(s, s - SLAB["wo"] + UNIT["wo"] - 1)
            with pool.Fori(0, KVH) as g:
                for n in range(NB):
                    lo = P if n == 0 else 0
                    pr = SC[:, n % 2, :, lo:]
                    den = sm[:, 4 + n % 2, :].unsqueeze(2).to_broadcast([P, 4, 2 * P - lo])
                    pool.wait_ge(S["at_den"], g * NB + (n + 1))
                    pool.tensor_tensor(pr, pr, den, ALU.mult).then_inc(S["at_norm"], 1)
            with pool.Fori(1, 4) as i:
                for b in range(2):
                    split(b, i * 2 + (SLAB["wo"] + b + 1), i * 16 + 16 * (SLAB["wo"] // 2 + 1), i * 2 + (UNIT["wo"] + b - 1))
            run(SLAB["mlp1"], UNIT["mlp1"], 64)
            run(SLAB["gate1"], UNIT["gate1"], 8)
            ups("up1", None, 0)

        @block.tensor
        def _(pe):
            for name in "hg_o_done at_vt_done at_qk_done at_pt_done".split():
                pe.nop().then_inc(S[name], CREDIT)
            def unit(acc, wh, wl, xh, xl, kts=KT, k0=0, ready=None):
                for k in range(kts):
                    if ready is not None:
                        pe.wait_ge(*ready(k))
                    for w, x in ((wh, xh), (wh, xl), (wl, xh)):
                        for h in range(2):
                            ins = pe.matmul(acc[:, h, :], w[:, k, :], x[:, k0 + k, h * HALF:(h + 1) * HALF],
                                            start=(k == 0 and w is wh and x is xh), stop=(k == kts - 1 and w is wl))
                ins.then_inc(S["acc_done"], 1)

            whs = [WH[:, b, :].rearrange("p (k n) -> p k n", n=P) for b in range(2)]
            wls = [WL[:, b, :].rearrange("p (k n) -> p k n", n=P) for b in range(2)]

            def one(s, u, x, **kw):
                pe.wait_ge(S["w_ready"], s + 1)
                if u >= 2:
                    pe.wait_ge(*free_of(u - 2))
                unit(ACC[u % 2], whs[s % 2], wls[s % 2], *x, **kw)

            def run(s0, u0, n, x):
                with pe.Fori(0, n // 2) as i:
                    for b in range(2):
                        pe.wait_ge(S["w_ready"], i * 2 + (s0 + b + 1))
                        pe.wait_ge(free_of(u0)[0], i * 2 + (free_of(u0)[1] + b - 2))
                        unit(ACC[b], whs[b], wls[b], *x)

            XA, XB = (XAh, XAl), (XBh, XBl)

            def x_ready(norm):
                return lambda k: (S["x_ready"], 8 * norm + k + 1)

            def sum_squares(n):
                pe.wait_ge(S["sumsq_ready"], n + 1)
                for h in range(2):
                    ins = pe.matmul(PS[:, 4 + h, :], ones[:, :], SUMSQ[:, h * HALF:(h + 1) * HALF], start=True, stop=True)
                ins.then_inc(S["ss_done"], 1)

            def first_two(s, u, norm):
                one(s, u, XA, ready=x_ready(norm))
                sum_squares(norm)
                one(s + 1, u + 1, XA)

            pe.wait_ge(S["consts_ready"], 1)
            pe.wait_ge(S["pool_step"], 2)
            pe.wait_ge(S["rows_loaded"], 16 * 10)
            pe.transpose(PS[:, 0, 0:N_ROWS], ROWS[:, :], ident[0:N_ROWS, 0:N_ROWS]).then_inc(S["cols_done"], 1)
            for t in range(NB):
                pe.wait_ge(x_loaded[t], 16)
                for h in range(2):
                    n = 2 * t + h
                    if t >= 2:
                        pe.wait_ge(S["x_tr_act" if h else "x_tr_dve"], t - 1)
                    for j in range(4):
                        k = 4 * h + j
                        ins = pe.transpose(PS[:, 4 + n % 4, j * P:(j + 1) * P], XS[:, t, k * P:(k + 1) * P], ident[:, :])
                    ins.then_inc(S["x_tr_done"], 1)
            pe.wait_ge(S["x_tr_dve"], NB)
            pe.wait_ge(S["x_tr_act"], NB)
            pe.wait_ge(S["cols_ready"], 1)
            first_two(0, 0, 0)
            for s in range(2, 4):
                one(s, s, XA)
            one(4, 4, XA)
            one(5, 5, XA)
            pe.wait_ge(S["ss_read"], 1)
            pe.wait_ge(S["s5_raw_loaded"], 16 * 13)
            for h in range(2):
                for r in range(2):
                    j = 2 * h + r
                    ins = pe.transpose(PS[:, 4, j * P:(j + 1) * P], CROW[:, h, r, :], ident[:, :])
            ins.then_inc(S["s5_c_tr"], 1)
            one(6, 6, XA)
            one(7, 7, XA)
            pe.wait_ge(S["s5_ba_ready"], 1)
            for n in range(8):
                if n == 0:
                    pe.wait_ge(S["s5_ca_ready"], 1)
                if n >= 4:
                    pe.wait_ge(S["s5_ew_copied"], n - 3)
                for j in range(4):
                    q, r = 2 * n + j // 2, j % 2
                    ins = pe.transpose(PS[:, 4 + n % 4, j * P:(j + 1) * P],
                                       BA[:, r, q, :, :].rearrange("p j h -> p (j h)"), ident[:, :])
                ins.then_inc(S["s5_ew_tr"], 1)
            def group(n, j):
                return 8 * (n // 2) + n % 2 + 2 * j

            for n in range(8):
                if n < 4:
                    pe.wait_ge(S["s5_ew_copied"], n + 5)
                else:
                    pe.wait_ge(S["s5_g_copied"], n - 3)
                for j in range(4):
                    g = group(n, j)
                    q, rows = g // 2, slice(STATES * (g % 2), STATES * (g % 2 + 1))
                    o = PS[0:GRP, 4 + n % 4, j * P:(j + 1) * P]
                    for r in range(2):
                        pe.matmul(o[:, 0:GRP], BB[rows, r, q, :], C0[rows, r, q, :], start=(r == 0), stop=(r == 1))
                    for r in range(2):
                        ins = pe.matmul(o[:, GRP:P], BB[rows, r, q, :],
                                        CA[rows, r, q, 0:L - 1, :].rearrange("p j h -> p (j h)"), start=(r == 0), stop=(r == 1))
                ins.then_inc(S["s5_g_done"], 1)
            one(8, 8, XA)
            one(9, 9, XA)
            pe.wait_ge(S["s5_u_loaded"], 16 * 8)
            pe.wait_ge(S["s5_g_copied"], 8)
            for half in range(2):
                if half:
                    one(10, 10, XA)
                    one(11, 11, XA)
                    pe.wait_ge(S["s5_end_read"], 1)
                for qq in range(8):
                    q = 8 * half + qq
                    for two in range(2):
                        for r in range(2):
                            o = PS[STATES * two:STATES * (two + 1), 4 + 2 * r + qq // 4, (qq % 4) * P:(qq % 4 + 1) * P]
                            ins = pe.matmul(o, EW[:, q, r, STATES * two:STATES * (two + 1)], U[:, 2 * q + two, :], start=True, stop=True)
                ins.then_inc(S["s5_end_done"], 1)
            one(12, 12, XA)
            one(13, 13, XA)
            pe.wait_ge(S["s5_t_loaded"], 16 * 8)
            pe.wait_ge(S["s5_states_ready"], 1)
            pe.wait_ge(S["s5_end_read"], 2)
            for n in range(8):
                if n >= 4:
                    pe.wait_ge(S["s5_y_copied"], n - 3)
                for j in range(4):
                    g = group(n, j)
                    q, rows = g // 2, slice(STATES * (g % 2), STATES * (g % 2 + 1))
                    o = PS[:, 4 + n % 4, j * P:(j + 1) * P]
                    pe.matmul(o, TOEP[:, g, :], U[:, g, :], start=True, stop=False)
                    for r in range(2):
                        ins = pe.matmul(o[:, 1:CH], CA[rows, r, q, :, :].rearrange("p j h -> p (j h)"),
                                        CR[rows, r, q, 0:CH - 1], start=False, stop=(r == 1))
                ins.then_inc(S["s5_y_done"], 1)
            run(14, 14, 6, XA)
            for s in range(2):
                pe.wait_ge(S["w_ready"], 21 + s)
                wh = WH[:, s, :].rearrange("p (k n) -> p k n", n=256)
                wl = WL[:, s, :].rearrange("p (k n) -> p k n", n=256)
                for j in range(2):
                    u = 20 + 2 * s + j
                    pe.wait_ge(*free_of(u - 2))
                    unit(ACC[j], wh[:, :, j * P:(j + 1) * P], wl[:, :, j * P:(j + 1) * P], XBh, XBl, kts=4, k0=4,
                         ready=(lambda k: (S["mid_ready"], k + 1)) if u == 20 else None)
            for u in (22, 23):
                pe.wait_ge(*free_of(u))
            pe.wait_ge(S["s5_y_copied"], 8)
            pe.wait_ge(S["masks_ready"], 1)
            with pe.Fori(0, HEADS) as hd:
                pe.wait_ge(S["hg_pool"], hd * 7 + 7)
                pe.wait_ge(S["hg_dve"], hd * 14 + 14)
                pe.wait_ge(S["hg_ss_read"], hd + CREDIT)
                for c in range(NB):
                    t = slice(c * P, (c + 1) * P)
                    b = c % 2
                    e = hd * NB + c
                    pe.wait_ge(S["hg_tr_copied"], e + CREDIT)
                    pe.transpose(PS[:, 3, 0:P], FQIG[:, 2, t], ident[:, :])
                    pe.transpose(PS[:, 3, P:2 * P], KD[:, t], ident[:, :]).then_inc(S["hg_tr"], 1)
                    pe.wait_ge(S["hg_lvl_read"], hd * NB + c + (CREDIT - 1)) if c >= 1 else pe.wait_ge(S["hg_lvl_read"], hd * NB + CREDIT)
                    for l in range(8):
                        o = PS[:, 4 + 2 * b + l // 4, (l % 4) * P:(l % 4 + 1) * P]
                        if l < 7:
                            ins = pe.matmul(o, LVL[:, l, t], LVL[:, l, t], start=True, stop=True)
                        else:
                            ins = pe.matmul(o, KK[:, t], FQIG[:, 1, t], start=True, stop=True)
                    ins.then_inc(S["hg_lvl_done"], 1)
                    pe.wait_ge(S["hg_tr_copied"], e + (1 + CREDIT))
                    pe.wait_ge(S["hg_state"], e + CREDIT)
                    pe.matmul(PS[:, 2, 0:P], KDT[:, b, :], VT[:, b, :], start=True, stop=True).then_inc(S["hg_ds_done"], 1)
                    pe.wait_ge(S["hg_o_copied"], e + (CREDIT - 1)) if c >= 1 else pe.wait_ge(S["hg_o_copied"], e + CREDIT)
                    if c:
                        pe.matmul(PS[:, b, 0:P], SS[:, :], QB[:, t], start=True, stop=False).then_inc(S["hg_o_done"], 1)
                        pe.wait_ge(S["hg_att"], e + 1)
                        pe.matmul(PS[:, b, 0:P], VT[:, b, :], AT[:, b, :], start=False, stop=True).then_inc(S["hg_o_done"], 1)
                    else:
                        pe.wait_ge(S["hg_att"], e + 1)
                        pe.matmul(PS[:, b, 0:P], VT[:, b, :], AT[:, b, :], start=True, stop=True).then_inc(S["hg_o_done"], 2)
                pe.wait_ge(S["hg_act"], hd * 14 + 12)
                pe.wait_ge(S["hg_lvl_read"], hd * NB + NB + CREDIT)
                for h in range(2):
                    ins = pe.matmul(PS[:, 4 + h, :], ones[:, :], TA[:, h * HALF:(h + 1) * HALF], start=True, stop=True)
                ins.then_inc(S["hg_ss"], 1)
            pe.wait_ge(S["hg_o_copied"], HEADS * NB + CREDIT)
            pe.wait_ge(S["mid_ready"], 12)
            one(22, 24, XB)
            one(23, 25, XB)
            run(24, 26, 6, XB)

            def mlp(name, norm, mid0):
                s, u = SLAB[name], UNIT[name]
                first_two(s, u, norm)
                run(s + 2, u + 2, 6, XA)

                def down_two(c):
                    for b in range(2):
                        pe.wait_ge(S["w_ready"], c * 16 + (s + 8 + b + 1))
                        pe.wait_ge(S["acc_free"], c * 16 + (free_of(u + 8)[1] + b - 2))
                        ready = (lambda k: (S["mid_ready"], c * 8 + (mid0 + k + 1))) if b == 0 else None
                        unit(ACC[b], whs[b], wls[b], *XB, ready=ready)

                def two(off, x):
                    for b in range(2):
                        pe.wait_ge(S["w_ready"], off + (s + b + 1))
                        pe.wait_ge(S["acc_free"], off + (free_of(u)[1] + b - 2))
                        unit(ACC[b], whs[b], wls[b], *x)

                with pe.Fori(0, 3) as c:
                    down_two(c)
                    with pe.Fori(0, 3) as m:
                        two(c * 16 + m * 2 + 10, XB)
                    with pe.Fori(0, 4) as m:
                        two(c * 16 + m * 2 + 16, XA)
                for b in range(2):
                    ready = (lambda k: (S["mid_ready"], mid0 + 24 + k + 1)) if b == 0 else None
                    one(s + 56 + b, u + 56 + b, XB, ready=ready)
                run(s + 58, u + 58, 6, XB)

            def embed(i, norm):
                s, u = SLAB[f"gate{i}"], UNIT[f"gate{i}"]
                first_two(s, u, norm)
                pe.wait_ge(S["p_loaded"], 16 * (i + 1))
                pe.wait_ge(S["ss_read"], norm + 1)
                for k in range(2):
                    for t in range(NB):
                        ins = pe.transpose(PS[:, 4 + 2 * k + t // 4, (t % 4) * P:(t % 4 + 1) * P],
                                           PIN[:, t, k * P:(k + 1) * P], ident[:, :])
                    ins.then_inc(S["p_tr"], 1)
                run(s + 2, u + 2, 6, XA)
                s, u = SLAB[f"up{i}"], UNIT[f"up{i}"]
                for n in range(2):
                    pe.wait_ge(S["w_ready"], s + n + 1)
                    wh = WH[:, n, :].rearrange("p (k n) -> p k n", n=HALF)
                    wl = WL[:, n, :].rearrange("p (k n) -> p k n", n=HALF)
                    if n == 0:
                        pe.wait_ge(S["p_ready"], 2 * (i + 1))
                    for j in range(4):
                        v = u + 4 * n + j
                        pe.wait_ge(*free_of(v - 2))
                        unit(ACC[v % 2], wh[:, :, j * P:(j + 1) * P], wl[:, :, j * P:(j + 1) * P], PTh, PTl, kts=2)

            mlp("mlp0", 1, 12)
            embed(0, 2)
            first_two(SLAB["qkv"], UNIT["qkv"], 3)
            run(SLAB["qkv"] + 2, UNIT["qkv"] + 2, 10, XA)
            for u in (122, 123):
                pe.wait_ge(*free_of(u))
            pe.wait_ge(S["ss_read"], 4)
            with pe.Fori(0, KVH) as g:
                pe.wait_ge(S["at_q_loaded"], g * 64 + 64)
                pe.wait_ge(S["at_o_done_lo"], g * NB + CREDIT)
                pe.nop().then_inc(S["pe_passed"], 1)
                for n in range(NB):
                    ins = pe.transpose(PS[:, 3, n * HD:(n + 1) * HD], AV[:, n * P:(n + 1) * P], ident[0:HD, 0:HD])
                ins.then_inc(S["at_vt_done"], 1)
                pe.wait_ge(S["at_vt_copied"], g + 1)

                def scores(n):
                    lo = P if n == 0 else 0
                    b = n % 2
                    e = g * NB + n
                    pe.wait_ge(S["at_scored"], e + (CREDIT - 1)) if n >= 1 else pe.wait_ge(S["at_scored"], e + CREDIT)
                    for j in range(4):
                        rows = slice(HD * (j % 2), HD * (j % 2 + 1))
                        o = PS[:, 4 + 2 * b + j % 2, (j // 2) * 256 + lo:(j // 2 + 1) * 256]
                        ins = pe.matmul(o, AQ[rows, j // 2, n * P:(n + 1) * P],
                                        AK[rows, (n - 1) * P + lo:(n + 1) * P], start=True, stop=True)
                    ins.then_inc(S["at_qk_done"], 1)

                def outputs(n):
                    b = n % 2
                    e = g * NB + n
                    halves = (1,) if n == 0 else (0, 1)
                    pe.wait_ge(S["at_norm"], e + 1)
                    pe.wait_ge(S["at_pt_copied"], e + CREDIT)
                    for h in halves:
                        for j in range(4):
                            ins = pe.transpose(PS[:, h, j * P:(j + 1) * P], SC[:, b, j, h * P:(h + 1) * P], ident[:, :])
                    ins.then_inc(S["at_pt_done"], 1)
                    pe.wait_ge(S["at_pt_copied"], e + (1 + CREDIT))
                    pe.wait_ge(S["at_o_done_lo"], e + (CREDIT - 1)) if n >= 1 else pe.wait_ge(S["at_o_done_lo"], e + CREDIT)
                    for r in range(2):
                        for h in halves:
                            ins = pe.matmul(PS[HD * r:HD * (r + 1), 2 + b, 0:256], AVT[:, n - 1 + h, :],
                                            PT[:, b, h, 2 * r:2 * r + 2, :], start=(h == halves[0]), stop=(h == 1))
                    ins.then_inc(S["at_o_done"], 1)

                scores(0)
                for n in range(1, NB):
                    scores(n)
                    outputs(n - 1)
                outputs(NB - 1)
            pe.wait_ge(S["at_o_done_lo"], KVH * NB + CREDIT)
            one(SLAB["wo"], UNIT["wo"], XB)
            one(SLAB["wo"] + 1, UNIT["wo"] + 1, XB)
            run(SLAB["wo"] + 2, UNIT["wo"] + 2, 6, XB)
            mlp("mlp1", 4, 44)
            embed(1, 5)
            sum_squares(6)
            pe.wait_ge(S["ss_read"], 7)
            for u in (210, 211):
                pe.wait_ge(*free_of(u))
            pe.wait_ge(S["fin_ready"], 8)
            for n in range(NB):
                for h in range(2):
                    e = 2 * n + h
                    if e >= 4:
                        pe.wait_ge(S["fin_copied"], n - 1)
                    for j in range(4):
                        ins = pe.transpose(PS[:, 4 + e % 4, j * P:(j + 1) * P], H[:, 4 * h + j, n * P:(n + 1) * P], ident[:, :])
                    ins.then_inc(S["fin_tr"], 1)

        @block.scalar
        def _(act):
            for name in "hg_tr_copied hg_o_copied at_pt_copied".split():
                act.nop().then_inc(S[name], CREDIT)
            own = Own(act, S["act_step"])

            def fn(o, i, f, **kw):
                return act.activation(o, i, f, **kw)

            def wait(s, n):
                act.wait_ge(S[s], n)
                settle()

            def settle():
                act.nop().then_inc(S["act_passed"], 1)

            def rows(name, n, src):
                act.dma_start(ROWS[ROW[name]:ROW[name] + n, :], src).then_inc(S["rows_loaded"], 16)

            rows("mix", 16, a["mix_norm"].rearrange("i (k p) -> (i k) p", p=P))
            rows("mlp", 16, a["mlp_norm"].rearrange("i (k p) -> (i k) p", p=P))
            rows("ple", 16, a["ple_norm"].rearrange("i (k p) -> (i k) p", p=P))
            rows("final", 8, a["final_norm"].rearrange("(k p) -> k p", p=P))
            rows("head_norm", 4, a["hgrn_norm"][0])
            rows("b_glu", 4, a["s5_b_glu"][0].rearrange("(k p) -> k p", p=P))
            rows("lb", 4, a["hgrn_lb_logits"][0].rearrange("(k p) -> k p", p=P))
            rows("d", 4, a["s5_d"][0].rearrange("(k g) h -> k (g h)", k=4))
            rows("lam_re", 16, a["s5_lam_re"][0].rearrange("(q two) p -> q (two p)", two=2))
            rows("lam_im", 16, a["s5_lam_im"][0].rearrange("(q two) p -> q (two p)", two=2))
            act.dma_start(sink[:, :], a["attn_sinks"][0].unsqueeze(0).to_broadcast([P, QH])).then_inc(S["sinks_loaded"], 16)
            act.dma_start(log_dt[:, :], a["s5_log_dt"][0].unsqueeze(0).to_broadcast([P, GROUPS])).then_inc(S["s5_raw_loaded"], 16)
            for r, (b, c) in enumerate((("s5_b_re", "s5_c_re"), ("s5_b_im", "s5_c_im"))):
                for two in range(2):
                    act.dma_start(BRAW[two * STATES:(two + 1) * STATES, r, :, :],
                                  a[b][0].rearrange("(q two) p h -> two p q h", two=2)[two]).then_inc(S["s5_raw_loaded"], 16)
                    for h in range(2):
                        act.dma_start(CROW[:, h, r, two * STATES:(two + 1) * STATES],
                                      a[c][0].rearrange("(h q two) c p -> h two q c p", h=2, two=2)[h, two])\
                            .then_inc(S["s5_raw_loaded"], 16)
            for t in range(NB):
                act.wait_ge(S["x_tr_done"], 2 * t + 2)
                fn(H[:, 4:8, t * P:(t + 1) * P], PS[:, 4 + (2 * t + 1) % 4, :].rearrange("p (k t) -> p k t", t=P), ACT.Copy)\
                    .then_inc(S["x_tr_act"], 1)

            def finish(norm, gain, g0, split=True):
                with act.Fori(0, KT) as m:
                    hm = H[:, bass.ds(m, 1), :].rearrange("p a t -> p (a t)")
                    wait("h_ready", m + (8 * norm + 1))
                    if split:
                        fn(XAh[:, bass.ds(m, 1), :].rearrange("p a t -> p (a t)"), hm, ACT.Identity,
                           scale=COLS[:, bass.ds(m + (ROW[gain] + g0), 1)]).then_inc(S["x_hi_done"], 1)
                    wait("sq_used", m + 8 * norm + CREDIT)
                    fn(SQ[:, :], hm, ACT.Square).then_inc(S["sq_done"], 1)

            def root(n):
                act.wait_ge(S["rcp_done"], n + 1)
                fn(RSTD[:, :], ST[1][:, :], ACT.Sqrt).then_inc(S["rstd_done"], 1)

            finish(0, "mix", 0)
            act.dma_start(h_dram.rearrange("(k p) t -> p k t", p=P), H[:, :, :]).then_inc(S["h_spilled"], 16)
            root(0)
            for u in range(4):
                act.wait_ge(S["acc_free"], u + 1)
                act.dma_start(u_dram[u * P:(u + 1) * P, :], ST[u % 2][:, :]).then_inc(spilled[u % 2], 16)
            act.wait_ge(S["lb_in"], 1)
            fn(floor_[:, :], floor_[:, :], ACT.Exp).then_inc(S["lb_exp"], 1)
            p = lambda i: PR[:, i, :]
            act.wait_ge(S["cols_ready"], 1)
            act.wait_ge(S["s5_dve"], 1)
            act.wait_ge(S["s5_raw_loaded"], 16 * 13)
            for two in range(2):
                half = slice(two * STATES, (two + 1) * STATES)
                own(fn(PR[half, 1, :], log_dt[half, two::2], ACT.Exp))
            act.nop().then_inc(S["s5_act"], 1)
            act.wait_ge(S["s5_dve"], 2)
            fn(p(3), p(2), ACT.Exp)
            fn(p(4), p(2), ACT.Exp, scale=float(L)).then_inc(S["s5_act"], 1)
            act.wait_ge(S["s5_dve"], 3)
            fn(p(6), p(5), ACT.Sin)
            fn(p(7), p(5), ACT.Sin, scale=0.5).then_inc(S["s5_act"], 1)

            def head_unit(u):
                b = u % 2
                act.wait_ge(S["acc_done"], u + 1)
                act.wait_ge(spilled[b], 16 * (u // 2))
                fn(ST[b][:, :], flat(ACC[b]), ACT.Copy).then_inc(S["acc_free_act"], 1)
                act.wait_ge(S["acc_free_act"], u - 3)
                act.dma_start(fqig_dram[(u - 4) * P:(u - 3) * P, :], ST[b][:, :]).then_inc(spilled[b], 16)

            for u in range(4, 8):
                head_unit(u)
            for n in range(8):
                act.wait_ge(S["s5_ew_tr"], n + 1)
                fn(EW[:, 2 * n:2 * n + 2, :, :].rearrange("p q r m -> p (q r m)"), PS[:, 4 + n % 4, :], ACT.Copy)\
                    .then_inc(S["s5_ew_copied"], 1)

            def four(n):
                g0 = 8 * (n // 2) + n % 2
                return slice(g0, g0 + 7, 2)

            for n in range(8):
                act.wait_ge(S["s5_g_done"], n + 1)
                if n == 0:
                    act.wait_ge(S["s5_ew_tr"], 8)
                fn(GK[:, four(n), :], PS[0:GRP, 4 + n % 4, :].rearrange("p (g m) -> p g m", m=P), ACT.Copy)\
                    .then_inc(S["s5_g_copied"], 1)
            for b in range(2):
                act.wait_ge(spilled[b], 16 * 4)
            act.wait_ge(S["h_spilled"], 16)
            for j in range(L):
                act.dma_start(U[j * GRP:(j + 1) * GRP, :, :],
                              u_dram[:, j * CH:(j + 1) * CH].rearrange("(g h) c -> h g c", h=GRP)).then_inc(S["s5_u_loaded"], 16)
            act.wait_ge(S["s5_g_copied"], 8)
            act.wait_ge(S["s5_t_zeroed"], 1)
            for j in range(L):
                act.dma_start(TOEP[j * GRP:(j + 1) * GRP, :, j * GRP:P], GK[:, :, 0:P - j * GRP]).then_inc(S["s5_t_loaded"], 16)
            for u in range(8, 14):
                head_unit(u)
            for n in range(8):
                act.wait_ge(S["s5_y_done"], n + 1)
                fn(YS[:, four(n), :], PS[:, 4 + n % 4, :].rearrange("p (g m) -> p g m", m=P), ACT.Copy)\
                    .then_inc(S["s5_y_copied"], 1)
            act.wait_ge(S["s5_y_copied"], 8)
            for j in range(L):
                act.dma_start(y_dram[:, j * CH:(j + 1) * CH].rearrange("(g h) c -> h g c", h=GRP),
                              YS[j * GRP:(j + 1) * GRP, :, :]).then_inc(S["s5_y_stored"], 16)
            head_unit(14)
            head_unit(15)
            head_unit(16)
            act.wait_ge(S["s5_y_stored"], 16 * 8)
            act.dma_start(YT[:, :, :], y_dram.rearrange("(k p) t -> p k t", p=P)).then_inc(S["s5_yt_loaded"], 16)
            act.dma_start(UT[:, :, :], u_dram.rearrange("(k p) t -> p k t", p=P)).then_inc(S["s5_yt_loaded"], 16)
            for k in range(4):
                act.wait_ge(S["glu_tanh_in"], k + 1)
                fn(ST[3][:, :], ST[2][:, :], ACT.Tanh).then_inc(S["glu_tanh"], 1)
                act.wait_ge(S["glu_zz"], k + 1)
                fn(XBh[:, 4 + k, :].rearrange("p (c j) -> p j c", j=L), YT[:, k, :].rearrange("p (j c) -> p j c", j=L),
                   ACT.Copy, scale=0.5).then_inc(S["mid_hi_done"], 1)
                if k < 3:
                    head_unit(17 + k)
            for m in range(4):
                act.wait_ge(S["acc_done"], 21 + m)
                if m:
                    act.wait_ge(S["mid_ready"], 4 + m)
                fn(ST[2][:, :], flat(ACC[m % 2]), ACT.Sigmoid, bias=col("b_glu", m)).then_inc(S["glu_sig"], 1)
                act.wait_ge(S["glu_zz"], 5 + m)
                fn(XBh[:, m, :], ST[3][:, :], ACT.Copy).then_inc(S["mid_hi_done"], 1)
            with own.loop(HEADS, 5) as hd:
                def want(n):
                    act.wait_ge(S["hg_dve"], hd * 14 + n)

                def tell(ins):
                    ins.then_inc(S["hg_act"], 1)

                want(1)
                own(fn(TB[:, :], TA[:, :], ACT.Exp, scale=-1.0))
                own(fn(TC[:, :], TB[:, :], ACT.Ln, bias=1.0))
                tell(fn(TC[:, :], TC[:, :], ACT.Exp, scale=-1.0))
                act.wait_ge(S["hg_act"], hd * 14 + 1)
                settle()
                tell(fn(TD[:, :], TC[:, :], ACT.Ln, scale=keep[:, bass.ds(hd, 1)], bias=floor_[:, bass.ds(hd, 1)]))
                want(3)
                tell(fn(TC[:, :], BC[:, :], ACT.Exp))
                want(4)
                tell(fn(TD[:, :], TD[:, :], ACT.Exp, scale=-1.0))
                for l in range(7):
                    want(7 + l)
                    tell(fn(LVL[:, l, :], LVL[:, l, :], ACT.Exp, scale=-1.0))
                for c in range(NB):
                    e = hd * NB + c
                    b = c % 2
                    act.wait_ge(S["hg_tr"], e + 1)
                    act.wait_ge(S["hg_o_done"], e * 2 + (CREDIT - 2) if c else e * 2 + CREDIT)
                    fn(VT[:, b, :], PS[:, 3, 0:P], ACT.Copy)
                    fn(KDT[:, b, :], PS[:, 3, P:2 * P], ACT.Copy).then_inc(S["hg_tr_copied"], 1)
                    act.wait_ge(S["hg_o_done"], e * 2 + (2 + CREDIT))
                    fn(OUTH[:, c * P:(c + 1) * P], PS[:, b, 0:P], ACT.Copy).then_inc(S["hg_o_copied"], 1)
                act.wait_ge(S["hg_o_copied"], hd * NB + NB + CREDIT)
                tell(fn(TA[:, :], OUTH[:, :], ACT.Square))
                act.wait_ge(S["hg_state"], hd * NB + NB + CREDIT)
                own(fn(TC[:, :], FQIG[:, 3, :], ACT.Exp, scale=-1.0))
                own(fn(TC[:, :], TC[:, :], ACT.Ln, bias=1.0))
                tell(fn(TC[:, :], TC[:, :], ACT.Exp, scale=-1.0))
                act.wait_ge(S["hg_ss_read"], hd + (1 + CREDIT))
                own(fn(TD[:, :], TD[:, :], ACT.Ln))
                tell(fn(TD[:, :], TD[:, :], ACT.Exp, scale=-0.5))
                act.wait_ge(S["hg_y_ready"], hd + 1)
                settle()
                fn(XBh[:, bass.ds(hd + 4, 1), :].rearrange("p a t -> p (a t)"), TD[:, :], ACT.Copy).then_inc(S["mid_hi_done"], 1)
            finish(1, "mlp", 0)

            def hidden(u, m):
                act.wait_ge(S["acc_free"], u)
                own(fn(ST[1][:, :], ST[0][:, :], ACT.Square))
                settle()
                fn(XBh[:, bass.ds(m, 1), :].rearrange("p a t -> p (a t)"), ST[1][:, :], ACT.Copy).then_inc(S["mid_hi_done"], 1)

            def mlp(name, norm_after, gain, g0):
                f0 = free_of(UNIT[name])[1]
                start = own.n
                with act.Fori(0, 4) as c:
                    with act.Fori(0, 8) as m:
                        own.n = c * 8 + m + start
                        hidden(c * 16 + m + f0, m)
                own.n = start + 32
                finish(norm_after, gain, g0)

            def embed(i, norm, nroot, after):
                u0 = UNIT[f"gate{i}"]
                act.wait_ge(S["acc_done"], u0)
                act.dma_start(PIN[:, :, :], a["p"][i, 0].rearrange("(t p) e -> p t e", p=P)).then_inc(S["p_loaded"], 16)
                root(nroot)
                for m in range(KT):
                    act.wait_ge(S["acc_free"], free_of(u0)[1] + m)
                    fn(GATE[:, m, :], ST[m % 2][:, :], ACT.Sigmoid).then_inc(S["gate_done"], 1)
                    if m in (2, 3):
                        k = m - 2
                        act.wait_ge(S["p_tr"], 2 * i + k + 1)
                        fn(PTh[:, k, :], flat(PS[:, 4 + 2 * k:6 + 2 * k, :]), ACT.Copy).then_inc(S["p_hi"], 1)
                finish(*after)

            mlp("mlp0", 2, "ple", 0)
            embed(0, 2, 1, (3, "mix", 8))
            root(2)
            for u in range(12):
                act.wait_ge(S["acc_free"], free_of(UNIT["qkv"])[1] + u)
                act.dma_start(qkv_dram[u * P:(u + 1) * P, :], ST[u % 2][:, :]).then_inc(spilled[u % 2], 16)
            with act.Fori(0, KVH) as g:
                act.wait_ge(S["at_vt_done"], g + (1 + CREDIT))
                fn(AVT[:, :, :].rearrange("p n d -> p (n d)"), PS[:, 3, :], ACT.Copy).then_inc(S["at_vt_copied"], 1)

                def exps(n):
                    b, lo, e = n % 2, (P if n == 0 else 0), g * NB + n
                    act.wait_ge(S["at_max"], e + 1)
                    for j in range(4):
                        fn(SC[:, b, j, lo:], SC[:, b, j, lo:], ACT.Exp, bias=sm[:, b, j:j + 1], accum_out=sm[:, 2 + b, j:j + 1])
                    fn(sm[:, 6 + b, :], sm[:, 6 + b, :], ACT.Exp).then_inc(S["at_exp"], 1)

                def outs(n):
                    b, e = n % 2, g * NB + n
                    halves = slice(1, 2) if n == 0 else slice(0, 2)
                    act.wait_ge(S["at_pt_done"], e + (1 + CREDIT))
                    fn(PT[:, b, halves, :, :].rearrange("p h j t -> p (h j t)"),
                       PS[:, halves, :].rearrange("p h t -> p (h t)"), ACT.Copy).then_inc(S["at_pt_copied"], 1)
                    act.wait_ge(S["at_o_done"], e + 1)
                    settle()
                    fn(XBh[:, bass.ds(g * 2, 2), n * P:(n + 1) * P], PS[:, 2 + b, 0:256].rearrange("p (j t) -> p j t", t=P),
                       ACT.Copy).then_inc(S["at_o_hi"], 1)

                exps(0)
                for n in range(1, NB):
                    exps(n)
                    outs(n - 1)
                outs(NB - 1)
            finish(4, "mlp", 8)
            mlp("mlp1", 5, "ple", 8)
            embed(1, 5, 3, (6, "final", 0, False))
            root(4)
            for n in range(NB):
                act.wait_ge(S["fin_tr"], 2 * n + 2)
                if n >= 2:
                    act.wait_ge(out_stored[n % 2], 16 * (n // 2))
                own(fn(OT[:, n % 2, :], PS[:, 4 + (2 * n) % 4:6 + (2 * n) % 4, :].rearrange("p a b -> p (a b)"), ACT.Copy))
                act.nop().then_inc(S["fin_copied"], 1)

        @block.vector
        def _(dve):
            for name in "hg_lvl_read hg_state hg_ss_read at_o_done_lo at_scored sq_used".split():
                dve.nop().then_inc(S[name], CREDIT)
            own = Own(dve, S["dve_step"])
            tt = dve.tensor_tensor

            dve.wait_ge(S["cols_done"], 1)
            dve.tensor_copy(COLS[:, :], PS[:, 0, 0:N_ROWS]).then_inc(S["cols_ready"], 1)
            for t in range(NB):
                dve.wait_ge(S["x_tr_done"], 2 * t + 1)
                dve.tensor_copy(H[:, 0:4, t * P:(t + 1) * P], PS[:, 4 + (2 * t) % 4, :].rearrange("p (k t) -> p k t", t=P))\
                    .then_inc(S["x_tr_dve"], 1)
            dve.wait_ge(S["x_tr_dve"], NB)
            dve.wait_ge(S["x_tr_act"], NB)
            dve.wait_ge(S["cols_ready"], 1)
            for _ in range(8):
                dve.nop().then_inc(S["h_ready"], 1)

            def tile(buf, m):
                return buf[:, m, :] if isinstance(m, int) else buf[:, bass.ds(m, 1), :].rearrange("p a t -> p (a t)")

            def add_squares(norm, m):
                dve.wait_ge(S["sq_done"], m + (8 * norm + 1))
                tt(SUMSQ[:, :], SUMSQ[:, :], SQ[:, :], ALU.add).then_inc(S["sq_used"], 1)
                dve.wait_ge(S["sq_used"], m + (8 * norm + 1 + CREDIT))

            def low(norm, m, g):
                dve.wait_ge(S["x_hi_done"], m + (8 * norm + 1))
                dve.scalar_tensor_tensor(tile(XAl, m), tile(H, m), COLS[:, bass.ds(m + g, 1)], tile(XAh, m).bitcast(F32),
                                         ALU.mult, ALU.subtract).then_inc(S["x_ready"], 1)
                add_squares(norm, m)

            def start_norm():
                own(dve.memset(SUMSQ[:, :], 0.0))

            def end_norm():
                dve.nop().then_inc(S["sumsq_ready"], 1)

            def variance(norm):
                dve.wait_ge(S["ss_done"], norm + 1)
                dve.tensor_scalar(ST[0][:, :], flat(PS[:, 4:6, :]), 1.0 / D, EPS, ALU.mult, ALU.add).then_inc(S["ss_read"], 1)
                dve.wait_ge(S["ss_read"], norm + 1)

            def rstd(norm, n):
                variance(norm)
                dve.reciprocal(ST[1][:, :], ST[0][:, :]).then_inc(S["rcp_done"], 1)
                dve.wait_ge(S["rstd_done"], n + 1)

            def rstd_squared(norm):
                variance(norm)
                own(dve.reciprocal(RSTD[:, :], ST[0][:, :]))

            x4 = COLS[:, ROW["lb"]:ROW["lb"] + HEADS]
            tt(floor_[:, :], x4, x4, ALU.subtract).then_inc(S["lb_in"], 1)
            start_norm()
            with dve.Fori(0, KT) as m:
                low(0, m, ROW["mix"])
            end_norm()
            rstd(0, 0)
            for u in range(4):
                dve.wait_ge(S["acc_done"], u + 1)
                if u >= 2:
                    dve.wait_ge(spilled[u % 2], 16)
                tt(ST[u % 2][:, :].rearrange("p (j c) -> p j c", j=L), flat(ACC[u % 2]).rearrange("p (c j) -> p j c", j=L),
                   RSTD[:, :].rearrange("p (c j) -> p j c", j=L), ALU.mult).then_inc(S["acc_free"], 1)
            dve.wait_ge(S["s5_raw_loaded"], 16 * 13)
            p = lambda i: PR[:, i, :]
            ph = lambda i: phase[:, i, :]
            colp = lambda name: COLS[:, ROW[name]:ROW[name] + PAIRS]

            def t2(o, x, y, op):
                own(tt(o, x, y, op))

            def ts(o, x, c, op, c2=None, op2=None):
                own(dve.tensor_scalar(o, x, c, c2, op) if op2 is None else dve.tensor_scalar(o, x, c, c2, op, op2))

            def cmul(or_, oi, ar, ai, br, bi, tmp):
                t2(tmp, ai, bi, ALU.mult)
                t2(or_, ar, br, ALU.mult)
                t2(or_, or_, tmp, ALU.subtract)
                t2(tmp, ai, br, ALU.mult)
                t2(oi, ar, bi, ALU.mult)
                t2(oi, oi, tmp, ALU.add)

            lr, li = p(0), colp("lam_im")
            ts(lr, colp("lam_re"), -1e-4, ALU.min)
            dve.nop().then_inc(S["s5_dve"], 1)
            dve.wait_ge(S["s5_act"], 1)
            t2(p(8), li, p(1), ALU.mult)
            t2(p(2), lr, p(1), ALU.mult)
            dve.nop().then_inc(S["s5_dve"], 1)
            ts(p(9), p(8), 1.0 / TWO_PI, ALU.mult, MAGIC, ALU.add)
            ts(p(9), p(9), MAGIC, ALU.subtract)
            c1 = 6.28125
            c2 = float(np.float32(TWO_PI - c1))
            c3 = float(TWO_PI - c1 - c2)
            own(dve.scalar_tensor_tensor(p(5), p(9), -c1, p(8), ALU.mult, ALU.add))
            own(dve.scalar_tensor_tensor(p(5), p(9), -c2, p(5), ALU.mult, ALU.add))
            own(dve.scalar_tensor_tensor(p(5), p(9), -c3, p(5), ALU.mult, ALU.add))
            ts(p(5), p(5), 3.14159, ALU.min, -3.14159, ALU.max)
            dve.nop().then_inc(S["s5_dve"], 1)
            dve.wait_ge(S["s5_act"], 3)
            sn, cs, ar, ai = p(6), p(10), p(11), p(12)
            t2(cs, p(7), p(7), ALU.mult)
            ts(cs, cs, -2.0, ALU.mult, 1.0, ALU.add)
            t2(ar, p(3), cs, ALU.mult)
            t2(ai, p(3), sn, ALU.mult)
            xr, den, zr, zi, tmp = p(13), p(14), p(15), p(16), p(17)
            ts(xr, ar, -1.0, ALU.add)
            t2(den, lr, lr, ALU.mult)
            t2(tmp, li, li, ALU.mult)
            t2(den, den, tmp, ALU.add)
            own(dve.reciprocal(den, den))
            t2(zr, xr, lr, ALU.mult)
            t2(tmp, ai, li, ALU.mult)
            t2(zr, zr, tmp, ALU.add)
            t2(zr, zr, den, ALU.mult)
            t2(zi, ai, lr, ALU.mult)
            t2(tmp, xr, li, ALU.mult)
            t2(zi, zi, tmp, ALU.subtract)
            t2(zi, zi, den, ALU.mult)
            own(dve.memset(PW[:, 0, :, 0:1], 1.0))
            own(dve.memset(PW[:, 1, :, 0:1], 0.0))
            for j in range(L):
                cmul(PW[:, 0, :, j + 1], PW[:, 1, :, j + 1], PW[:, 0, :, j], PW[:, 1, :, j], ar, ai, tmp)

            def wide(ap, n):
                return ap.unsqueeze(2).to_broadcast([P, PAIRS, n])

            tq = PT1[:, 0:PAIRS * GRP].rearrange("p (q h) -> p q h", h=GRP)
            cmul(BB[:, 0], BB[:, 1], BRAW[:, 0], BRAW[:, 1], wide(zr, GRP), wide(zi, GRP), tq)
            for j in range(L):
                pw = [wide(PW[:, r, :, L - 1 - j], GRP) for r in range(2)]
                cmul(BA[:, 0, :, j, :], BA[:, 1, :, j, :], BB[:, 0], BB[:, 1], pw[0], pw[1], tq)
            dve.nop().then_inc(S["s5_ba_ready"], 1)
            dve.wait_ge(S["s5_c_tr"], 1)
            for h in range(2):
                src = PS[:, 4, h * 256:(h + 1) * 256].rearrange("p (r q h) -> p r q h", r=2, h=GRP)
                own(dve.tensor_copy(C0[:, 0, 8 * h:8 * h + 8, :], src[:, 0]))
                ts(C0[:, 1, 8 * h:8 * h + 8, :], src[:, 1], -1.0, ALU.mult)
            for j in range(L):
                pr_, pi_ = (wide(PW[:, r, :, j + 1], GRP) for r in range(2))
                t2(tq, C0[:, 1], pi_, ALU.mult)
                t2(CA[:, 0, :, j, :], C0[:, 0], pr_, ALU.mult)
                t2(CA[:, 0, :, j, :], CA[:, 0, :, j, :], tq, ALU.add)
                t2(tq, C0[:, 0], pi_, ALU.mult)
                t2(CA[:, 1, :, j, :], C0[:, 1], pr_, ALU.mult)
                t2(CA[:, 1, :, j, :], CA[:, 1, :, j, :], tq, ALU.subtract)
            dve.nop().then_inc(S["s5_ca_ready"], 1)
            dve.wait_ge(S["h_spilled"], 16)
            own(dve.memset(TOEP[:, :, :], 0.0))
            dve.nop().then_inc(S["s5_t_zeroed"], 1)
            w8r, w8i = ph(0), ph(1)
            ur, ui, vr, vi = p(18), p(19), p(20), p(21)
            cmul(ur, ui, cs, sn, cs, sn, tmp)
            cmul(vr, vi, ur, ui, ur, ui, tmp)
            cmul(w8r, w8i, vr, vi, vr, vi, tmp)
            own(dve.tensor_copy(ph(2), p(4)))
            dve.wait_ge(S["s5_g_copied"], 8)
            own(dve.memset(ROT[:, 0, :, 0:1], 1.0))
            own(dve.memset(ROT[:, 1, :, 0:1], 0.0))
            n = 1
            while n < CH:
                wr, wi = (wide(ph(r), n) for r in range(2))
                tr = ST[2][:, 0:PAIRS * n].rearrange("p (q c) -> p q c", c=n)
                cmul(ROT[:, 0, :, n:2 * n], ROT[:, 1, :, n:2 * n], ROT[:, 0, :, 0:n], ROT[:, 1, :, 0:n], wr, wi, tr)
                if 2 * n < CH:
                    cmul(ph(3), ph(4), ph(0), ph(1), ph(0), ph(1), ph(5))
                    own(dve.tensor_copy(ph(0), ph(3)))
                    own(dve.tensor_copy(ph(1), ph(4)))
                n *= 2
            dve.wait_ge(S["s5_t_loaded"], 16 * 8)
            t1 = ST[2][:, :].rearrange("p (q c) -> p q c", c=CH)
            t2_ = ST[3][:, :].rearrange("p (q c) -> p q c", c=CH)
            for half in range(2):
                q = slice(8 * half, 8 * half + 8)
                er, ei = (flat(PS[:, 4 + 2 * r:6 + 2 * r, :]).rearrange("p (q c) -> p q c", c=CH) for r in range(2))
                dve.wait_ge(S["s5_end_done"], half + 1)
                t2(t1, ei, ROT[:, 1, q, :], ALU.mult)
                t2(CR[:, 0, q, :], er, ROT[:, 0, q, :], ALU.mult)
                t2(CR[:, 0, q, :], CR[:, 0, q, :], t1, ALU.add)
                t2(t1, er, ROT[:, 1, q, :], ALU.mult)
                t2(CR[:, 1, q, :], ei, ROT[:, 0, q, :], ALU.mult)
                dve.nop().then_inc(S["s5_end_read"], 1)
                t2(CR[:, 1, q, :], CR[:, 1, q, :], t1, ALU.subtract)
            for r in range(2):
                for q in range(PAIRS):
                    ins = dve.tensor_tensor_scan(CR[:, r, q, :], ph(2)[:, q:q + 1].to_broadcast([P, CH]), CR[:, r, q, :],
                                                 0.0, ALU.mult, ALU.add)
                    own(ins)
            for half in range(2):
                q = slice(8 * half, 8 * half + 8)
                t2(t1, CR[:, 1, q, :], ROT[:, 1, q, :], ALU.mult)
                t2(t2_, CR[:, 0, q, :], ROT[:, 1, q, :], ALU.mult)
                t2(CR[:, 0, q, :], CR[:, 0, q, :], ROT[:, 0, q, :], ALU.mult)
                t2(CR[:, 0, q, :], CR[:, 0, q, :], t1, ALU.subtract)
                t2(CR[:, 1, q, :], CR[:, 1, q, :], ROT[:, 0, q, :], ALU.mult)
                t2(CR[:, 1, q, :], CR[:, 1, q, :], t2_, ALU.add)
            dve.nop().then_inc(S["s5_states_ready"], 1)
            dve.wait_ge(S["lb_exp"], 1)
            own(dve.reciprocal(keep[:, :], floor_[:, :]))
            t2(keep[:, :], keep[:, :], floor_[:, :], ALU.mult)
            t2(floor_[:, :], keep[:, :], keep[:, :], ALU.subtract)
            ts(keep[:, :], floor_[:, :], -1.0, ALU.mult, 1.0, ALU.add)
            ts(floor_[:, :], floor_[:, :], 1e-30, ALU.max)
            dve.wait_ge(S["s5_yt_loaded"], 32)
            for k in range(4):
                y = YT[:, k, :]
                own(dve.scalar_tensor_tensor(y, UT[:, k, :], col("d", k), y, ALU.mult, ALU.add))
                t2(ST[2][:, :], y, y, ALU.mult)
                c = float(np.sqrt(2.0 / np.pi))
                ts(ST[2][:, :], ST[2][:, :], c * 0.044715, ALU.mult, c, ALU.add)
                tt(ST[2][:, :], ST[2][:, :], y, ALU.mult).then_inc(S["glu_tanh_in"], 1)
                dve.wait_ge(S["glu_tanh"], k + 1)
                dve.scalar_tensor_tensor(y, ST[3][:, :], 1.0, y, ALU.add, ALU.mult).then_inc(S["glu_zz"], 1)
                dve.wait_ge(S["mid_hi_done"], k + 1)
                dve.scalar_tensor_tensor(XBl[:, 4 + k, :].rearrange("p (c j) -> p j c", j=L), y.rearrange("p (j c) -> p j c", j=L),
                                         0.5, XBh[:, 4 + k, :].bitcast(F32).rearrange("p (c j) -> p j c", j=L),
                                         ALU.mult, ALU.subtract).then_inc(S["mid_ready"], 1)
            for m in range(4):
                dve.wait_ge(S["glu_sig"], m + 1)
                dve.nop().then_inc(S["acc_free"], 1)
                dve.scalar_tensor_tensor(ST[3][:, :].rearrange("p (c j) -> p c j", j=L), YT[:, m, :].rearrange("p (j c) -> p c j", j=L),
                                         0.5, ST[2][:, :].rearrange("p (c j) -> p c j", j=L), ALU.mult, ALU.mult).then_inc(S["glu_zz"], 1)
                dve.wait_ge(S["mid_hi_done"], 5 + m)
                tt(XBl[:, m, :], ST[3][:, :], XBh[:, m, :].bitcast(F32), ALU.subtract).then_inc(S["mid_ready"], 1)
            dve.wait_ge(S["mid_ready"], 8)
            dve.wait_ge(S["masks_ready"], 1)
            with own.loop(HEADS, HG_STEPS) as hd:
                def told(ins):
                    ins.then_inc(S["hg_dve"], 1)

                f, q, v, g = (FQIG[:, j, :] for j in range(4))
                dve.wait_ge(S["hg_loaded"], hd * 16 + 16)
                t2(TA[:, :], f, RSTD[:, :], ALU.mult)
                told(dve.tensor_scalar(TA[:, :], TA[:, :], -80.0, None, ALU.max))
                t2(q, q, RSTD[:, :], ALU.mult)
                t2(v, v, RSTD[:, :], ALU.mult)
                t2(g, g, RSTD[:, :], ALU.mult)
                dve.wait_ge(S["hg_act"], hd * 14 + 1)
                told(dve.scalar_tensor_tensor(KK[:, :], TB[:, :], keep[:, bass.ds(hd, 1)], TC[:, :], ALU.mult, ALU.mult))
                dve.wait_ge(S["hg_act"], hd * 14 + 2)
                for c in range(NB):
                    t = slice(c * P, (c + 1) * P)
                    own(dve.tensor_tensor_scan(BC[:, t], ones[:, :], TD[:, t], 0.0, ALU.mult, ALU.add))
                dve.nop().then_inc(S["hg_dve"], 1)
                bc = BC[:, :].rearrange("p (c t) -> p c t", t=P)
                told(tt(TD[:, :].rearrange("p (c t) -> p c t", t=P), bc, bc[:, :, P - 1:P].to_broadcast([P, NB, P]), ALU.subtract))
                dve.wait_ge(S["hg_act"], hd * 14 + 3)
                told(tt(QB[:, :], q, TC[:, :], ALU.mult))
                dve.wait_ge(S["hg_dve"], hd * 14 + 2)
                dve.wait_ge(S["hg_act"], hd * 14 + 4)
                told(tt(KD[:, :], KK[:, :], TD[:, :], ALU.mult))
                for l, w in enumerate(LEVELS):
                    b4 = BC[:, :].rearrange("p (n two w) -> p n two w", two=2, w=w)
                    lv = LVL[:, l, :].rearrange("p (n two w) -> p n two w", two=2, w=w)
                    ref = b4[:, :, 0, w - 1:w].to_broadcast([P, T // (2 * w), w])
                    own(tt(lv[:, :, 0, :], b4[:, :, 0, :], ref, ALU.subtract))
                    told(tt(lv[:, :, 1, :], ref, b4[:, :, 1, :], ALU.subtract))
                own(dve.memset(SS[:, :], 0.0))
                dve.nop().then_inc(S["hg_dve"], 1)
                for c in range(NB):
                    b, e = c % 2, hd * NB + c
                    dve.wait_ge(S["hg_lvl_done"], e + 1)
                    tt(MP[:, b, :, :].rearrange("p l t -> p (l t)"), flat(PS[:, 4 + 2 * b:6 + 2 * b, :]),
                       MASK[:, :, :].rearrange("p l t -> p (l t)"), ALU.mult).then_inc(S["hg_lvl_read"], 1)
                    dve.wait_ge(S["hg_lvl_read"], e + (1 + CREDIT))
                    dve.wait_ge(S["hg_o_done"], e * 2 + (CREDIT - 2)) if c >= 1 else dve.wait_ge(S["hg_o_done"], e * 2 + CREDIT)
                    dve.tensor_reduce(AT[:, b, :], MP[:, b, :, :].rearrange("p l t -> p t l"), X, ALU.add).then_inc(S["hg_att"], 1)
                    dve.wait_ge(S["hg_ds_done"], e + 1)
                    if c:
                        dve.wait_ge(S["hg_o_done"], e * 2 + (1 + CREDIT))
                    dve.wait_ge(S["hg_state"], e + CREDIT)
                    end = TC[:, (c + 1) * P - 1:(c + 1) * P]
                    dve.scalar_tensor_tensor(SS[:, :], SS[:, :], end, PS[:, 2, 0:P], ALU.mult, ALU.add).then_inc(S["hg_state"], 1)
                dve.wait_ge(S["hg_ss"], hd + 1)
                dve.tensor_scalar(TD[:, :], flat(PS[:, 4:6, :]), 1.0 / P, EPS, ALU.mult, ALU.add).then_inc(S["hg_ss_read"], 1)
                dve.wait_ge(S["hg_act"], hd * 14 + 14)
                t2(OUTH[:, :], OUTH[:, :], TD[:, :], ALU.mult)
                t2(TC[:, :], TC[:, :], g, ALU.mult)
                dve.scalar_tensor_tensor(TD[:, :], OUTH[:, :], COLS[:, bass.ds(hd + ROW["head_norm"], 1)], TC[:, :],
                                         ALU.mult, ALU.mult).then_inc(S["hg_y_ready"], 1)
                dve.wait_ge(S["mid_hi_done"], hd + 9)
                tt(tile(XBl, hd + 4), TD[:, :], tile(XBh, hd + 4).bitcast(F32), ALU.subtract).then_inc(S["mid_ready"], 1)
                dve.wait_ge(S["mid_ready"], hd + 9)
                dve.nop().then_inc(S["hg_head_done"], 1)

            def residual(u0, norm, gain, factor):
                start_norm()
                with dve.Fori(0, KT // 2) as i:
                    for b in range(2):
                        m = i * 2 + b
                        dve.wait_ge(S["acc_done"], i * 2 + (u0 + b + 1))
                        h = tile(H, m)
                        if factor is None:
                            tt(h, flat(ACC[b]), h, ALU.add).then_inc(S["acc_free"], 1)
                            dve.wait_ge(S["acc_free"], i * 2 + (free_of(u0)[1] + b))
                        else:
                            tt(ST[0][:, :], flat(ACC[b]), factor, ALU.mult).then_inc(S["acc_free"], 1)
                            dve.wait_ge(S["acc_free"], i * 2 + (free_of(u0)[1] + b))
                            tt(h, h, ST[0][:, :], ALU.add).then_inc(S["h_ready"], 1)
                        if factor is None:
                            dve.nop().then_inc(S["h_ready"], 1)
                        low(norm, m, ROW[gain[0]] + gain[1])
                end_norm()

            def mlp(name, norm, mid0, after):
                u0 = UNIT[name]
                f0 = free_of(u0)[1]

                def up(c):
                    with dve.Fori(0, 4) as i:
                        for b in range(2):
                            off = c * 16 + i * 2 + b
                            dve.wait_ge(S["acc_done"], off + (u0 + 1))
                            dve.tensor_scalar(ST[0][:, :], flat(ACC[b]), 0.0, None, ALU.max).then_inc(S["acc_free"], 1)
                            dve.wait_ge(S["mid_hi_done"], c * 8 + i * 2 + (mid0 + b + 1))
                            tt(tile(XBl, i * 2 + b), ST[1][:, :], tile(XBh, i * 2 + b).bitcast(F32), ALU.subtract).then_inc(S["mid_ready"], 1)

                def down(c):
                    base_ = own.n
                    with dve.Fori(0, 4) as i:
                        for b in range(2):
                            off = c * 16 + i * 2 + b
                            dve.wait_ge(S["acc_done"], off + (u0 + 9))
                            tt(ST[0][:, :], flat(ACC[b]), RSTD[:, :], ALU.mult).then_inc(S["acc_free"], 1)
                            dve.wait_ge(S["acc_free"], off + (f0 + 8))
                            h = tile(H, i * 2 + b)
                            own.n = c * 8 + i * 2 + (start + b)
                            own(tt(h, h, ST[0][:, :], ALU.add))

                with dve.Fori(0, 4) as i:
                    for b in range(2):
                        dve.wait_ge(S["acc_done"], i * 2 + (u0 + b + 1))
                        dve.tensor_scalar(ST[0][:, :], flat(ACC[b]), 0.0, None, ALU.max).then_inc(S["acc_free"], 1)
                        dve.wait_ge(S["mid_hi_done"], i * 2 + (mid0 + b + 1))
                        tt(tile(XBl, i * 2 + b), ST[1][:, :], tile(XBh, i * 2 + b).bitcast(F32), ALU.subtract).then_inc(S["mid_ready"], 1)
                dve.wait_ge(S["mid_ready"], mid0 + 8)
                rstd_squared(norm)
                start = own.n
                with dve.Fori(0, 3) as c:
                    down(c)
                    up(c + 1)
                own.n = start + 24
                residual(u0 + 56, *after, RSTD[:, :])

            def embed(i, norm, nroot, after, gain, last=False):
                u0 = UNIT[f"gate{i}"]
                rstd(norm, nroot)
                for m in range(KT):
                    dve.wait_ge(S["acc_done"], u0 + m + 1)
                    if m >= 2:
                        dve.wait_ge(S["gate_done"], 8 * i + m - 1)
                    tt(ST[m % 2][:, :], flat(ACC[m % 2]), RSTD[:, :], ALU.mult).then_inc(S["acc_free"], 1)
                    dve.wait_ge(S["acc_free"], free_of(u0)[1] + m)
                    if m in (2, 3):
                        k = m - 2
                        dve.wait_ge(S["p_hi"], 2 * i + k + 1)
                        tt(PTl[:, k, :], flat(PS[:, 4 + 2 * k:6 + 2 * k, :]), PTh[:, k, :].bitcast(F32), ALU.subtract).then_inc(S["p_ready"], 1)
                dve.wait_ge(S["gate_done"], 8 * i + 8)
                u0 = UNIT[f"up{i}"]
                start_norm()
                for m in range(KT):
                    dve.wait_ge(S["acc_done"], u0 + m + 1)
                    tt(ST[0][:, :], flat(ACC[m % 2]), GATE[:, m, :], ALU.mult).then_inc(S["acc_free"], 1)
                    dve.wait_ge(S["acc_free"], free_of(u0)[1] + m)
                    tt(H[:, m, :], H[:, m, :], ST[0][:, :], ALU.add).then_inc(S["h_ready"], 1)
                    if last:
                        add_squares(after, m)
                    else:
                        low(after, m, ROW[gain[0]] + gain[1])
                end_norm()

            dve.wait_ge(S["h_restored"], 16)
            residual(UNIT["out"], 1, ("mlp", 0), None)
            mlp("mlp0", 1, 12, (2, ("ple", 0)))
            embed(0, 2, 1, 3, ("mix", 8))
            rstd(3, 2)
            for u in range(12):
                dve.wait_ge(S["acc_done"], UNIT["qkv"] + u + 1)
                dve.wait_ge(spilled[u % 2], 16 * (10 + u // 2))
                tt(ST[u % 2][:, :], flat(ACC[u % 2]), RSTD[:, :], ALU.mult).then_inc(S["acc_free"], 1)
            dve.wait_ge(S["dist_ready"], 1)
            dve.wait_ge(S["slopes_ready"], 1)
            dve.wait_ge(S["sinks_loaded"], 16)
            with own.loop(KVH, AT_STEPS) as g:
                dve.wait_ge(S["at_q_loaded"], g * 64 + 64)
                for j in range(4):
                    own(dve.tensor_scalar(BIAS[:, j, :], dist[:, :], slope[:, bass.ds(g * 4 + (0, 2, 1, 3)[j], 1)], None, ALU.mult))

                def score(n):
                    b, lo, e = n % 2, (P if n == 0 else 0), g * NB + n
                    sc = SC[:, b, :, lo:]
                    dve.wait_ge(S["at_qk_done"], e + (1 + CREDIT))
                    dve.wait_ge(S["at_pt_done"], e + (CREDIT - 1)) if n >= 1 else dve.wait_ge(S["at_pt_done"], e + CREDIT)
                    ps = PS[:, 4 + 2 * b:6 + 2 * b, :].rearrange("p a (j s) -> p (a j) s", j=2)[:, :, lo:]
                    dve.scalar_tensor_tensor(sc, ps, HD ** -0.5, BIAS[:, :, lo:], ALU.mult, ALU.add).then_inc(S["at_scored"], 1)
                    dve.wait_ge(S["at_scored"], e + (1 + CREDIT))
                    own(dve.tensor_reduce(sm[:, b, :], sc, X, ALU.max))
                    sk = sink[:, bass.ds(g * 4, 4)].rearrange("p (j r) -> p r j", r=2)
                    mx, ex = (sm[:, i, :].rearrange("p (r j) -> p r j", r=2) for i in (b, 6 + b))
                    own(tt(mx, mx, sk, ALU.max))
                    own(tt(ex, sk, mx, ALU.subtract))
                    dve.tensor_scalar(sm[:, b, :], sm[:, b, :], -1.0, None, ALU.mult).then_inc(S["at_max"], 1)

                def denominators(n):
                    b, e = n % 2, g * NB + n
                    dve.wait_ge(S["at_exp"], e + 1)
                    own(tt(sm[:, 4 + b, :], sm[:, 2 + b, :], sm[:, 6 + b, :], ALU.add))
                    dve.reciprocal(sm[:, 4 + b, :], sm[:, 4 + b, :]).then_inc(S["at_den"], 1)

                def outs(n):
                    b, e = n % 2, g * NB + n
                    dve.wait_ge(S["at_o_hi"], e + 1)
                    t = slice(n * P, (n + 1) * P)
                    tt(XBl[:, bass.ds(g * 2, 2), t], PS[:, 2 + b, 0:256].rearrange("p (j t) -> p j t", t=P),
                       XBh[:, bass.ds(g * 2, 2), t].bitcast(F32), ALU.subtract).then_inc(S["at_o_done_lo"], 1)

                score(0)
                for n in range(1, NB):
                    score(n)
                    denominators(n - 1)
                    if n >= 2:
                        outs(n - 2)
                denominators(NB - 1)
                outs(NB - 2)
                outs(NB - 1)
            residual(UNIT["wo"], 4, ("mlp", 8), None)
            mlp("mlp1", 4, 44, (5, ("ple", 8)))
            embed(1, 5, 3, 6, None, last=True)
            rstd(6, 4)
            for m in range(KT):
                dve.scalar_tensor_tensor(H[:, m, :], H[:, m, :], col("final", m), RSTD[:, :], ALU.mult, ALU.mult).then_inc(S["fin_ready"], 1)


_SHAPES = dict(
    x=(1, T, D), p=(2, 1, T, PLE), mix_norm=(2, D), mlp_norm=(2, D), ple_norm=(2, D), final_norm=(D,),
    w_in_even=(1, D, 5 * S5W), w_out_even=(1, D, D), s5_lam_re=(1, GROUPS, STATES), s5_lam_im=(1, GROUPS, STATES),
    s5_log_dt=(1, GROUPS), s5_b_re=(1, GROUPS, STATES, GRP), s5_b_im=(1, GROUPS, STATES, GRP),
    s5_c_re=(1, GROUPS, GRP, STATES), s5_c_im=(1, GROUPS, GRP, STATES), s5_d=(1, GROUPS, GRP),
    s5_w_glu=(1, S5W, S5W), s5_b_glu=(1, S5W), hgrn_lb_logits=(1, S5W), hgrn_norm=(1, HEADS, P),
    w_qkv_odd=(1, D, 12 * P), w_o_odd=(1, D, D), attn_sinks=(1, QH), w_mlp_in=(2, D, FF), w_mlp_out=(2, FF, D),
    w_ple_up=(2, PLE, D), w_ple_gate=(2, D, D))


def kernel(**inputs):
    import concourse.bacc as bacc
    from concourse.bass_utils import run_bass_kernel_spmd

    nc = bacc.Bacc("TRN2", target_bir_lowering=False, num_devices=1)
    arrays = {f"{n}_in": np.ascontiguousarray(inputs[n]) for n in _SHAPES}
    a = {n: nc.dram_tensor(f"{n}_in", shape, F32, kind="ExternalInput").ap() for n, shape in _SHAPES.items()}
    out = nc.dram_tensor("out", (1, T, D), F32, kind="ExternalOutput").ap()
    build(nc, a, out)
    return run_bass_kernel_spmd(nc, [arrays], core_ids=[0]).results[0]["out"]
```

```python
from contextlib import ExitStack, contextmanager

import numpy as np

import concourse.bass as bass
from concourse import mybir

F32, F32R = mybir.dt.float32, mybir.dt.float32r
ALU, ACT = mybir.AluOpType, mybir.ActivationFunctionType
X = mybir.AxisListType.X

P = 128
D, T, FF, PLE = 1024, 1024, 4096, 256
KT = D // P
NB = T // P
HALF = 512
EPS = 1e-6
S5W, GRP, STATES = 512, 16, 64
GROUPS, PAIRS = 32, 16
L = 8
CH = T // L
HEADS = 4
LEVELS = [64, 32, 16, 8, 4, 2, 1]
AT_STEPS = 72
QH, KVH, HD = 16, 4, 64
BODY = 2 * NB
AHEAD = 3
RING = 4
FAR = 1.0e32
CREDIT = 1
TWO_PI = 6.283185307179586
MAGIC = 12582912.0

SLAB = dict(u=0, heads=4, glu=20, out=22, mlp0=30, gate0=94, up0=102, qkv=104, wo=116, mlp1=124, gate1=188, up1=196)
UNIT = dict(u=0, heads=4, glu=20, out=24, mlp0=32, gate0=96, up0=104, qkv=112, wo=124, mlp1=132, gate1=196, up1=204)
ROW = dict(mix=0, mlp=16, ple=32, final=48, head_norm=56, b_glu=60, lb=64, d=68, lam_re=72, lam_im=88)
N_ROWS = 104


class Own:

    def __init__(self, eng, sem):
        self.eng, self.sem, self.n, self.taken = eng, sem, 0, 0

    def __call__(self, ins):
        ins.then_inc(self.sem, 1)
        self.n = self.n + 1
        self.taken += 1
        self.eng.wait_ge(self.sem, self.n)

    @contextmanager
    def loop(self, count, steps):
        base, outer = self.n, self.taken
        with self.eng.Fori(0, count) as i:
            self.n, self.taken = i * steps + base, 0
            yield i
        assert self.taken == steps, (self.taken, steps)
        self.n, self.taken = base + count * steps, outer + count * steps


def build(nc, a, out):
    ctx = ExitStack()
    base = 16512

    def at(name, shape, dt, offset):
        return nc.alloc_sbuf_tensor_at(name, shape, dt, offset=offset)

    K = 1024
    H_AT, XAH_AT, XAL_AT, XBH_AT, XBL_AT = (base + i * 32 * K for i in range(5))
    RAW_AT = base + 160 * K
    W_AT = RAW_AT + 8 * K
    MISC_AT = W_AT + 16 * K

    H = at("residual", [P, KT, T], F32, H_AT)
    XAh, XAl = at("x_hi", [P, KT, T], F32R, XAH_AT), at("x_lo", [P, KT, T], F32R, XAL_AT)
    XBh, XBl = at("mid_hi", [P, KT, T], F32R, XBH_AT), at("mid_lo", [P, KT, T], F32R, XBL_AT)
    RAW = at("w_raw", [P, 2, KT * P], F32, RAW_AT)
    WH, WL = at("w_hi", [P, 2, KT * P], F32R, W_AT), at("w_lo", [P, 2, KT * P], F32R, W_AT + 8 * K)
    RSTD = at("rstd", [P, T], F32, MISC_AT)
    ST = [at(f"stage{i}", [P, T], F32, MISC_AT + (1 + i) * 4 * K) for i in range(4)]
    SUMSQ, SQ = ST[3], ST[2]
    small_at = [MISC_AT + 20 * K]

    def small(name, shape):
        n = -(-int(np.prod(shape[1:])) * 4 // 32) * 32
        o = small_at[0]
        small_at[0] += n
        assert small_at[0] <= 229368, small_at[0]
        return at(name, shape, F32, o)

    ident, ones = small("identity", [P, P]), small("ones", [P, P])
    COLS = small("vectors", [P, N_ROWS])
    dist = small("distance", [P, 2 * P])
    sink, slope = small("sinks", [P, QH]), small("neg_slopes", [P, QH])
    log_dt = small("s5_log_dt", [P, GROUPS])
    keep, floor_ = small("one_minus_lb", [P, HEADS]), small("lb_floor", [P, HEADS])
    sm = small("softmax_stats", [P, 4, RING, 4])
    phase = small("s5_phase", [P, 6, PAIRS])

    def col(name, i):
        return COLS[:, ROW[name] + i:ROW[name] + i + 1]

    U = at("s5_u", [P, GROUPS, CH], F32, H_AT)
    TOEP = at("s5_toeplitz", [P, GROUPS, P], F32, H_AT + 16 * K)
    EW = at("s5_end_weights", [P, PAIRS, 2, P], F32, XBH_AT)
    YS = at("s5_y_chunks", [P, GROUPS, CH], F32, XBH_AT)
    BA = at("s5_ba", [P, 2, PAIRS, L, GRP], F32, XBH_AT + 16 * K)
    GK = at("s5_kernel", [GRP, GROUPS, P], F32, XBH_AT + 16 * K)
    CR = at("s5_state", [P, 2, PAIRS, CH], F32, XBH_AT + 16 * K)
    ROT = at("s5_rotation", [P, 2, PAIRS, CH], F32, XBL_AT)
    CA = at("s5_ca", [P, 2, PAIRS, L, GRP], F32, XBL_AT + 16 * K)
    CROW = at("s5_c_rows", [P, 2, 2, P], F32, XBL_AT)
    BRAW = at("s5_b", [P, 2, PAIRS, GRP], F32, XBL_AT + 2 * K)
    BB = at("s5_bbar", [P, 2, PAIRS, GRP], F32, XBL_AT + 4 * K)
    C0 = at("s5_c", [P, 2, PAIRS, GRP], F32, XBL_AT + 6 * K)
    PW = at("s5_powers", [P, 2, PAIRS, L + 1], F32, XBL_AT + 8 * K)
    PR = at("s5_params", [P, 28, PAIRS], F32, XBL_AT + 10 * K)
    PT1 = at("s5_tmp", [P, 1024], F32, XBL_AT + 12 * K)
    YT = at("s5_y", [P, 4, T], F32, H_AT)
    UT = at("s5_ut", [P, 4, T], F32, H_AT + 16 * K)

    XS = at("x_tokens", [P, NB, D], F32, XBH_AT)
    ROWS = at("vector_rows", [N_ROWS, P], F32, MISC_AT + 4 * K)

    hg = XAH_AT
    QV = at("hg_qv", [P, 2, 2, HALF], F32, hg)
    G = at("hg_g", [P, T], F32, hg + 8 * K)
    LVL = at("hg_levels", [P, 2, 7, HALF], F32, hg + 12 * K)
    KK = at("hg_k", [P, 2, HALF], F32, hg + 40 * K)
    QB = at("hg_q_decayed", [P, 2, HALF], F32, hg + 44 * K)
    KD = at("hg_k_decayed", [P, 2, HALF], F32, hg + 48 * K)
    OUTH = at("hg_out", [P, 2, HALF], F32, hg + 52 * K)
    F = at("hg_f", [P, HALF], F32, hg + 56 * K)
    BC = at("hg_cumulative", [P, HALF], F32, hg + 58 * K)
    TA = at("hg_tmp_a", [P, HALF], F32, hg + 60 * K)
    TB = at("hg_tmp_b", [P, HALF], F32, hg + 62 * K)
    TC = at("hg_tmp_c", [P, HALF], F32, H_AT + 0)
    TD = at("hg_tmp_d", [P, HALF], F32, H_AT + 2 * K)
    PA = at("hg_squares", [P, HALF], F32, H_AT + 4 * K)
    PD = at("hg_product", [P, HALF], F32, H_AT + 6 * K)
    PC = at("hg_gate", [P, T], F32, H_AT + 8 * K)
    ENDS = at("hg_chunk_decay", [P, 2, HALF // P], F32, H_AT + 12 * K)
    MASK = at("hg_masks", [P, 8, P], F32, H_AT + 16 * K)
    MP = at("hg_masked", [P, 2, 8, P], F32, H_AT + 20 * K)
    VT = at("hg_v_tokens", [P, 2, P], F32, H_AT + 28 * K)
    KDT = at("hg_kd_tokens", [P, 2, P], F32, H_AT + 29 * K)
    AT = at("hg_att", [P, 2, P], F32, H_AT + 30 * K)
    SS = at("hg_state", [P, P], F32, H_AT + 31 * K)

    AQ = at("at_q", [P, 2, 2, T], F32, XAH_AT)
    AK = at("at_k", [P, 2, T], F32, XAH_AT + 16 * K)
    AV = at("at_v", [HD, 2, T], F32, XAH_AT + 24 * K)
    AVT = at("at_v_tokens", [P, 2, NB, HD], F32, XAL_AT)
    BIAS = at("at_bias", [P, 2, 4, 2 * P], F32, XAL_AT + 4 * K)
    SC = at("at_scores", [P, RING, 4, 2 * P], F32, XAL_AT + 12 * K)
    PT = at("at_probs_t", [P, 2, 4, P], F32, XAL_AT + 28 * K)

    PTh, PTl = at("p_hi", [P, 2, T], F32R, XBH_AT), at("p_lo", [P, 2, T], F32R, XBH_AT + 8 * K)
    PIN = at("p_tokens", [P, NB, PLE], F32, XBH_AT + 16 * K)
    GATE = at("gate", [P, KT, T], F32, XBL_AT)
    OT = at("out_tokens", [P, 2, D], F32, XBL_AT)

    def dram(name, shape):
        return nc.dram_tensor(name, shape, F32, kind="Internal").ap()

    h_dram = dram("residual_dram", [D, T])
    u_dram = dram("u_dram", [S5W, T])
    y_dram = dram("y_dram", [S5W, T])
    fqig_dram = dram("fqig_dram", [HEADS * 4 * P, T])
    qkv_dram = dram("qkv_dram", [12 * P, T])

    with ctx:
        PS = ctx.enter_context(nc.psum_tensor("ps", [P, 8, HALF], F32))
        ACC = [PS[:, 0:2, :], PS[:, 2:4, :]]

        def flat(ap):
            return ap.rearrange("p a b -> p (a b)")

        def sem(name):
            return ctx.enter_context(nc.semaphore(name))

        names = """acc_done acc_free acc_free_act w_hi_done w_ready x_hi_done x_ready mid_hi_done mid_ready
        h_ready sq_done sq_used sumsq_ready ss_done ss_read rcp_done rstd_done relu_sq_done
        consts_ready rows_loaded cols_done cols_ready sinks_loaded x_tr_done x_tr_dve x_tr_act
        dve_step act_step pool_step act_passed pool_passed pe_passed h_spilled h_restored
        s5_raw_loaded s5_c_tr s5_dve s5_act s5_ba_ready s5_ca_ready s5_ew_tr s5_ew_copied s5_g_done s5_g_copied
        s5_t_zeroed s5_t_loaded s5_u_loaded s5_end_done s5_end_read s5_states_ready s5_y_done s5_y_copied s5_y_stored
        s5_yt_loaded lb_in lb_exp glu_tanh_in glu_tanh glu_zz glu_sig masks_ready
        hg_f_loaded hg_g_loaded hg_f hg_sigmoid_f hg_log_f hg_k_made hg_cumulated hg_to_end hg_exp_b hg_exp_end hg_level hg_level_exp
        hg_qv_scaled hg_decayed hg_levels hg_g_scaled hg_sigmoid_g hg_gate_made
        hg_tr hg_tr_copied hg_lvl_done hg_lvl_read hg_att hg_ds_done hg_state hg_o_done hg_o_copied
        hg_squares_made hg_ss hg_ss_read hg_rstd hg_y_ready hg_y_high hg_y_low dist_ready slopes_ready
        at_vt_done at_vt_copied at_qk_done at_scored at_max at_exp at_den at_norm at_pt_done at_pt_copied at_o_done at_o_hi at_o_done_lo
        p_loaded p_tr p_hi p_ready gate_done fin_ready fin_tr fin_copied""".split()
        S = {n: sem(n) for n in names}
        w_loaded = [sem(f"w_loaded{i}") for i in range(2)]
        spilled = [sem(f"spilled{i}") for i in range(2)]
        x_loaded = [sem(f"x_loaded{i}") for i in range(NB)]
        hg_qv_loaded = [sem(f"hg_qv_loaded{i}") for i in range(2)]
        at_loaded = [sem(f"at_loaded{i}") for i in range(2)]
        out_stored = [sem(f"out_stored{i}") for i in range(2)]

        def free_of(u):
            if 4 <= u < 20:
                return S["acc_free_act"], u - 3
            return S["acc_free"], (u + 1 if u < 4 else u - 15)

        block = ctx.enter_context(nc.Block())

        @block.sync
        def _(sp):
            def load(b, need, src):
                if need is not None:
                    sp.wait_ge(S["w_ready"], need)
                dst = RAW[:, b, :].rearrange("p (k n) -> p k n", n=src.shape[-1])
                sp.dma_start(dst, src).then_inc(w_loaded[b], 16)

            def cols(w, c):
                return w[:, c].rearrange("(k p) n -> p k n", p=P)

            def run(s0, n, w, c0=0):
                with sp.Fori(0, n // 2) as i:
                    for b in range(2):
                        load(b, i * 2 + (s0 + b - 1), cols(w, bass.ds(i * 2 * P + (c0 + b * P), P)))

            def mlp(s0, i):
                w_in, w_out = a["w_mlp_in"][i], a["w_mlp_out"][i]
                with sp.Fori(0, 4) as c:
                    with sp.Fori(0, 4) as m:
                        for b in range(2):
                            load(b, c * 16 + m * 2 + (s0 + b - 1), cols(w_in, bass.ds(c * 1024 + m * 256 + b * P, P)))
                    with sp.Fori(0, 4) as m:
                        for b in range(2):
                            src = w_out[bass.ds(c * 1024, 1024), bass.ds(m * 256 + b * P, P)]
                            load(b, c * 16 + m * 2 + (s0 + 8 + b - 1), src.rearrange("(k p) n -> p k n", p=P))

            def ple_up(s0, i):
                for s in range(2):
                    src = a["w_ple_up"][i][:, s * HALF:(s + 1) * HALF].rearrange("(k p) n -> p k n", p=P)
                    load(s, s0 + s - 1, src)

            w_in = a["w_in_even"][0]
            for t in range(NB):
                sp.dma_start(XS[:, t, :], a["x"][0, t * P:(t + 1) * P, :]).then_inc(x_loaded[t], 16)
                if t in (1, 3):
                    b = (t - 1) // 2
                    load(b, None, cols(w_in, slice(b * P, (b + 1) * P)))
            for s in range(2, 4):
                load(s % 2, s - 1, cols(w_in, slice(s * P, (s + 1) * P)))
            with sp.Fori(0, HEADS) as hd:
                for j, c0 in enumerate((2 * S5W, S5W, 3 * S5W, 4 * S5W)):
                    load(j % 2, hd * 4 + (4 + j - 1), cols(w_in, bass.ds(hd * P + c0, P)))
            for s in range(2):
                src = a["s5_w_glu"][0][:, s * 256:(s + 1) * 256].rearrange("(k p) n -> p k n", p=P)
                load(s, 20 + s - 1, src)
            w = a["w_out_even"][0]
            for b in range(2):
                load(b, 22 + b - 1, cols(w, slice(b * P, (b + 1) * P)))
            for b in range(2):
                sp.wait_ge(spilled[b], 16 * 10)
            sp.wait_ge(S["acc_done"], 20)

            def hg_load(dst, hd, j, cols_, signal):
                sp.dma_start(dst, fqig_dram[bass.ds(hd * 4 * P + j * P, P), cols_]).then_inc(signal, 16)

            def f_load(hd, half):
                hg_load(F[:, :], hd, 0, slice(half * HALF, (half + 1) * HALF), S["hg_f_loaded"])

            def qv_load(hd, half):
                for j in range(2):
                    hg_load(QV[:, half, j, :], hd, 1 + j, slice(half * HALF, (half + 1) * HALF), hg_qv_loaded[half])

            f_load(0, 0)
            qv_load(0, 0)
            qv_load(0, 1)
            hg_load(G[:, :], 0, 3, slice(0, T), S["hg_g_loaded"])
            sp.wait_ge(S["hg_f"], 1)
            f_load(0, 1)
            with sp.Fori(1, HEADS) as hd:
                for half in range(2):
                    sp.wait_ge(S["hg_f"], hd * 2 + half)
                    f_load(hd, half)
                    sp.wait_ge(S["hg_lvl_done"], hd * NB + (half - 1) * NB // 2)
                    qv_load(hd, half)
                    if half == 0:
                        sp.wait_ge(S["hg_gate_made"], hd)
                        hg_load(G[:, :], hd, 3, slice(0, T), S["hg_g_loaded"])
            sp.wait_ge(S["hg_y_low"], 2 * HEADS)
            sp.wait_ge(S["h_spilled"], 16)
            sp.dma_start(H[:, :, :], h_dram.rearrange("(k p) t -> p k t", p=P)).then_inc(S["h_restored"], 16)
            with sp.Fori(1, 4) as i:
                for b in range(2):
                    load(b, i * 2 + (22 + b - 1), cols(w, bass.ds(i * 256 + b * P, P)))
            mlp(SLAB["mlp0"], 0)
            run(SLAB["gate0"], 8, a["w_ple_gate"][0])
            ple_up(SLAB["up0"], 0)
            run(SLAB["qkv"], 12, a["w_qkv_odd"][0])
            w = a["w_o_odd"][0]
            for b in range(2):
                load(b, SLAB["wo"] + b - 1, cols(w, slice(b * P, (b + 1) * P)))
            for b in range(2):
                sp.wait_ge(spilled[b], 16 * 16)
            for g in range(KVH):
                par = g % 2
                if g >= 2:
                    sp.wait_ge(S["at_vt_done"], g - 1 + CREDIT)
                    sp.wait_ge(S["at_qk_done"], (g - 1) * NB + CREDIT)
                q = qkv_dram[g * 256:(g + 1) * 256, :].rearrange("(j p) t -> p j t", p=P)
                sp.dma_start(AQ[:, par, :, :], q).then_inc(at_loaded[par], 16)
                for r in range(2):
                    k = qkv_dram[1024 + g * HD:1024 + (g + 1) * HD, :]
                    sp.dma_start(AK[r * HD:(r + 1) * HD, par, :], k).then_inc(at_loaded[par], 16)
                sp.dma_start(AV[:, par, :], qkv_dram[1280 + g * HD:1280 + (g + 1) * HD, :]).then_inc(at_loaded[par], 16)
            with sp.Fori(1, 4) as i:
                for b in range(2):
                    load(b, i * 2 + (SLAB["wo"] + b - 1), cols(w, bass.ds(i * 256 + b * P, P)))
            mlp(SLAB["mlp1"], 1)
            run(SLAB["gate1"], 8, a["w_ple_gate"][1])
            ple_up(SLAB["up1"], 1)
            for n in range(NB):
                sp.wait_ge(S["fin_copied"], n + 1)
                sp.dma_start(out[0, n * P:(n + 1) * P, :], OT[:, n % 2, :]).then_inc(out_stored[n % 2], 16)
            for b in range(2):
                sp.wait_ge(out_stored[b], 16 * NB // 2)

        @block.gpsimd
        def _(pool):
            own = Own(pool, S["pool_step"])

            own(pool.memset(ident[:, :], 1.0))
            own(pool.affine_select(out=ident[:, :], in_=ident[:, :], compare_op=ALU.is_equal, fill=0.0,
                                   base=0, pattern=[[-1, P]], channel_multiplier=1))
            pool.memset(ones[:, :], 1.0).then_inc(S["consts_ready"], 1)
            own(pool.iota(dist[:, :], [[-1, 2 * P]], base=P, channel_multiplier=1, allow_small_or_imprecise_dtypes=True))
            own(pool.affine_select(out=dist[:, :], in_=dist[:, :], compare_op=ALU.is_ge, fill=FAR,
                                   base=P, pattern=[[-1, 2 * P]], channel_multiplier=1))
            pool.affine_select(out=dist[:, :], in_=dist[:, :], compare_op=ALU.is_ge, fill=FAR,
                               base=-1, pattern=[[1, 2 * P]], channel_multiplier=-1).then_inc(S["dist_ready"], 1)
            for h in range(QH):
                ins = pool.memset(slope[:, h:h + 1], -2.0 ** (-8.0 * (h + 1) / QH))
            ins.then_inc(S["slopes_ready"], 1)

            def split(b, s, visit, used):
                pool.wait_ge(w_loaded[b], visit)
                if used is not None:
                    pool.wait_ge(S["acc_done"], used)
                pool.nop().then_inc(S["pool_passed"], 1)
                pool.tensor_copy(WH[:, b, :], RAW[:, b, :]).then_inc(S["w_hi_done"], 1)
                pool.wait_ge(S["w_hi_done"], s)
                pool.tensor_tensor(WL[:, b, :], RAW[:, b, :], WH[:, b, :].bitcast(F32), ALU.subtract).then_inc(S["w_ready"], 1)

            def one(s, used):
                split(s % 2, s + 1, 16 * (s // 2 + 1), used)

            def run(s0, u0, n):
                with pool.Fori(0, n // 2) as i:
                    for b in range(2):
                        split(b, i * 2 + (s0 + b + 1), i * 16 + 16 * (s0 // 2 + 1), i * 2 + (u0 + b - 1))

            for s in range(2):
                one(s, None)
            for s in range(2, 4):
                one(s, s - 1)
            run(4, 4, 16)
            one(20, 19)
            one(21, 20)
            pool.wait_ge(S["glu_zz"], 4)
            own(pool.memset(MASK[:, :, :], 1.0))
            for l, w in enumerate(LEVELS):
                m = MASK[:, l, :]
                n = P // (2 * w)
                own(pool.affine_select(out=m, in_=m, compare_op=ALU.is_ge, fill=0.0, base=0,
                                       pattern=[[-2 * w, n], [0, 2 * w]], channel_multiplier=1))
                own(pool.affine_select(out=m, in_=m, compare_op=ALU.is_ge, fill=0.0, base=w - 1,
                                       pattern=[[2 * w, n], [0, 2 * w]], channel_multiplier=-1))
                own(pool.affine_select(out=m, in_=m, compare_op=ALU.is_ge, fill=0.0, base=-w,
                                       pattern=[[0, n], [1, 2 * w]], channel_multiplier=0))
            pool.affine_select(out=MASK[:, 7, :], in_=MASK[:, 7, :], compare_op=ALU.is_equal, fill=0.0,
                               base=0, pattern=[[-1, P]], channel_multiplier=1).then_inc(S["masks_ready"], 1)
            one(22, 22)
            one(23, 24)
            def keys_and_queries(hd, half):
                un = hd * 2 + half
                pool.wait_ge(hg_qv_loaded[half], hd * 32 + 32)
                for j in range(2):
                    ins = pool.tensor_tensor(QV[:, half, j, :], QV[:, half, j, :], RSTD[:, half * HALF:(half + 1) * HALF], ALU.mult)
                ins.then_inc(S["hg_qv_scaled"], 1)
                pool.wait_ge(S["hg_exp_b"], un + 1)
                pool.wait_ge(S["hg_qv_scaled"], un + 1)
                if not (isinstance(hd, int) and hd == 0 and half == 0):
                    pool.wait_ge(S["hg_o_done"], un * 4 + (CREDIT - 4))
                pool.tensor_tensor(QB[:, half, :], QV[:, half, 0, :], TC[:, :], ALU.mult)
                pool.wait_ge(S["hg_exp_end"], un + 1)
                pool.tensor_tensor(KD[:, half, :], KK[:, half, :], TD[:, :], ALU.mult).then_inc(S["hg_decayed"], 1)

            def levels(hd, half):
                for l, w in enumerate(LEVELS):
                    v, k, q = (ap.rearrange("p (n two w) -> p n two w", two=2, w=w)
                               for ap in (LVL[:, half, l, :], KK[:, half, :], QV[:, half, 0, :]))
                    pool.wait_ge(S["hg_level_exp"], hd * 14 + (7 * half + l + 1))
                    pool.tensor_tensor(v[:, :, 0, :], v[:, :, 0, :], k[:, :, 0, :], ALU.mult)
                    ins = pool.tensor_tensor(v[:, :, 1, :], v[:, :, 1, :], q[:, :, 1, :], ALU.mult)
                ins.then_inc(S["hg_levels"], 1)

            def heads_chunks(hd, last):
                keys_and_queries(hd, 1)
                levels(hd, 1)
                pool.wait_ge(S["hg_g_loaded"], hd * 16 + 16)
                pool.tensor_tensor(G[:, :], G[:, :], RSTD[:, :], ALU.mult).then_inc(S["hg_g_scaled"], 1)
                if not last:
                    keys_and_queries(hd + 1, 0)
                pool.wait_ge(S["hg_sigmoid_g"], hd + 1)
                pool.tensor_tensor(PC[:, :], PC[:, :], G[:, :], ALU.mult).then_inc(S["hg_gate_made"], 1)
                if not last:
                    levels(hd + 1, 0)

            keys_and_queries(0, 0)
            levels(0, 0)
            with pool.Fori(0, HEADS - 1) as hd:
                heads_chunks(hd, False)
            heads_chunks(HEADS - 1, True)
            with pool.Fori(0, 3) as i:
                for b in range(2):
                    split(b, i * 2 + (24 + b + 1), i * 16 + 16 * 13, i * 2 + (26 + b - 1))
            run(SLAB["mlp0"], UNIT["mlp0"], 64)
            run(SLAB["gate0"], UNIT["gate0"], 8)

            def ups(name, nxt, n_next):
                s, u = SLAB[name], UNIT[name]
                one(s, u - 1)
                one(s + 1, u)
                if nxt:
                    s, u = SLAB[nxt], UNIT[nxt]
                    one(s, u - 4)
                    one(s + 1, u)
                    with pool.Fori(1, n_next // 2) as i:
                        for b in range(2):
                            split(b, i * 2 + (s + b + 1), i * 16 + 16 * (s // 2 + 1), i * 2 + (u + b - 1))

            ups("up0", "qkv", 12)
            for s in range(SLAB["wo"], SLAB["wo"] + 2):
                one(s, s - SLAB["wo"] + UNIT["wo"] - 1)
            with pool.Fori(0, KVH // 2) as gp:
                for i in range(BODY):
                    lo = P if i % NB == 0 else 0
                    pr = SC[:, i % RING, :, lo:]
                    den = sm[:, 2, i % RING, :].unsqueeze(2).to_broadcast([P, 4, 2 * P - lo])
                    pool.wait_ge(S["at_den"], gp * BODY + (i + 1))
                    pool.tensor_tensor(pr, pr, den, ALU.mult).then_inc(S["at_norm"], 1)
            with pool.Fori(1, 4) as i:
                for b in range(2):
                    split(b, i * 2 + (SLAB["wo"] + b + 1), i * 16 + 16 * (SLAB["wo"] // 2 + 1), i * 2 + (UNIT["wo"] + b - 1))
            run(SLAB["mlp1"], UNIT["mlp1"], 64)
            run(SLAB["gate1"], UNIT["gate1"], 8)
            ups("up1", None, 0)

        @block.tensor
        def _(pe):
            for name in "hg_o_done at_vt_done at_qk_done at_pt_done".split():
                pe.nop().then_inc(S[name], CREDIT)
            def unit(acc, wh, wl, xh, xl, kts=KT, k0=0, ready=None):
                for k in range(kts):
                    if ready is not None:
                        pe.wait_ge(*ready(k))
                    for w, x in ((wh, xh), (wh, xl), (wl, xh)):
                        for h in range(2):
                            ins = pe.matmul(acc[:, h, :], w[:, k, :], x[:, k0 + k, h * HALF:(h + 1) * HALF],
                                            start=(k == 0 and w is wh and x is xh), stop=(k == kts - 1 and w is wl))
                ins.then_inc(S["acc_done"], 1)

            whs = [WH[:, b, :].rearrange("p (k n) -> p k n", n=P) for b in range(2)]
            wls = [WL[:, b, :].rearrange("p (k n) -> p k n", n=P) for b in range(2)]

            def one(s, u, x, **kw):
                pe.wait_ge(S["w_ready"], s + 1)
                if u >= 2:
                    pe.wait_ge(*free_of(u - 2))
                unit(ACC[u % 2], whs[s % 2], wls[s % 2], *x, **kw)

            def run(s0, u0, n, x):
                with pe.Fori(0, n // 2) as i:
                    for b in range(2):
                        pe.wait_ge(S["w_ready"], i * 2 + (s0 + b + 1))
                        pe.wait_ge(free_of(u0)[0], i * 2 + (free_of(u0)[1] + b - 2))
                        unit(ACC[b], whs[b], wls[b], *x)

            XA, XB = (XAh, XAl), (XBh, XBl)

            def x_ready(norm):
                return lambda k: (S["x_ready"], 8 * norm + k + 1)

            def sum_squares(n):
                pe.wait_ge(S["sumsq_ready"], n + 1)
                for h in range(2):
                    ins = pe.matmul(PS[:, 4 + h, :], ones[:, :], SUMSQ[:, h * HALF:(h + 1) * HALF], start=True, stop=True)
                ins.then_inc(S["ss_done"], 1)

            def first_two(s, u, norm):
                one(s, u, XA, ready=x_ready(norm))
                sum_squares(norm)
                one(s + 1, u + 1, XA)

            pe.wait_ge(S["consts_ready"], 1)
            pe.wait_ge(S["pool_step"], 2)
            pe.wait_ge(S["rows_loaded"], 16 * 10)
            pe.transpose(PS[:, 0, 0:N_ROWS], ROWS[:, :], ident[0:N_ROWS, 0:N_ROWS]).then_inc(S["cols_done"], 1)
            for t in range(NB):
                pe.wait_ge(x_loaded[t], 16)
                for h in range(2):
                    n = 2 * t + h
                    if t >= 2:
                        pe.wait_ge(S["x_tr_act" if h else "x_tr_dve"], t - 1)
                    for j in range(4):
                        k = 4 * h + j
                        ins = pe.transpose(PS[:, 4 + n % 4, j * P:(j + 1) * P], XS[:, t, k * P:(k + 1) * P], ident[:, :])
                    ins.then_inc(S["x_tr_done"], 1)
            pe.wait_ge(S["x_tr_dve"], NB)
            pe.wait_ge(S["x_tr_act"], NB)
            pe.wait_ge(S["cols_ready"], 1)
            first_two(0, 0, 0)
            for s in range(2, 4):
                one(s, s, XA)
            one(4, 4, XA)
            one(5, 5, XA)
            pe.wait_ge(S["ss_read"], 1)
            pe.wait_ge(S["s5_raw_loaded"], 16 * 13)
            for h in range(2):
                for r in range(2):
                    j = 2 * h + r
                    ins = pe.transpose(PS[:, 4, j * P:(j + 1) * P], CROW[:, h, r, :], ident[:, :])
            ins.then_inc(S["s5_c_tr"], 1)
            one(6, 6, XA)
            one(7, 7, XA)
            pe.wait_ge(S["s5_ba_ready"], 1)
            for n in range(8):
                if n == 0:
                    pe.wait_ge(S["s5_ca_ready"], 1)
                if n >= 4:
                    pe.wait_ge(S["s5_ew_copied"], n - 3)
                for j in range(4):
                    q, r = 2 * n + j // 2, j % 2
                    ins = pe.transpose(PS[:, 4 + n % 4, j * P:(j + 1) * P],
                                       BA[:, r, q, :, :].rearrange("p j h -> p (j h)"), ident[:, :])
                ins.then_inc(S["s5_ew_tr"], 1)
            def group(n, j):
                return 8 * (n // 2) + n % 2 + 2 * j

            for n in range(8):
                if n < 4:
                    pe.wait_ge(S["s5_ew_copied"], n + 5)
                else:
                    pe.wait_ge(S["s5_g_copied"], n - 3)
                for j in range(4):
                    g = group(n, j)
                    q, rows = g // 2, slice(STATES * (g % 2), STATES * (g % 2 + 1))
                    o = PS[0:GRP, 4 + n % 4, j * P:(j + 1) * P]
                    for r in range(2):
                        pe.matmul(o[:, 0:GRP], BB[rows, r, q, :], C0[rows, r, q, :], start=(r == 0), stop=(r == 1))
                    for r in range(2):
                        ins = pe.matmul(o[:, GRP:P], BB[rows, r, q, :],
                                        CA[rows, r, q, 0:L - 1, :].rearrange("p j h -> p (j h)"), start=(r == 0), stop=(r == 1))
                ins.then_inc(S["s5_g_done"], 1)
            one(8, 8, XA)
            one(9, 9, XA)
            pe.wait_ge(S["s5_u_loaded"], 16 * 8)
            pe.wait_ge(S["s5_g_copied"], 8)
            for half in range(2):
                if half:
                    one(10, 10, XA)
                    one(11, 11, XA)
                    pe.wait_ge(S["s5_end_read"], 1)
                for qq in range(8):
                    q = 8 * half + qq
                    for two in range(2):
                        for r in range(2):
                            o = PS[STATES * two:STATES * (two + 1), 4 + 2 * r + qq // 4, (qq % 4) * P:(qq % 4 + 1) * P]
                            ins = pe.matmul(o, EW[:, q, r, STATES * two:STATES * (two + 1)], U[:, 2 * q + two, :], start=True, stop=True)
                ins.then_inc(S["s5_end_done"], 1)
            one(12, 12, XA)
            one(13, 13, XA)
            pe.wait_ge(S["s5_t_loaded"], 16 * 8)
            pe.wait_ge(S["s5_states_ready"], 1)
            pe.wait_ge(S["s5_end_read"], 2)
            for n in range(8):
                if n >= 4:
                    pe.wait_ge(S["s5_y_copied"], n - 3)
                for j in range(4):
                    g = group(n, j)
                    q, rows = g // 2, slice(STATES * (g % 2), STATES * (g % 2 + 1))
                    o = PS[:, 4 + n % 4, j * P:(j + 1) * P]
                    pe.matmul(o, TOEP[:, g, :], U[:, g, :], start=True, stop=False)
                    for r in range(2):
                        ins = pe.matmul(o[:, 1:CH], CA[rows, r, q, :, :].rearrange("p j h -> p (j h)"),
                                        CR[rows, r, q, 0:CH - 1], start=False, stop=(r == 1))
                ins.then_inc(S["s5_y_done"], 1)
            run(14, 14, 6, XA)
            for s in range(2):
                pe.wait_ge(S["w_ready"], 21 + s)
                wh = WH[:, s, :].rearrange("p (k n) -> p k n", n=256)
                wl = WL[:, s, :].rearrange("p (k n) -> p k n", n=256)
                for j in range(2):
                    u = 20 + 2 * s + j
                    pe.wait_ge(*free_of(u - 2))
                    unit(ACC[j], wh[:, :, j * P:(j + 1) * P], wl[:, :, j * P:(j + 1) * P], XBh, XBl, kts=4, k0=4,
                         ready=(lambda k: (S["mid_ready"], k + 1)) if u == 20 else None)
            for u in (22, 23):
                pe.wait_ge(*free_of(u))
            pe.wait_ge(S["s5_y_copied"], 8)
            pe.wait_ge(S["masks_ready"], 1)

            def head(hd):
                for c in range(NB + 1):
                    half, t, b = c // 4, slice(c % 4 * P, (c % 4 + 1) * P), c % 2
                    if c < NB:
                        if c % 4 == 0:
                            pe.wait_ge(S["hg_decayed"], hd * 2 + (half + 1))
                        pe.wait_ge(S["hg_tr_copied"], hd * NB + (c + CREDIT))
                        pe.transpose(PS[:, 3, 0:P], QV[:, half, 1, t], ident[:, :])
                        pe.transpose(PS[:, 3, P:2 * P], KD[:, half, t], ident[:, :]).then_inc(S["hg_tr"], 1)
                        if c % 4 == 0:
                            pe.wait_ge(S["hg_levels"], hd * 2 + (half + 1))
                        pe.wait_ge(S["hg_lvl_read"], hd * NB + (max(c - 1, 0) + CREDIT))
                        for l in range(8):
                            o = PS[:, 4 + 2 * b + l // 4, (l % 4) * P:(l % 4 + 1) * P]
                            if l < 7:
                                ins = pe.matmul(o, LVL[:, half, l, t], LVL[:, half, l, t], start=True, stop=True)
                            else:
                                ins = pe.matmul(o, KK[:, half, t], QV[:, half, 0, t], start=True, stop=True)
                        ins.then_inc(S["hg_lvl_done"], 1)
                    if c == 0:
                        continue
                    c, b = c - 1, 1 - b
                    half, t = c // 4, slice(c % 4 * P, (c % 4 + 1) * P)
                    pe.wait_ge(S["hg_tr_copied"], hd * NB + (c + 1 + CREDIT))
                    pe.wait_ge(S["hg_state"], hd * (NB - 1) + (c + CREDIT))
                    if c < NB - 1:
                        ins = pe.matmul(PS[:, 2, 0:P], KDT[:, b, :], VT[:, b, :], start=True, stop=True)
                        if c == 0:
                            ins.then_inc(S["hg_ds_done"], 1)
                    pe.wait_ge(S["hg_o_copied"], hd * NB + (max(c - 1, 0) + CREDIT))
                    if c in (1, 5):
                        pe.wait_ge(S["hg_ss_read"], hd * 2 + (c // 4 + CREDIT))
                    if c:
                        ins = pe.matmul(PS[:, b, 0:P], SS[:, :], QB[:, half, t], start=True, stop=False)
                        if c < NB - 1:
                            ins.then_inc(S["hg_ds_done"], 1)
                    pe.wait_ge(S["hg_att"], hd * NB + (c + 1))
                    pe.matmul(PS[:, b, 0:P], VT[:, b, :], AT[:, b, :], start=(c == 0), stop=True).then_inc(S["hg_o_done"], 1)
                    if c in (4, 7):
                        pe.wait_ge(S["hg_squares_made"], hd * 2 + (c // 4 if c == 4 else 2))
                        pe.matmul(PS[:, 1, :], ones[:, :], PA[:, :], start=True, stop=True).then_inc(S["hg_ss"], 1)

            with pe.Fori(0, HEADS) as hd:
                head(hd)
            pe.wait_ge(S["hg_y_low"], 2 * HEADS)
            pe.wait_ge(S["mid_ready"], 8)
            one(22, 24, XB)
            one(23, 25, XB)
            run(24, 26, 6, XB)

            def mlp(name, norm, mid0):
                s, u = SLAB[name], UNIT[name]
                first_two(s, u, norm)
                run(s + 2, u + 2, 6, XA)

                def down_two(c):
                    for b in range(2):
                        pe.wait_ge(S["w_ready"], c * 16 + (s + 8 + b + 1))
                        pe.wait_ge(S["acc_free"], c * 16 + (free_of(u + 8)[1] + b - 2))
                        ready = (lambda k: (S["mid_ready"], c * 8 + (mid0 + k + 1))) if b == 0 else None
                        unit(ACC[b], whs[b], wls[b], *XB, ready=ready)

                def two(off, x):
                    for b in range(2):
                        pe.wait_ge(S["w_ready"], off + (s + b + 1))
                        pe.wait_ge(S["acc_free"], off + (free_of(u)[1] + b - 2))
                        unit(ACC[b], whs[b], wls[b], *x)

                with pe.Fori(0, 3) as c:
                    down_two(c)
                    with pe.Fori(0, 3) as m:
                        two(c * 16 + m * 2 + 10, XB)
                    with pe.Fori(0, 4) as m:
                        two(c * 16 + m * 2 + 16, XA)
                for b in range(2):
                    ready = (lambda k: (S["mid_ready"], mid0 + 24 + k + 1)) if b == 0 else None
                    one(s + 56 + b, u + 56 + b, XB, ready=ready)
                run(s + 58, u + 58, 6, XB)

            def embed(i, norm):
                s, u = SLAB[f"gate{i}"], UNIT[f"gate{i}"]
                first_two(s, u, norm)
                pe.wait_ge(S["p_loaded"], 16 * (i + 1))
                pe.wait_ge(S["ss_read"], norm + 1)
                for k in range(2):
                    for t in range(NB):
                        ins = pe.transpose(PS[:, 4 + 2 * k + t // 4, (t % 4) * P:(t % 4 + 1) * P],
                                           PIN[:, t, k * P:(k + 1) * P], ident[:, :])
                    ins.then_inc(S["p_tr"], 1)
                run(s + 2, u + 2, 6, XA)
                s, u = SLAB[f"up{i}"], UNIT[f"up{i}"]
                for n in range(2):
                    pe.wait_ge(S["w_ready"], s + n + 1)
                    wh = WH[:, n, :].rearrange("p (k n) -> p k n", n=HALF)
                    wl = WL[:, n, :].rearrange("p (k n) -> p k n", n=HALF)
                    if n == 0:
                        pe.wait_ge(S["p_ready"], 2 * (i + 1))
                    for j in range(4):
                        v = u + 4 * n + j
                        pe.wait_ge(*free_of(v - 2))
                        unit(ACC[v % 2], wh[:, :, j * P:(j + 1) * P], wl[:, :, j * P:(j + 1) * P], PTh, PTl, kts=2)

            mlp("mlp0", 1, 8)
            embed(0, 2)
            first_two(SLAB["qkv"], UNIT["qkv"], 3)
            run(SLAB["qkv"] + 2, UNIT["qkv"] + 2, 10, XA)
            for u in (122, 123):
                pe.wait_ge(*free_of(u))
            pe.wait_ge(S["ss_read"], 4)
            with pe.Fori(0, KVH // 2) as gp:

                def after(name, i):
                    pe.wait_ge(S[name], gp * BODY + (max(i + 1, 0) + CREDIT))

                def v_tokens(i):
                    par = i // NB
                    pe.wait_ge(at_loaded[par], gp * 64 + 64)
                    after("at_o_done_lo", i - AHEAD - 2)
                    pe.nop().then_inc(S["pe_passed"], 1)
                    for n in range(NB):
                        ins = pe.transpose(PS[:, 3, n * HD:(n + 1) * HD], AV[:, par, n * P:(n + 1) * P], ident[0:HD, 0:HD])
                    ins.then_inc(S["at_vt_done"], 1)

                def scores(i):
                    par, n, b = i // NB, i % NB, i % 2
                    lo = P if n == 0 else 0
                    after("at_scored", i - 2)
                    for j in range(4):
                        rows = slice(HD * (j % 2), HD * (j % 2 + 1))
                        o = PS[:, 4 + 2 * b + j % 2, (j // 2) * 256 + lo:(j // 2 + 1) * 256]
                        ins = pe.matmul(o, AQ[rows, par, j // 2, n * P:(n + 1) * P],
                                        AK[rows, par, (n - 1) * P + lo:(n + 1) * P], start=True, stop=True)
                    ins.then_inc(S["at_qk_done"], 1)

                def transposes(i):
                    pe.wait_ge(S["at_norm"], gp * BODY + (i + 1))
                    after("at_pt_copied", i - 1)
                    for h in ((1,) if i % NB == 0 else (0, 1)):
                        for j in range(4):
                            ins = pe.transpose(PS[:, h, j * P:(j + 1) * P], SC[:, i % RING, j, h * P:(h + 1) * P], ident[:, :])
                    ins.then_inc(S["at_pt_done"], 1)

                def outputs(i):
                    par, n, b = i // NB, i % NB, i % 2
                    after("at_pt_copied", i)
                    after("at_o_done_lo", i - 2)
                    for r in range(2):
                        for h in ((1,) if n == 0 else (0, 1)):
                            ins = pe.matmul(PS[HD * r:HD * (r + 1), 2 + b, 0:256], AVT[:, par, n - 1 + h, :],
                                            PT[:, h, 2 * r:2 * r + 2, :], start=(h == 0 or n == 0), stop=(h == 1))
                    ins.then_inc(S["at_o_done"], 1)

                for i in range(BODY + AHEAD):
                    if i >= AHEAD:
                        transposes(i - AHEAD)
                    if i < BODY:
                        if i % NB == 0:
                            v_tokens(i)
                        scores(i)
                    if i % NB == 0 and i < BODY:
                        pe.wait_ge(S["at_vt_copied"], gp * 2 + (i // NB + 1))
                    if i >= AHEAD:
                        outputs(i - AHEAD)
            pe.wait_ge(S["at_o_done_lo"], KVH * NB + CREDIT)
            one(SLAB["wo"], UNIT["wo"], XB)
            one(SLAB["wo"] + 1, UNIT["wo"] + 1, XB)
            run(SLAB["wo"] + 2, UNIT["wo"] + 2, 6, XB)
            mlp("mlp1", 4, 40)
            embed(1, 5)
            sum_squares(6)
            pe.wait_ge(S["ss_read"], 7)
            for u in (210, 211):
                pe.wait_ge(*free_of(u))
            pe.wait_ge(S["fin_ready"], 8)
            for n in range(NB):
                for h in range(2):
                    e = 2 * n + h
                    if e >= 4:
                        pe.wait_ge(S["fin_copied"], n - 1)
                    for j in range(4):
                        ins = pe.transpose(PS[:, 4 + e % 4, j * P:(j + 1) * P], H[:, 4 * h + j, n * P:(n + 1) * P], ident[:, :])
                    ins.then_inc(S["fin_tr"], 1)

        @block.scalar
        def _(act):
            for name in "hg_tr_copied hg_o_copied at_pt_copied".split():
                act.nop().then_inc(S[name], CREDIT)
            own = Own(act, S["act_step"])

            def fn(o, i, f, **kw):
                return act.activation(o, i, f, **kw)

            def wait(s, n):
                act.wait_ge(S[s], n)
                settle()

            def settle():
                act.nop().then_inc(S["act_passed"], 1)

            def rows(name, n, src):
                act.dma_start(ROWS[ROW[name]:ROW[name] + n, :], src).then_inc(S["rows_loaded"], 16)

            rows("mix", 16, a["mix_norm"].rearrange("i (k p) -> (i k) p", p=P))
            rows("mlp", 16, a["mlp_norm"].rearrange("i (k p) -> (i k) p", p=P))
            rows("ple", 16, a["ple_norm"].rearrange("i (k p) -> (i k) p", p=P))
            rows("final", 8, a["final_norm"].rearrange("(k p) -> k p", p=P))
            rows("head_norm", 4, a["hgrn_norm"][0])
            rows("b_glu", 4, a["s5_b_glu"][0].rearrange("(k p) -> k p", p=P))
            rows("lb", 4, a["hgrn_lb_logits"][0].rearrange("(k p) -> k p", p=P))
            rows("d", 4, a["s5_d"][0].rearrange("(k g) h -> k (g h)", k=4))
            rows("lam_re", 16, a["s5_lam_re"][0].rearrange("(q two) p -> q (two p)", two=2))
            rows("lam_im", 16, a["s5_lam_im"][0].rearrange("(q two) p -> q (two p)", two=2))
            act.dma_start(sink[:, :], a["attn_sinks"][0].unsqueeze(0).to_broadcast([P, QH])).then_inc(S["sinks_loaded"], 16)
            act.dma_start(log_dt[:, :], a["s5_log_dt"][0].unsqueeze(0).to_broadcast([P, GROUPS])).then_inc(S["s5_raw_loaded"], 16)
            for r, (b, c) in enumerate((("s5_b_re", "s5_c_re"), ("s5_b_im", "s5_c_im"))):
                for two in range(2):
                    act.dma_start(BRAW[two * STATES:(two + 1) * STATES, r, :, :],
                                  a[b][0].rearrange("(q two) p h -> two p q h", two=2)[two]).then_inc(S["s5_raw_loaded"], 16)
                    for h in range(2):
                        act.dma_start(CROW[:, h, r, two * STATES:(two + 1) * STATES],
                                      a[c][0].rearrange("(h q two) c p -> h two q c p", h=2, two=2)[h, two])\
                            .then_inc(S["s5_raw_loaded"], 16)
            for t in range(NB):
                act.wait_ge(S["x_tr_done"], 2 * t + 2)
                fn(H[:, 4:8, t * P:(t + 1) * P], PS[:, 4 + (2 * t + 1) % 4, :].rearrange("p (k t) -> p k t", t=P), ACT.Copy)\
                    .then_inc(S["x_tr_act"], 1)

            def finish(norm, gain, g0, split=True):
                with act.Fori(0, KT) as m:
                    hm = H[:, bass.ds(m, 1), :].rearrange("p a t -> p (a t)")
                    wait("h_ready", m + (8 * norm + 1))
                    if split:
                        fn(XAh[:, bass.ds(m, 1), :].rearrange("p a t -> p (a t)"), hm, ACT.Identity,
                           scale=COLS[:, bass.ds(m + (ROW[gain] + g0), 1)]).then_inc(S["x_hi_done"], 1)
                    wait("sq_used", m + 8 * norm + CREDIT)
                    fn(SQ[:, :], hm, ACT.Square).then_inc(S["sq_done"], 1)

            def root(n):
                act.wait_ge(S["rcp_done"], n + 1)
                fn(RSTD[:, :], ST[1][:, :], ACT.Sqrt).then_inc(S["rstd_done"], 1)

            finish(0, "mix", 0)
            act.dma_start(h_dram.rearrange("(k p) t -> p k t", p=P), H[:, :, :]).then_inc(S["h_spilled"], 16)
            root(0)
            for u in range(4):
                act.wait_ge(S["acc_free"], u + 1)
                act.dma_start(u_dram[u * P:(u + 1) * P, :], ST[u % 2][:, :]).then_inc(spilled[u % 2], 16)
            act.wait_ge(S["lb_in"], 1)
            fn(floor_[:, :], floor_[:, :], ACT.Exp).then_inc(S["lb_exp"], 1)
            p = lambda i: PR[:, i, :]
            act.wait_ge(S["cols_ready"], 1)
            act.wait_ge(S["s5_dve"], 1)
            act.wait_ge(S["s5_raw_loaded"], 16 * 13)
            for two in range(2):
                half = slice(two * STATES, (two + 1) * STATES)
                own(fn(PR[half, 1, :], log_dt[half, two::2], ACT.Exp))
            act.nop().then_inc(S["s5_act"], 1)
            act.wait_ge(S["s5_dve"], 2)
            fn(p(3), p(2), ACT.Exp)
            fn(p(4), p(2), ACT.Exp, scale=float(L)).then_inc(S["s5_act"], 1)
            act.wait_ge(S["s5_dve"], 3)
            fn(p(6), p(5), ACT.Sin)
            fn(p(7), p(5), ACT.Sin, scale=0.5).then_inc(S["s5_act"], 1)

            def head_unit(u):
                b = u % 2
                act.wait_ge(S["acc_done"], u + 1)
                act.wait_ge(spilled[b], 16 * (u // 2))
                fn(ST[b][:, :], flat(ACC[b]), ACT.Copy).then_inc(S["acc_free_act"], 1)
                act.wait_ge(S["acc_free_act"], u - 3)
                act.dma_start(fqig_dram[(u - 4) * P:(u - 3) * P, :], ST[b][:, :]).then_inc(spilled[b], 16)

            for u in range(4, 8):
                head_unit(u)
            for n in range(8):
                act.wait_ge(S["s5_ew_tr"], n + 1)
                fn(EW[:, 2 * n:2 * n + 2, :, :].rearrange("p q r m -> p (q r m)"), PS[:, 4 + n % 4, :], ACT.Copy)\
                    .then_inc(S["s5_ew_copied"], 1)

            def four(n):
                g0 = 8 * (n // 2) + n % 2
                return slice(g0, g0 + 7, 2)

            for n in range(8):
                act.wait_ge(S["s5_g_done"], n + 1)
                if n == 0:
                    act.wait_ge(S["s5_ew_tr"], 8)
                fn(GK[:, four(n), :], PS[0:GRP, 4 + n % 4, :].rearrange("p (g m) -> p g m", m=P), ACT.Copy)\
                    .then_inc(S["s5_g_copied"], 1)
            for b in range(2):
                act.wait_ge(spilled[b], 16 * 4)
            act.wait_ge(S["h_spilled"], 16)
            for j in range(L):
                act.dma_start(U[j * GRP:(j + 1) * GRP, :, :],
                              u_dram[:, j * CH:(j + 1) * CH].rearrange("(g h) c -> h g c", h=GRP)).then_inc(S["s5_u_loaded"], 16)
            act.wait_ge(S["s5_g_copied"], 8)
            act.wait_ge(S["s5_t_zeroed"], 1)
            for j in range(L):
                act.dma_start(TOEP[j * GRP:(j + 1) * GRP, :, j * GRP:P], GK[:, :, 0:P - j * GRP]).then_inc(S["s5_t_loaded"], 16)
            for u in range(8, 14):
                head_unit(u)
            for n in range(8):
                act.wait_ge(S["s5_y_done"], n + 1)
                fn(YS[:, four(n), :], PS[:, 4 + n % 4, :].rearrange("p (g m) -> p g m", m=P), ACT.Copy)\
                    .then_inc(S["s5_y_copied"], 1)
            act.wait_ge(S["s5_y_copied"], 8)
            for j in range(L):
                act.dma_start(y_dram[:, j * CH:(j + 1) * CH].rearrange("(g h) c -> h g c", h=GRP),
                              YS[j * GRP:(j + 1) * GRP, :, :]).then_inc(S["s5_y_stored"], 16)
            head_unit(14)
            head_unit(15)
            head_unit(16)
            act.wait_ge(S["s5_y_stored"], 16 * 8)
            act.dma_start(YT[:, :, :], y_dram.rearrange("(k p) t -> p k t", p=P)).then_inc(S["s5_yt_loaded"], 16)
            act.dma_start(UT[:, :, :], u_dram.rearrange("(k p) t -> p k t", p=P)).then_inc(S["s5_yt_loaded"], 16)
            for k in range(4):
                act.wait_ge(S["glu_tanh_in"], k + 1)
                fn(ST[3][:, :], ST[2][:, :], ACT.Tanh).then_inc(S["glu_tanh"], 1)
                act.wait_ge(S["glu_zz"], k + 1)
                fn(XBh[:, 4 + k, :].rearrange("p (c j) -> p j c", j=L), YT[:, k, :].rearrange("p (j c) -> p j c", j=L),
                   ACT.Copy, scale=0.5).then_inc(S["mid_hi_done"], 1)
                if k < 3:
                    head_unit(17 + k)
            for m in range(4):
                act.wait_ge(S["acc_done"], 21 + m)
                if m:
                    act.wait_ge(S["mid_ready"], 4 + m)
                fn(ST[2][:, :], flat(ACC[m % 2]), ACT.Sigmoid, bias=col("b_glu", m)).then_inc(S["glu_sig"], 1)
                act.wait_ge(S["glu_zz"], 5 + m)
                fn(XBh[:, m, :], ST[3][:, :], ACT.Copy).then_inc(S["mid_hi_done"], 1)
            def told(ins, name):
                ins.then_inc(S[name], 1)

            def sigmoid(o, tmp, i, name):
                own(fn(tmp, i, ACT.Exp, scale=-1.0))
                own(fn(o, tmp, ACT.Ln, bias=1.0))
                told(fn(o, o, ACT.Exp, scale=-1.0), name)

            def decay(hd, half):
                un = hd * 2 + half
                act.wait_ge(S["hg_f"], un + 1)
                if not (isinstance(hd, int) and hd == 0 and half == 0):
                    act.wait_ge(S["hg_decayed"], un)
                sigmoid(TC[:, :], TB[:, :], TA[:, :], "hg_sigmoid_f")
                act.wait_ge(S["hg_sigmoid_f"], un + 1)
                settle()
                told(fn(TD[:, :], TC[:, :], ACT.Ln, scale=keep[:, bass.ds(hd, 1)], bias=floor_[:, bass.ds(hd, 1)]), "hg_log_f")

            def cumulated(hd, half):
                act.wait_ge(S["hg_cumulated"], hd * 2 + (half + 1))
                act.wait_ge(S["hg_k_made"], hd * 2 + (half + 1))
                fn(TC[:, :], BC[:, :], ACT.Exp)
                told(fn(ENDS[:, half, :], BC[:, P - 1::P], ACT.Exp), "hg_exp_b")
                act.wait_ge(S["hg_to_end"], hd * 2 + (half + 1))
                told(fn(TD[:, :], TD[:, :], ACT.Exp, scale=-1.0), "hg_exp_end")

            def level_exps(hd, half, some):
                for l in some:
                    act.wait_ge(S["hg_level"], hd * 14 + (7 * half + l + 1))
                    told(fn(LVL[:, half, l, :], LVL[:, half, l, :], ACT.Exp, scale=-1.0), "hg_level_exp")

            def rstd_head(hd, half):
                act.wait_ge(S["hg_ss_read"], hd * 2 + (half + 1 + CREDIT))
                own(fn(PD[:, :], PD[:, :], ACT.Ln))
                told(fn(PD[:, :], PD[:, :], ACT.Exp, scale=-0.5), "hg_rstd")

            def squares(hd, half):
                act.wait_ge(S["hg_o_copied"], hd * NB + (4 * half + 4 + CREDIT))
                told(fn(PA[:, :], OUTH[:, half, :], ACT.Square), "hg_squares_made")

            def y_high(hd, half):
                act.wait_ge(S["hg_y_ready"], hd * 2 + (half + 1))
                settle()
                told(fn(XBh[:, bass.ds(hd + 4, 1), half * HALF:(half + 1) * HALF].rearrange("p a t -> p (a t)"), PD[:, :], ACT.Copy),
                     "hg_y_high")

            def head(hd, last):
                for c in range(NB + 1):
                    half, b = c // 4, c % 2
                    if c < NB:
                        act.wait_ge(S["hg_tr"], hd * NB + (c + 1))
                        fn(VT[:, b, :], PS[:, 3, 0:P], ACT.Copy)
                        fn(KDT[:, b, :], PS[:, 3, P:2 * P], ACT.Copy).then_inc(S["hg_tr_copied"], 1)
                    if c:
                        act.wait_ge(S["hg_o_done"], hd * NB + (c + CREDIT))
                        o = (c - 1) % 4 * P
                        fn(OUTH[:, (c - 1) // 4, o:o + P], PS[:, 1 - b, 0:P], ACT.Copy).then_inc(S["hg_o_copied"], 1)
                    if c == 4:
                        squares(hd, 0)
                        act.wait_ge(S["hg_g_scaled"], hd + 1)
                        sigmoid(PC[:, :], PC[:, :], G[:, :], "hg_sigmoid_g")
                    if c == 6:
                        rstd_head(hd, 0)
                    unit = (hd + half, 1 - half)
                    if c < NB and not (last and half == 1):
                        if c % 4 == 1:
                            cumulated(*unit)
                        if c % 4 == 2:
                            level_exps(*unit, range(4))
                        if c % 4 == 3:
                            level_exps(*unit, range(4, 7))
                            if not last:
                                decay(hd + 1, half)
                squares(hd, 1)
                y_high(hd, 0)
                rstd_head(hd, 1)
                y_high(hd, 1)

            decay(0, 0)
            cumulated(0, 0)
            level_exps(0, 0, range(7))
            decay(0, 1)
            with own.loop(HEADS - 1, 8) as hd:
                head(hd, False)
            head(HEADS - 1, True)
            finish(1, "mlp", 0)

            def hidden(u, m):
                act.wait_ge(S["acc_free"], u)
                own(fn(ST[1][:, :], ST[0][:, :], ACT.Square))
                settle()
                fn(XBh[:, bass.ds(m, 1), :].rearrange("p a t -> p (a t)"), ST[1][:, :], ACT.Copy).then_inc(S["mid_hi_done"], 1)

            def mlp(name, norm_after, gain, g0):
                f0 = free_of(UNIT[name])[1]
                start = own.n
                with act.Fori(0, 4) as c:
                    with act.Fori(0, 8) as m:
                        own.n = c * 8 + m + start
                        hidden(c * 16 + m + f0, m)
                own.n = start + 32
                finish(norm_after, gain, g0)

            def embed(i, norm, nroot, after):
                u0 = UNIT[f"gate{i}"]
                act.wait_ge(S["acc_done"], u0)
                act.dma_start(PIN[:, :, :], a["p"][i, 0].rearrange("(t p) e -> p t e", p=P)).then_inc(S["p_loaded"], 16)
                root(nroot)
                for m in range(KT):
                    act.wait_ge(S["acc_free"], free_of(u0)[1] + m)
                    fn(GATE[:, m, :], ST[m % 2][:, :], ACT.Sigmoid).then_inc(S["gate_done"], 1)
                    if m in (2, 3):
                        k = m - 2
                        act.wait_ge(S["p_tr"], 2 * i + k + 1)
                        fn(PTh[:, k, :], flat(PS[:, 4 + 2 * k:6 + 2 * k, :]), ACT.Copy).then_inc(S["p_hi"], 1)
                finish(*after)

            mlp("mlp0", 2, "ple", 0)
            embed(0, 2, 1, (3, "mix", 8))
            root(2)
            for u in range(12):
                act.wait_ge(S["acc_free"], free_of(UNIT["qkv"])[1] + u)
                act.dma_start(qkv_dram[u * P:(u + 1) * P, :], ST[u % 2][:, :]).then_inc(spilled[u % 2], 16)
            with act.Fori(0, KVH // 2) as gp:

                def v_copy(par):
                    act.wait_ge(S["at_vt_done"], gp * 2 + (par + 1 + CREDIT))
                    fn(AVT[:, par, :, :].rearrange("p n d -> p (n d)"), PS[:, 3, :], ACT.Copy).then_inc(S["at_vt_copied"], 1)

                def exps(i):
                    s, lo = i % RING, (P if i % NB == 0 else 0)
                    act.wait_ge(S["at_max"], gp * BODY + (i + 1))
                    for j in range(4):
                        fn(SC[:, s, j, lo:], SC[:, s, j, lo:], ACT.Exp, bias=sm[:, 0, s, j:j + 1], accum_out=sm[:, 1, s, j:j + 1])
                    fn(sm[:, 3, s, :], sm[:, 3, s, :], ACT.Exp).then_inc(S["at_exp"], 1)

                def probs(i):
                    halves = slice(1, 2) if i % NB == 0 else slice(0, 2)
                    act.wait_ge(S["at_pt_done"], gp * BODY + (i + 1 + CREDIT))
                    fn(PT[:, halves, :, :].rearrange("p h j t -> p (h j t)"),
                       PS[:, halves, :].rearrange("p h t -> p (h t)"), ACT.Copy).then_inc(S["at_pt_copied"], 1)

                def out_high(i):
                    n = i % NB
                    act.wait_ge(S["at_o_done"], gp * BODY + (i + 1))
                    settle()
                    fn(XBh[:, bass.ds(gp * 4 + 2 * (i // NB), 2), n * P:(n + 1) * P],
                       PS[:, 2 + i % 2, 0:256].rearrange("p (j t) -> p j t", t=P), ACT.Copy).then_inc(S["at_o_hi"], 1)

                for i in range(BODY + AHEAD + 1):
                    if i > AHEAD:
                        out_high(i - AHEAD - 1)
                    if i % NB == 0 and i < BODY:
                        v_copy(i // NB)
                    if AHEAD <= i < BODY + AHEAD:
                        probs(i - AHEAD)
                    if i < BODY:
                        exps(i)
            finish(4, "mlp", 8)
            mlp("mlp1", 5, "ple", 8)
            embed(1, 5, 3, (6, "final", 0, False))
            root(4)
            for n in range(NB):
                act.wait_ge(S["fin_tr"], 2 * n + 2)
                if n >= 2:
                    act.wait_ge(out_stored[n % 2], 16 * (n // 2))
                own(fn(OT[:, n % 2, :], PS[:, 4 + (2 * n) % 4:6 + (2 * n) % 4, :].rearrange("p a b -> p (a b)"), ACT.Copy))
                act.nop().then_inc(S["fin_copied"], 1)

        @block.vector
        def _(dve):
            for name in "hg_lvl_read hg_state hg_ss_read at_o_done_lo at_scored sq_used".split():
                dve.nop().then_inc(S[name], CREDIT)
            own = Own(dve, S["dve_step"])
            tt = dve.tensor_tensor

            dve.wait_ge(S["cols_done"], 1)
            dve.tensor_copy(COLS[:, :], PS[:, 0, 0:N_ROWS]).then_inc(S["cols_ready"], 1)
            for t in range(NB):
                dve.wait_ge(S["x_tr_done"], 2 * t + 1)
                dve.tensor_copy(H[:, 0:4, t * P:(t + 1) * P], PS[:, 4 + (2 * t) % 4, :].rearrange("p (k t) -> p k t", t=P))\
                    .then_inc(S["x_tr_dve"], 1)
            dve.wait_ge(S["x_tr_dve"], NB)
            dve.wait_ge(S["x_tr_act"], NB)
            dve.wait_ge(S["cols_ready"], 1)
            for _ in range(8):
                dve.nop().then_inc(S["h_ready"], 1)

            def tile(buf, m):
                return buf[:, m, :] if isinstance(m, int) else buf[:, bass.ds(m, 1), :].rearrange("p a t -> p (a t)")

            def add_squares(norm, m):
                dve.wait_ge(S["sq_done"], m + (8 * norm + 1))
                tt(SUMSQ[:, :], SUMSQ[:, :], SQ[:, :], ALU.add).then_inc(S["sq_used"], 1)
                dve.wait_ge(S["sq_used"], m + (8 * norm + 1 + CREDIT))

            def low(norm, m, g):
                dve.wait_ge(S["x_hi_done"], m + (8 * norm + 1))
                dve.scalar_tensor_tensor(tile(XAl, m), tile(H, m), COLS[:, bass.ds(m + g, 1)], tile(XAh, m).bitcast(F32),
                                         ALU.mult, ALU.subtract).then_inc(S["x_ready"], 1)
                add_squares(norm, m)

            def start_norm():
                own(dve.memset(SUMSQ[:, :], 0.0))

            def end_norm():
                dve.nop().then_inc(S["sumsq_ready"], 1)

            def variance(norm):
                dve.wait_ge(S["ss_done"], norm + 1)
                dve.tensor_scalar(ST[0][:, :], flat(PS[:, 4:6, :]), 1.0 / D, EPS, ALU.mult, ALU.add).then_inc(S["ss_read"], 1)
                dve.wait_ge(S["ss_read"], norm + 1)

            def rstd(norm, n):
                variance(norm)
                dve.reciprocal(ST[1][:, :], ST[0][:, :]).then_inc(S["rcp_done"], 1)
                dve.wait_ge(S["rstd_done"], n + 1)

            def rstd_squared(norm):
                variance(norm)
                own(dve.reciprocal(RSTD[:, :], ST[0][:, :]))

            x4 = COLS[:, ROW["lb"]:ROW["lb"] + HEADS]
            tt(floor_[:, :], x4, x4, ALU.subtract).then_inc(S["lb_in"], 1)
            start_norm()
            with dve.Fori(0, KT) as m:
                low(0, m, ROW["mix"])
            end_norm()
            rstd(0, 0)
            for u in range(4):
                dve.wait_ge(S["acc_done"], u + 1)
                if u >= 2:
                    dve.wait_ge(spilled[u % 2], 16)
                tt(ST[u % 2][:, :].rearrange("p (j c) -> p j c", j=L), flat(ACC[u % 2]).rearrange("p (c j) -> p j c", j=L),
                   RSTD[:, :].rearrange("p (c j) -> p j c", j=L), ALU.mult).then_inc(S["acc_free"], 1)
            dve.wait_ge(S["s5_raw_loaded"], 16 * 13)
            p = lambda i: PR[:, i, :]
            ph = lambda i: phase[:, i, :]
            colp = lambda name: COLS[:, ROW[name]:ROW[name] + PAIRS]

            def t2(o, x, y, op):
                own(tt(o, x, y, op))

            def ts(o, x, c, op, c2=None, op2=None):
                own(dve.tensor_scalar(o, x, c, c2, op) if op2 is None else dve.tensor_scalar(o, x, c, c2, op, op2))

            def cmul(or_, oi, ar, ai, br, bi, tmp):
                t2(tmp, ai, bi, ALU.mult)
                t2(or_, ar, br, ALU.mult)
                t2(or_, or_, tmp, ALU.subtract)
                t2(tmp, ai, br, ALU.mult)
                t2(oi, ar, bi, ALU.mult)
                t2(oi, oi, tmp, ALU.add)

            lr, li = p(0), colp("lam_im")
            ts(lr, colp("lam_re"), -1e-4, ALU.min)
            dve.nop().then_inc(S["s5_dve"], 1)
            dve.wait_ge(S["s5_act"], 1)
            t2(p(8), li, p(1), ALU.mult)
            t2(p(2), lr, p(1), ALU.mult)
            dve.nop().then_inc(S["s5_dve"], 1)
            ts(p(9), p(8), 1.0 / TWO_PI, ALU.mult, MAGIC, ALU.add)
            ts(p(9), p(9), MAGIC, ALU.subtract)
            c1 = 6.28125
            c2 = float(np.float32(TWO_PI - c1))
            c3 = float(TWO_PI - c1 - c2)
            own(dve.scalar_tensor_tensor(p(5), p(9), -c1, p(8), ALU.mult, ALU.add))
            own(dve.scalar_tensor_tensor(p(5), p(9), -c2, p(5), ALU.mult, ALU.add))
            own(dve.scalar_tensor_tensor(p(5), p(9), -c3, p(5), ALU.mult, ALU.add))
            ts(p(5), p(5), 3.14159, ALU.min, -3.14159, ALU.max)
            dve.nop().then_inc(S["s5_dve"], 1)
            dve.wait_ge(S["s5_act"], 3)
            sn, cs, ar, ai = p(6), p(10), p(11), p(12)
            t2(cs, p(7), p(7), ALU.mult)
            ts(cs, cs, -2.0, ALU.mult, 1.0, ALU.add)
            t2(ar, p(3), cs, ALU.mult)
            t2(ai, p(3), sn, ALU.mult)
            xr, den, zr, zi, tmp = p(13), p(14), p(15), p(16), p(17)
            ts(xr, ar, -1.0, ALU.add)
            t2(den, lr, lr, ALU.mult)
            t2(tmp, li, li, ALU.mult)
            t2(den, den, tmp, ALU.add)
            own(dve.reciprocal(den, den))
            t2(zr, xr, lr, ALU.mult)
            t2(tmp, ai, li, ALU.mult)
            t2(zr, zr, tmp, ALU.add)
            t2(zr, zr, den, ALU.mult)
            t2(zi, ai, lr, ALU.mult)
            t2(tmp, xr, li, ALU.mult)
            t2(zi, zi, tmp, ALU.subtract)
            t2(zi, zi, den, ALU.mult)
            own(dve.memset(PW[:, 0, :, 0:1], 1.0))
            own(dve.memset(PW[:, 1, :, 0:1], 0.0))
            for j in range(L):
                cmul(PW[:, 0, :, j + 1], PW[:, 1, :, j + 1], PW[:, 0, :, j], PW[:, 1, :, j], ar, ai, tmp)

            def wide(ap, n):
                return ap.unsqueeze(2).to_broadcast([P, PAIRS, n])

            tq = PT1[:, 0:PAIRS * GRP].rearrange("p (q h) -> p q h", h=GRP)
            cmul(BB[:, 0], BB[:, 1], BRAW[:, 0], BRAW[:, 1], wide(zr, GRP), wide(zi, GRP), tq)
            for j in range(L):
                pw = [wide(PW[:, r, :, L - 1 - j], GRP) for r in range(2)]
                cmul(BA[:, 0, :, j, :], BA[:, 1, :, j, :], BB[:, 0], BB[:, 1], pw[0], pw[1], tq)
            dve.nop().then_inc(S["s5_ba_ready"], 1)
            dve.wait_ge(S["s5_c_tr"], 1)
            for h in range(2):
                src = PS[:, 4, h * 256:(h + 1) * 256].rearrange("p (r q h) -> p r q h", r=2, h=GRP)
                own(dve.tensor_copy(C0[:, 0, 8 * h:8 * h + 8, :], src[:, 0]))
                ts(C0[:, 1, 8 * h:8 * h + 8, :], src[:, 1], -1.0, ALU.mult)
            for j in range(L):
                pr_, pi_ = (wide(PW[:, r, :, j + 1], GRP) for r in range(2))
                t2(tq, C0[:, 1], pi_, ALU.mult)
                t2(CA[:, 0, :, j, :], C0[:, 0], pr_, ALU.mult)
                t2(CA[:, 0, :, j, :], CA[:, 0, :, j, :], tq, ALU.add)
                t2(tq, C0[:, 0], pi_, ALU.mult)
                t2(CA[:, 1, :, j, :], C0[:, 1], pr_, ALU.mult)
                t2(CA[:, 1, :, j, :], CA[:, 1, :, j, :], tq, ALU.subtract)
            dve.nop().then_inc(S["s5_ca_ready"], 1)
            dve.wait_ge(S["h_spilled"], 16)
            own(dve.memset(TOEP[:, :, :], 0.0))
            dve.nop().then_inc(S["s5_t_zeroed"], 1)
            w8r, w8i = ph(0), ph(1)
            ur, ui, vr, vi = p(18), p(19), p(20), p(21)
            cmul(ur, ui, cs, sn, cs, sn, tmp)
            cmul(vr, vi, ur, ui, ur, ui, tmp)
            cmul(w8r, w8i, vr, vi, vr, vi, tmp)
            own(dve.tensor_copy(ph(2), p(4)))
            dve.wait_ge(S["s5_g_copied"], 8)
            own(dve.memset(ROT[:, 0, :, 0:1], 1.0))
            own(dve.memset(ROT[:, 1, :, 0:1], 0.0))
            n = 1
            while n < CH:
                wr, wi = (wide(ph(r), n) for r in range(2))
                tr = ST[2][:, 0:PAIRS * n].rearrange("p (q c) -> p q c", c=n)
                cmul(ROT[:, 0, :, n:2 * n], ROT[:, 1, :, n:2 * n], ROT[:, 0, :, 0:n], ROT[:, 1, :, 0:n], wr, wi, tr)
                if 2 * n < CH:
                    cmul(ph(3), ph(4), ph(0), ph(1), ph(0), ph(1), ph(5))
                    own(dve.tensor_copy(ph(0), ph(3)))
                    own(dve.tensor_copy(ph(1), ph(4)))
                n *= 2
            dve.wait_ge(S["s5_t_loaded"], 16 * 8)
            t1 = ST[2][:, :].rearrange("p (q c) -> p q c", c=CH)
            t2_ = ST[3][:, :].rearrange("p (q c) -> p q c", c=CH)
            for half in range(2):
                q = slice(8 * half, 8 * half + 8)
                er, ei = (flat(PS[:, 4 + 2 * r:6 + 2 * r, :]).rearrange("p (q c) -> p q c", c=CH) for r in range(2))
                dve.wait_ge(S["s5_end_done"], half + 1)
                t2(t1, ei, ROT[:, 1, q, :], ALU.mult)
                t2(CR[:, 0, q, :], er, ROT[:, 0, q, :], ALU.mult)
                t2(CR[:, 0, q, :], CR[:, 0, q, :], t1, ALU.add)
                t2(t1, er, ROT[:, 1, q, :], ALU.mult)
                t2(CR[:, 1, q, :], ei, ROT[:, 0, q, :], ALU.mult)
                dve.nop().then_inc(S["s5_end_read"], 1)
                t2(CR[:, 1, q, :], CR[:, 1, q, :], t1, ALU.subtract)
            for r in range(2):
                for q in range(PAIRS):
                    ins = dve.tensor_tensor_scan(CR[:, r, q, :], ph(2)[:, q:q + 1].to_broadcast([P, CH]), CR[:, r, q, :],
                                                 0.0, ALU.mult, ALU.add)
                    own(ins)
            for half in range(2):
                q = slice(8 * half, 8 * half + 8)
                t2(t1, CR[:, 1, q, :], ROT[:, 1, q, :], ALU.mult)
                t2(t2_, CR[:, 0, q, :], ROT[:, 1, q, :], ALU.mult)
                t2(CR[:, 0, q, :], CR[:, 0, q, :], ROT[:, 0, q, :], ALU.mult)
                t2(CR[:, 0, q, :], CR[:, 0, q, :], t1, ALU.subtract)
                t2(CR[:, 1, q, :], CR[:, 1, q, :], ROT[:, 0, q, :], ALU.mult)
                t2(CR[:, 1, q, :], CR[:, 1, q, :], t2_, ALU.add)
            dve.nop().then_inc(S["s5_states_ready"], 1)
            dve.wait_ge(S["lb_exp"], 1)
            own(dve.reciprocal(keep[:, :], floor_[:, :]))
            t2(keep[:, :], keep[:, :], floor_[:, :], ALU.mult)
            t2(floor_[:, :], keep[:, :], keep[:, :], ALU.subtract)
            ts(keep[:, :], floor_[:, :], -1.0, ALU.mult, 1.0, ALU.add)
            ts(floor_[:, :], floor_[:, :], 1e-30, ALU.max)
            dve.wait_ge(S["s5_yt_loaded"], 32)
            for k in range(4):
                y = YT[:, k, :]
                own(dve.scalar_tensor_tensor(y, UT[:, k, :], col("d", k), y, ALU.mult, ALU.add))
                t2(ST[2][:, :], y, y, ALU.mult)
                c = float(np.sqrt(2.0 / np.pi))
                ts(ST[2][:, :], ST[2][:, :], c * 0.044715, ALU.mult, c, ALU.add)
                tt(ST[2][:, :], ST[2][:, :], y, ALU.mult).then_inc(S["glu_tanh_in"], 1)
                dve.wait_ge(S["glu_tanh"], k + 1)
                dve.scalar_tensor_tensor(y, ST[3][:, :], 1.0, y, ALU.add, ALU.mult).then_inc(S["glu_zz"], 1)
                dve.wait_ge(S["mid_hi_done"], k + 1)
                dve.scalar_tensor_tensor(XBl[:, 4 + k, :].rearrange("p (c j) -> p j c", j=L), y.rearrange("p (j c) -> p j c", j=L),
                                         0.5, XBh[:, 4 + k, :].bitcast(F32).rearrange("p (c j) -> p j c", j=L),
                                         ALU.mult, ALU.subtract).then_inc(S["mid_ready"], 1)
            for m in range(4):
                dve.wait_ge(S["glu_sig"], m + 1)
                dve.nop().then_inc(S["acc_free"], 1)
                dve.scalar_tensor_tensor(ST[3][:, :].rearrange("p (c j) -> p c j", j=L), YT[:, m, :].rearrange("p (j c) -> p c j", j=L),
                                         0.5, ST[2][:, :].rearrange("p (c j) -> p c j", j=L), ALU.mult, ALU.mult).then_inc(S["glu_zz"], 1)
                dve.wait_ge(S["mid_hi_done"], 5 + m)
                tt(XBl[:, m, :], ST[3][:, :], XBh[:, m, :].bitcast(F32), ALU.subtract).then_inc(S["mid_ready"], 1)
            dve.wait_ge(S["mid_ready"], 8)
            dve.wait_ge(S["masks_ready"], 1)

            def told(ins, name):
                ins.then_inc(S[name], 1)

            def clamp_f(hd, half):
                dve.wait_ge(S["hg_f_loaded"], hd * 32 + (16 * half + 16))
                t2(TA[:, :], F[:, :], RSTD[:, half * HALF:(half + 1) * HALF], ALU.mult)
                told(dve.tensor_scalar(TA[:, :], TA[:, :], -80.0, None, ALU.max), "hg_f")

            def cumulate(hd, half):
                un = hd * 2 + half
                dve.wait_ge(S["hg_sigmoid_f"], un + 1)
                told(dve.scalar_tensor_tensor(KK[:, half, :], TB[:, :], keep[:, bass.ds(hd, 1)], TC[:, :], ALU.mult, ALU.mult), "hg_k_made")
                dve.wait_ge(S["hg_log_f"], un + 1)
                for c in range(4):
                    t = slice(c * P, (c + 1) * P)
                    ins = dve.tensor_tensor_scan(BC[:, t], ones[:, :], TD[:, t], 0.0, ALU.mult, ALU.add)
                told(ins, "hg_cumulated")
                dve.wait_ge(S["hg_cumulated"], un + 1)
                bc = BC[:, :].rearrange("p (c t) -> p c t", t=P)
                told(tt(TD[:, :].rearrange("p (c t) -> p c t", t=P), bc, bc[:, :, P - 1:P].to_broadcast([P, 4, P]), ALU.subtract), "hg_to_end")

            def level_exponents(half, some):
                for l in some:
                    w = LEVELS[l]
                    b4, lv = (ap.rearrange("p (n two w) -> p n two w", two=2, w=w) for ap in (BC[:, :], LVL[:, half, l, :]))
                    ref = b4[:, :, 0, w - 1:w].to_broadcast([P, HALF // (2 * w), w])
                    tt(lv[:, :, 0, :], b4[:, :, 0, :], ref, ALU.subtract)
                    told(tt(lv[:, :, 1, :], ref, b4[:, :, 1, :], ALU.subtract), "hg_level")

            def mean_square(hd, half):
                dve.wait_ge(S["hg_ss"], hd * 2 + (half + 1))
                if half == 1:
                    dve.wait_ge(S["hg_y_low"], hd * 2 + 1)
                told(dve.tensor_scalar(PD[:, :], PS[:, 1, :], 1.0 / P, EPS, ALU.mult, ALU.add), "hg_ss_read")

            def product(hd, half):
                o = OUTH[:, half, :]
                dve.wait_ge(S["hg_rstd"], hd * 2 + (half + 1))
                if half == 0:
                    dve.wait_ge(S["hg_gate_made"], hd + 1)
                t2(o, o, PD[:, :], ALU.mult)
                told(dve.scalar_tensor_tensor(PD[:, :], o, COLS[:, bass.ds(hd + ROW["head_norm"], 1)], PC[:, half * HALF:(half + 1) * HALF],
                                              ALU.mult, ALU.mult), "hg_y_ready")

            def y_low(hd, half):
                dve.wait_ge(S["hg_y_high"], hd * 2 + (half + 1))
                t = slice(half * HALF, (half + 1) * HALF)
                hi, lo = (x[:, bass.ds(hd + 4, 1), t].rearrange("p a t -> p (a t)") for x in (XBh, XBl))
                told(tt(lo, PD[:, :], hi.bitcast(F32), ALU.subtract), "hg_y_low")

            def head(hd, last):
                for c in range(NB):
                    half, b = c // 4, c % 2
                    if c:
                        dve.wait_ge(S["hg_ds_done"], hd * (NB - 1) + c)
                        if c == 1:
                            told(dve.tensor_copy(SS[:, :], PS[:, 2, 0:P]), "hg_state")
                        else:
                            end = ENDS[:, (c - 1) // 4, (c - 1) % 4:(c - 1) % 4 + 1]
                            dve.wait_ge(S["hg_state"], hd * (NB - 1) + (c - 1 + CREDIT))
                            told(dve.scalar_tensor_tensor(SS[:, :], SS[:, :], end, PS[:, 2, 0:P], ALU.mult, ALU.add), "hg_state")
                    dve.wait_ge(S["hg_lvl_done"], hd * NB + (c + 1))
                    told(tt(MP[:, b, :, :].rearrange("p l t -> p (l t)"), flat(PS[:, 4 + 2 * b:6 + 2 * b, :]),
                            MASK[:, :, :].rearrange("p l t -> p (l t)"), ALU.mult), "hg_lvl_read")
                    dve.wait_ge(S["hg_lvl_read"], hd * NB + (c + 1 + CREDIT))
                    told(dve.tensor_reduce(AT[:, b, :], MP[:, b, :, :].rearrange("p l t -> p t l"), X, ALU.add), "hg_att")
                    if c == 5:
                        mean_square(hd, 0)
                    if c == 7:
                        product(hd, 0)
                    if not (last and half == 1):
                        if c % 4 == 0:
                            cumulate(hd + half, 1 - half)
                        if c % 4 == 1:
                            level_exponents(1 - half, range(4))
                        if c % 4 == 2:
                            level_exponents(1 - half, range(4, 7))
                            if not last:
                                clamp_f(hd + 1, half)
                y_low(hd, 0)
                mean_square(hd, 1)
                product(hd, 1)
                y_low(hd, 1)

            clamp_f(0, 0)
            cumulate(0, 0)
            level_exponents(0, range(7))
            clamp_f(0, 1)
            with own.loop(HEADS - 1, 4) as hd:
                head(hd, False)
            head(HEADS - 1, True)

            def residual(u0, norm, gain, factor):
                start_norm()
                with dve.Fori(0, KT // 2) as i:
                    for b in range(2):
                        m = i * 2 + b
                        dve.wait_ge(S["acc_done"], i * 2 + (u0 + b + 1))
                        h = tile(H, m)
                        if factor is None:
                            tt(h, flat(ACC[b]), h, ALU.add).then_inc(S["acc_free"], 1)
                            dve.wait_ge(S["acc_free"], i * 2 + (free_of(u0)[1] + b))
                        else:
                            tt(ST[0][:, :], flat(ACC[b]), factor, ALU.mult).then_inc(S["acc_free"], 1)
                            dve.wait_ge(S["acc_free"], i * 2 + (free_of(u0)[1] + b))
                            tt(h, h, ST[0][:, :], ALU.add).then_inc(S["h_ready"], 1)
                        if factor is None:
                            dve.nop().then_inc(S["h_ready"], 1)
                        low(norm, m, ROW[gain[0]] + gain[1])
                end_norm()

            def mlp(name, norm, mid0, after):
                u0 = UNIT[name]
                f0 = free_of(u0)[1]

                def up(c):
                    with dve.Fori(0, 4) as i:
                        for b in range(2):
                            off = c * 16 + i * 2 + b
                            dve.wait_ge(S["acc_done"], off + (u0 + 1))
                            dve.tensor_scalar(ST[0][:, :], flat(ACC[b]), 0.0, None, ALU.max).then_inc(S["acc_free"], 1)
                            dve.wait_ge(S["mid_hi_done"], c * 8 + i * 2 + (mid0 + b + 1))
                            tt(tile(XBl, i * 2 + b), ST[1][:, :], tile(XBh, i * 2 + b).bitcast(F32), ALU.subtract).then_inc(S["mid_ready"], 1)

                def down(c):
                    base_ = own.n
                    with dve.Fori(0, 4) as i:
                        for b in range(2):
                            off = c * 16 + i * 2 + b
                            dve.wait_ge(S["acc_done"], off + (u0 + 9))
                            tt(ST[0][:, :], flat(ACC[b]), RSTD[:, :], ALU.mult).then_inc(S["acc_free"], 1)
                            dve.wait_ge(S["acc_free"], off + (f0 + 8))
                            h = tile(H, i * 2 + b)
                            own.n = c * 8 + i * 2 + (start + b)
                            own(tt(h, h, ST[0][:, :], ALU.add))

                with dve.Fori(0, 4) as i:
                    for b in range(2):
                        dve.wait_ge(S["acc_done"], i * 2 + (u0 + b + 1))
                        dve.tensor_scalar(ST[0][:, :], flat(ACC[b]), 0.0, None, ALU.max).then_inc(S["acc_free"], 1)
                        dve.wait_ge(S["mid_hi_done"], i * 2 + (mid0 + b + 1))
                        tt(tile(XBl, i * 2 + b), ST[1][:, :], tile(XBh, i * 2 + b).bitcast(F32), ALU.subtract).then_inc(S["mid_ready"], 1)
                dve.wait_ge(S["mid_ready"], mid0 + 8)
                rstd_squared(norm)
                start = own.n
                with dve.Fori(0, 3) as c:
                    down(c)
                    up(c + 1)
                own.n = start + 24
                residual(u0 + 56, *after, RSTD[:, :])

            def embed(i, norm, nroot, after, gain, last=False):
                u0 = UNIT[f"gate{i}"]
                rstd(norm, nroot)
                for m in range(KT):
                    dve.wait_ge(S["acc_done"], u0 + m + 1)
                    if m >= 2:
                        dve.wait_ge(S["gate_done"], 8 * i + m - 1)
                    tt(ST[m % 2][:, :], flat(ACC[m % 2]), RSTD[:, :], ALU.mult).then_inc(S["acc_free"], 1)
                    dve.wait_ge(S["acc_free"], free_of(u0)[1] + m)
                    if m in (2, 3):
                        k = m - 2
                        dve.wait_ge(S["p_hi"], 2 * i + k + 1)
                        tt(PTl[:, k, :], flat(PS[:, 4 + 2 * k:6 + 2 * k, :]), PTh[:, k, :].bitcast(F32), ALU.subtract).then_inc(S["p_ready"], 1)
                dve.wait_ge(S["gate_done"], 8 * i + 8)
                u0 = UNIT[f"up{i}"]
                start_norm()
                for m in range(KT):
                    dve.wait_ge(S["acc_done"], u0 + m + 1)
                    tt(ST[0][:, :], flat(ACC[m % 2]), GATE[:, m, :], ALU.mult).then_inc(S["acc_free"], 1)
                    dve.wait_ge(S["acc_free"], free_of(u0)[1] + m)
                    tt(H[:, m, :], H[:, m, :], ST[0][:, :], ALU.add).then_inc(S["h_ready"], 1)
                    if last:
                        add_squares(after, m)
                    else:
                        low(after, m, ROW[gain[0]] + gain[1])
                end_norm()

            dve.wait_ge(S["h_restored"], 16)
            residual(UNIT["out"], 1, ("mlp", 0), None)
            mlp("mlp0", 1, 8, (2, ("ple", 0)))
            embed(0, 2, 1, 3, ("mix", 8))
            rstd(3, 2)
            for u in range(12):
                dve.wait_ge(S["acc_done"], UNIT["qkv"] + u + 1)
                dve.wait_ge(spilled[u % 2], 16 * (10 + u // 2))
                tt(ST[u % 2][:, :], flat(ACC[u % 2]), RSTD[:, :], ALU.mult).then_inc(S["acc_free"], 1)
            dve.wait_ge(S["dist_ready"], 1)
            dve.wait_ge(S["slopes_ready"], 1)
            dve.wait_ge(S["sinks_loaded"], 16)
            with own.loop(KVH // 2, AT_STEPS) as gp:

                def bias(par):
                    dve.wait_ge(at_loaded[par], gp * 64 + 64)
                    for s, j in enumerate((0, 2, 1, 3)):
                        own(dve.tensor_scalar(BIAS[:, par, s, :], dist[:, :], slope[:, bass.ds(gp * 8 + (4 * par + j), 1)], None, ALU.mult))

                def score(i):
                    par, s, lo = i // NB, i % RING, (P if i % NB == 0 else 0)
                    sc = SC[:, s, :, lo:]
                    dve.wait_ge(S["at_qk_done"], gp * BODY + (i + 1 + CREDIT))
                    dve.wait_ge(S["at_pt_done"], gp * BODY + (max(i - RING + 1, 0) + CREDIT))
                    b = i % 2
                    ps = PS[:, 4 + 2 * b:6 + 2 * b, :].rearrange("p a (j s) -> p (a j) s", j=2)[:, :, lo:]
                    dve.scalar_tensor_tensor(sc, ps, HD ** -0.5, BIAS[:, par, :, lo:], ALU.mult, ALU.add).then_inc(S["at_scored"], 1)
                    dve.wait_ge(S["at_scored"], gp * BODY + (i + 1 + CREDIT))
                    own(dve.tensor_reduce(sm[:, 0, s, :], sc, X, ALU.max))
                    sk = sink[:, bass.ds(gp * 8 + 4 * par, 4)].rearrange("p (j r) -> p r j", r=2)
                    mx, ex = (sm[:, k, s, :].rearrange("p (r j) -> p r j", r=2) for k in (0, 3))
                    own(tt(mx, mx, sk, ALU.max))
                    own(tt(ex, sk, mx, ALU.subtract))
                    dve.tensor_scalar(sm[:, 0, s, :], sm[:, 0, s, :], -1.0, None, ALU.mult).then_inc(S["at_max"], 1)

                def denominators(i):
                    s = i % RING
                    dve.wait_ge(S["at_exp"], gp * BODY + (i + 1))
                    own(tt(sm[:, 2, s, :], sm[:, 1, s, :], sm[:, 3, s, :], ALU.add))
                    dve.reciprocal(sm[:, 2, s, :], sm[:, 2, s, :]).then_inc(S["at_den"], 1)

                def out_low(i):
                    n = i % NB
                    dve.wait_ge(S["at_o_hi"], gp * BODY + (i + 1))
                    t, heads = slice(n * P, (n + 1) * P), bass.ds(gp * 4 + 2 * (i // NB), 2)
                    tt(XBl[:, heads, t], PS[:, 2 + i % 2, 0:256].rearrange("p (j t) -> p j t", t=P),
                       XBh[:, heads, t].bitcast(F32), ALU.subtract).then_inc(S["at_o_done_lo"], 1)

                for i in range(BODY + AHEAD + 1):
                    if i < BODY:
                        if i % NB == 0:
                            bias(i // NB)
                        score(i)
                    if 1 <= i <= BODY:
                        denominators(i - 1)
                    if i > AHEAD:
                        out_low(i - AHEAD - 1)
            residual(UNIT["wo"], 4, ("mlp", 8), None)
            mlp("mlp1", 4, 40, (5, ("ple", 8)))
            embed(1, 5, 3, 6, None, last=True)
            rstd(6, 4)
            for m in range(KT):
                dve.scalar_tensor_tensor(H[:, m, :], H[:, m, :], col("final", m), RSTD[:, :], ALU.mult, ALU.mult).then_inc(S["fin_ready"], 1)


_SHAPES = dict(
    x=(1, T, D), p=(2, 1, T, PLE), mix_norm=(2, D), mlp_norm=(2, D), ple_norm=(2, D), final_norm=(D,),
    w_in_even=(1, D, 5 * S5W), w_out_even=(1, D, D), s5_lam_re=(1, GROUPS, STATES), s5_lam_im=(1, GROUPS, STATES),
    s5_log_dt=(1, GROUPS), s5_b_re=(1, GROUPS, STATES, GRP), s5_b_im=(1, GROUPS, STATES, GRP),
    s5_c_re=(1, GROUPS, GRP, STATES), s5_c_im=(1, GROUPS, GRP, STATES), s5_d=(1, GROUPS, GRP),
    s5_w_glu=(1, S5W, S5W), s5_b_glu=(1, S5W), hgrn_lb_logits=(1, S5W), hgrn_norm=(1, HEADS, P),
    w_qkv_odd=(1, D, 12 * P), w_o_odd=(1, D, D), attn_sinks=(1, QH), w_mlp_in=(2, D, FF), w_mlp_out=(2, FF, D),
    w_ple_up=(2, PLE, D), w_ple_gate=(2, D, D))


def kernel(**inputs):
    import concourse.bacc as bacc
    from concourse.bass_utils import run_bass_kernel_spmd

    nc = bacc.Bacc("TRN2", target_bir_lowering=False, num_devices=1)
    arrays = {f"{n}_in": np.ascontiguousarray(inputs[n]) for n in _SHAPES}
    a = {n: nc.dram_tensor(f"{n}_in", shape, F32, kind="ExternalInput").ap() for n, shape in _SHAPES.items()}
    out = nc.dram_tensor("out", (1, T, D), F32, kind="ExternalOutput").ap()
    build(nc, a, out)
    return run_bass_kernel_spmd(nc, [arrays], core_ids=[0]).results[0]["out"]
```

```python
from contextlib import ExitStack, contextmanager

import numpy as np

import concourse.bass as bass
from concourse import mybir

F32, F32R = mybir.dt.float32, mybir.dt.float32r
ALU, ACT = mybir.AluOpType, mybir.ActivationFunctionType
X = mybir.AxisListType.X

P = 128
D, T, FF, PLE = 1024, 1024, 4096, 256
KT = D // P
NB = T // P
HALF = 512
EPS = 1e-6
S5W, GRP, STATES = 512, 16, 64
GROUPS, PAIRS = 32, 16
L = 8
CH = T // L
HEADS = 4
LEVELS = [64, 32, 16, 8, 4, 2, 1]
AT_STEPS = 56
QH, KVH, HD = 16, 4, 64
BODY = 2 * NB
AHEAD = 3
RING = 4
FAR = 1.0e32
CREDIT = 1
TWO_PI = 6.283185307179586
MAGIC = 12582912.0

SLAB = dict(u=0, heads=4, glu=20, out=22, mlp0=30, gate0=94, up0=102, qkv=104, wo=116, mlp1=124, gate1=188, up1=196)
UNIT = dict(u=0, heads=4, glu=20, out=24, mlp0=32, gate0=96, up0=104, qkv=112, wo=124, mlp1=132, gate1=196, up1=204)
ROW = dict(mix=0, mlp=16, ple=32, final=48, head_norm=56, b_glu=60, lb=64, d=68, lam_re=72, lam_im=88)
N_ROWS = 104


class Own:

    def __init__(self, eng, sem):
        self.eng, self.sem, self.n, self.taken = eng, sem, 0, 0

    def __call__(self, ins):
        ins.then_inc(self.sem, 1)
        self.n = self.n + 1
        self.taken += 1
        self.eng.wait_ge(self.sem, self.n)

    @contextmanager
    def loop(self, count, steps):
        base, outer = self.n, self.taken
        with self.eng.Fori(0, count) as i:
            self.n, self.taken = i * steps + base, 0
            yield i
        assert self.taken == steps, (self.taken, steps)
        self.n, self.taken = base + count * steps, outer + count * steps


def build(nc, a, out):
    ctx = ExitStack()
    base = 16512

    def at(name, shape, dt, offset):
        return nc.alloc_sbuf_tensor_at(name, shape, dt, offset=offset)

    K = 1024
    H_AT, XAH_AT, XAL_AT, XBH_AT, XBL_AT = (base + i * 32 * K for i in range(5))
    RAW_AT = base + 160 * K
    W_AT = RAW_AT + 8 * K
    MISC_AT = W_AT + 16 * K

    H = at("residual", [P, KT, T], F32, H_AT)
    XAh, XAl = at("x_hi", [P, KT, T], F32R, XAH_AT), at("x_lo", [P, KT, T], F32R, XAL_AT)
    XBh, XBl = at("mid_hi", [P, KT, T], F32R, XBH_AT), at("mid_lo", [P, KT, T], F32R, XBL_AT)
    RAW = at("w_raw", [P, 2, KT * P], F32, RAW_AT)
    WH, WL = at("w_hi", [P, 2, KT * P], F32R, W_AT), at("w_lo", [P, 2, KT * P], F32R, W_AT + 8 * K)
    RSTD = at("rstd", [P, T], F32, MISC_AT)
    ST = [at(f"stage{i}", [P, T], F32, MISC_AT + (1 + i) * 4 * K) for i in range(4)]
    SUMSQ, SQ = ST[3], ST[2]
    small_at = [MISC_AT + 20 * K]

    def small(name, shape):
        n = -(-int(np.prod(shape[1:])) * 4 // 32) * 32
        o = small_at[0]
        small_at[0] += n
        assert small_at[0] <= 229368, small_at[0]
        return at(name, shape, F32, o)

    ident, ones = small("identity", [P, P]), small("ones", [P, P])
    COLS = small("vectors", [P, N_ROWS])
    dist = small("distance", [P, 2 * P])
    sink, neg_sink, slope = small("sinks", [P, QH]), small("neg_sinks", [P, QH]), small("neg_slopes", [P, QH])
    log_dt = small("s5_log_dt", [P, GROUPS])
    keep, floor_ = small("one_minus_lb", [P, HEADS]), small("lb_floor", [P, HEADS])
    sm = small("softmax_stats", [P, 4, RING, 4])
    root_mean = small("final_rstd", [P, 2, NB // 2])
    phase = small("s5_phase", [P, 6, PAIRS])

    def col(name, i):
        return COLS[:, ROW[name] + i:ROW[name] + i + 1]

    U = at("s5_u", [P, GROUPS, CH], F32, H_AT)
    TOEP = at("s5_toeplitz", [P, GROUPS, P], F32, H_AT + 16 * K)
    EW = at("s5_end_weights", [P, PAIRS, 2, P], F32, XBH_AT)
    YS = at("s5_y_chunks", [P, GROUPS, CH], F32, XBH_AT)
    BA = at("s5_ba", [P, 2, PAIRS, L, GRP], F32, XBH_AT + 16 * K)
    GK = at("s5_kernel", [GRP, GROUPS, P], F32, XBH_AT + 16 * K)
    CR = at("s5_state", [P, 2, PAIRS, CH], F32, XBH_AT + 16 * K)
    ROT = at("s5_rotation", [P, 2, PAIRS, CH], F32, XBL_AT)
    CA = at("s5_ca", [P, 2, PAIRS, L, GRP], F32, XBL_AT + 16 * K)
    CROW = at("s5_c_rows", [P, 2, 2, P], F32, XBL_AT)
    BRAW = at("s5_b", [P, 2, PAIRS, GRP], F32, XBL_AT + 2 * K)
    BB = at("s5_bbar", [P, 2, PAIRS, GRP], F32, XBL_AT + 4 * K)
    C0 = at("s5_c", [P, 2, PAIRS, GRP], F32, XBL_AT + 6 * K)
    PW = at("s5_powers", [P, 2, PAIRS, L + 1], F32, XBL_AT + 8 * K)
    PR = at("s5_params", [P, 28, PAIRS], F32, XBL_AT + 10 * K)
    PT1 = at("s5_tmp", [P, 1024], F32, XBL_AT + 12 * K)
    YT = at("s5_y", [P, 4, T], F32, H_AT)
    UT = at("s5_ut", [P, 4, T], F32, XBL_AT)

    XS = at("x_tokens", [P, KT, NB, P], F32, XBH_AT)
    ROWS = at("vector_rows", [N_ROWS, P], F32, MISC_AT + 4 * K)

    hg = XAH_AT
    QV = at("hg_qv", [P, 2, 2, HALF], F32, hg)
    G = at("hg_g", [P, T], F32, hg + 8 * K)
    LVL = at("hg_levels", [P, 2, 7, HALF], F32, hg + 12 * K)
    KK = at("hg_k", [P, 2, HALF], F32, hg + 40 * K)
    QB = at("hg_q_decayed", [P, 2, HALF], F32, hg + 44 * K)
    KD = at("hg_k_decayed", [P, 2, HALF], F32, hg + 48 * K)
    OUTH = at("hg_out", [P, 2, HALF], F32, hg + 52 * K)
    F = at("hg_f", [P, HALF], F32, hg + 56 * K)
    BC = at("hg_cumulative", [P, HALF], F32, hg + 58 * K)
    TA = at("hg_tmp_a", [P, HALF], F32, hg + 60 * K)
    TB = at("hg_tmp_b", [P, HALF], F32, hg + 62 * K)
    TC = at("hg_tmp_c", [P, HALF], F32, H_AT + 20 * K)
    TD = at("hg_tmp_d", [P, HALF], F32, H_AT + 22 * K)
    ENDS = at("hg_chunk_decay", [P, 2, HALF // P], F32, H_AT + 24 * K)
    MASK = at("hg_masks", [P, 8, P], F32, H_AT + 16 * K)
    MP = at("hg_masked", [P, 2, 8, P], F32, H_AT)
    PC = at("hg_gate", [P, T], F32, H_AT + 8 * K)
    PA = at("hg_squares", [P, HALF], F32, H_AT + 12 * K)
    PD = at("hg_product", [P, HALF], F32, H_AT + 14 * K)
    VK = at("hg_v_kd_tokens", [P, 2, 2, P], F32, H_AT + 28 * K)
    AT = at("hg_att", [P, 2, P], F32, H_AT + 30 * K)
    SS = at("hg_state", [P, P], F32, H_AT + 31 * K)

    AQ = at("at_q", [P, 2, 2, T], F32, XAH_AT)
    AK = at("at_k", [P, 2, T], F32, XAH_AT + 16 * K)
    AV = at("at_v", [HD, 2, T], F32, XAH_AT + 24 * K)
    AVT = at("at_v_tokens", [P, 2, NB, HD], F32, XAL_AT)
    BIAS = at("at_bias", [P, 2, 4, 2 * P], F32, XAL_AT + 4 * K)
    SC = at("at_scores", [P, RING, 4, 2 * P], F32, XAL_AT + 12 * K)
    PT = at("at_probs_t", [P, 2, 4, P], F32, XAL_AT + 28 * K)

    PTh, PTl = at("p_hi", [P, 2, T], F32R, XBH_AT), at("p_lo", [P, 2, T], F32R, XBH_AT + 8 * K)
    PIN = at("p_tokens", [P, NB, PLE], F32, XBH_AT + 16 * K)
    GATE = at("gate", [P, KT, T], F32, XBL_AT)

    OT = at("out_tokens", [P, NB, D], F32, XAH_AT)
    HG = at("residual_gain", [P, KT, T], F32, XAL_AT)

    def dram(name, shape):
        return nc.dram_tensor(name, shape, F32, kind="Internal").ap()

    h_dram = dram("residual_dram", [D, T])
    u_dram = dram("u_dram", [S5W, T])
    y_dram = dram("y_dram", [S5W, T])
    fqig_dram = dram("fqig_dram", [HEADS * 4 * P, T])
    qkv_dram = dram("qkv_dram", [12 * P, T])

    with ctx:
        PS = ctx.enter_context(nc.psum_tensor("ps", [P, 8, HALF], F32))
        ACC = [PS[:, 0:2, :], PS[:, 2:4, :]]

        def flat(ap):
            return ap.rearrange("p a b -> p (a b)")

        def sem(name):
            return ctx.enter_context(nc.semaphore(name))

        names = """acc_done acc_free acc_free_act w_hi_done w_ready x_hi_done x_ready mid_hi_done mid_ready h_ready sq_done
        sq_used sumsq_ready ss_done ss_read rcp_done rstd_done consts_ready gains_loaded rows_loaded cols_done
        cols_ready sinks_loaded x_tr_done x_tr_dve x_tr_act dve_step act_step pool_step act_passed pool_passed
        pe_passed h_spilled h_restored s5_raw_loaded s5_c_tr s5_dve s5_act s5_ba_ready s5_ca_ready s5_ew_tr
        s5_ew_copied s5_g_done s5_g_copied s5_t_zeroed s5_t_loaded s5_u_loaded s5_end_done s5_end_read s5_states_ready
        s5_y_done s5_y_copied s5_y_stored s5_ut_loaded lb_in lb_exp glu_tanh_in glu_tanh glu_zz glu_sig masks_ready
        hg_f_loaded hg_g_loaded hg_f hg_sigmoid_f hg_log_f hg_k_made hg_cumulated hg_to_end hg_exp_b hg_exp_end
        hg_level hg_level_exp hg_qv_scaled hg_decayed hg_levels hg_g_scaled hg_sigmoid_g hg_gate_made hg_tr
        hg_tr_copied hg_lvl_done hg_lvl_read hg_att hg_ds_done hg_state hg_o_done hg_o_copied hg_squares_made hg_ss
        hg_ss_read hg_rstd hg_y_ready hg_y_high hg_y_low dist_ready slopes_ready at_vt_done at_vt_copied at_qk_done
        at_scored at_max at_exp at_den at_norm at_pt_done at_pt_copied at_o_done at_o_hi at_o_done_lo p_loaded p_tr
        p_hi p_ready gate_done last_done last_free last_h last_sq last_sq_used last_gain last_tr last_copied last_ss
        last_var last_root scaled_dve scaled_act""".split()
        S = {n: sem(n) for n in names}
        w_loaded = [sem(f"w_loaded{i}") for i in range(2)]
        spilled = [sem(f"spilled{i}") for i in range(2)]
        yt_loaded = [sem(f"s5_yt_loaded{i}") for i in range(4)]
        x_loaded = [sem(f"x_loaded{i}") for i in range(NB)]
        hg_qv_loaded = [sem(f"hg_qv_loaded{i}") for i in range(2)]
        at_loaded = [sem(f"at_loaded{i}") for i in range(2)]
        out_stored = [sem(f"out_stored{i}") for i in range(2)]

        def free_of(u):
            if 4 <= u < 20:
                return S["acc_free_act"], u - 3
            return S["acc_free"], (u + 1 if u < 4 else u - 15)

        block = ctx.enter_context(nc.Block())

        @block.sync
        def _(sp):
            def load(b, need, src):
                if need is not None:
                    sp.wait_ge(S["w_ready"], need)
                dst = RAW[:, b, :].rearrange("p (k n) -> p k n", n=src.shape[-1])
                sp.dma_start(dst, src).then_inc(w_loaded[b], 16)

            def cols(w, c):
                return w[:, c].rearrange("(k p) n -> p k n", p=P)

            def run(s0, n, w, c0=0):
                with sp.Fori(0, n // 2) as i:
                    for b in range(2):
                        load(b, i * 2 + (s0 + b - 1), cols(w, bass.ds(i * 2 * P + (c0 + b * P), P)))

            def mlp(s0, i):
                w_in, w_out = a["w_mlp_in"][i], a["w_mlp_out"][i]
                with sp.Fori(0, 4) as c:
                    with sp.Fori(0, 4) as m:
                        for b in range(2):
                            load(b, c * 16 + m * 2 + (s0 + b - 1), cols(w_in, bass.ds(c * 1024 + m * 256 + b * P, P)))
                    with sp.Fori(0, 4) as m:
                        for b in range(2):
                            src = w_out[bass.ds(c * 1024, 1024), bass.ds(m * 256 + b * P, P)]
                            load(b, c * 16 + m * 2 + (s0 + 8 + b - 1), src.rearrange("(k p) n -> p k n", p=P))

            def ple_up(s0, i):
                for s in range(2):
                    src = a["w_ple_up"][i][:, s * HALF:(s + 1) * HALF].rearrange("(k p) n -> p k n", p=P)
                    load(s, s0 + s - 1, src)

            w_in = a["w_in_even"][0]
            def rows(name, n, src):
                sp.dma_start(ROWS[ROW[name]:ROW[name] + n, :], src).then_inc(S["rows_loaded"], 16)

            sp.dma_start(ROWS[0:16, :], a["mix_norm"].rearrange("i (k p) -> (i k) p", p=P)).then_inc(S["gains_loaded"], 16)
            for k in range(KT):
                src = a["x"][0, :, k * P:(k + 1) * P].rearrange("(n p) f -> p n f", p=P)
                sp.dma_start(XS[:, k, :, :], src).then_inc(x_loaded[k], 16)
                if k < 2:
                    load(k, None, cols(w_in, slice(k * P, (k + 1) * P)))
            rows("mlp", 16, a["mlp_norm"].rearrange("i (k p) -> (i k) p", p=P))
            rows("ple", 16, a["ple_norm"].rearrange("i (k p) -> (i k) p", p=P))
            rows("final", 8, a["final_norm"].rearrange("(k p) -> k p", p=P))
            rows("head_norm", 4, a["hgrn_norm"][0])
            rows("b_glu", 4, a["s5_b_glu"][0].rearrange("(k p) -> k p", p=P))
            rows("lb", 4, a["hgrn_lb_logits"][0].rearrange("(k p) -> k p", p=P))
            rows("d", 4, a["s5_d"][0].rearrange("(k g) h -> k (g h)", k=4))
            rows("lam_re", 16, a["s5_lam_re"][0].rearrange("(q two) p -> q (two p)", two=2))
            rows("lam_im", 16, a["s5_lam_im"][0].rearrange("(q two) p -> q (two p)", two=2))
            sp.dma_start(sink[:, :], a["attn_sinks"][0].unsqueeze(0).to_broadcast([P, QH])).then_inc(S["sinks_loaded"], 16)
            sp.dma_start(log_dt[:, :], a["s5_log_dt"][0].unsqueeze(0).to_broadcast([P, GROUPS])).then_inc(S["s5_raw_loaded"], 16)
            for r, (b, c) in enumerate((("s5_b_re", "s5_c_re"), ("s5_b_im", "s5_c_im"))):
                for two in range(2):
                    sp.dma_start(BRAW[two * STATES:(two + 1) * STATES, r, :, :],
                                  a[b][0].rearrange("(q two) p h -> two p q h", two=2)[two]).then_inc(S["s5_raw_loaded"], 16)
                    for h in range(2):
                        sp.dma_start(CROW[:, h, r, two * STATES:(two + 1) * STATES],
                                      a[c][0].rearrange("(h q two) c p -> h two q c p", h=2, two=2)[h, two])\
                            .then_inc(S["s5_raw_loaded"], 16)
            for s in range(2, 4):
                load(s % 2, s - 1, cols(w_in, slice(s * P, (s + 1) * P)))
            with sp.Fori(0, HEADS) as hd:
                for j, c0 in enumerate((2 * S5W, S5W, 3 * S5W, 4 * S5W)):
                    load(j % 2, hd * 4 + (4 + j - 1), cols(w_in, bass.ds(hd * P + c0, P)))
            for s in range(2):
                src = a["s5_w_glu"][0][:, s * 256:(s + 1) * 256].rearrange("(k p) n -> p k n", p=P)
                load(s, 20 + s - 1, src)
            w = a["w_out_even"][0]
            for b in range(2):
                load(b, 22 + b - 1, cols(w, slice(b * P, (b + 1) * P)))
            for b in range(2):
                sp.wait_ge(spilled[b], 16 * 10)
            sp.wait_ge(S["acc_done"], 20)

            def hg_load(dst, hd, j, tokens, signal):
                sp.dma_start(dst, fqig_dram[bass.ds(hd * 4 * P + j * P, P), tokens]).then_inc(signal, 16)

            def f_load(hd, half):
                hg_load(F[:, :], hd, 0, slice(half * HALF, (half + 1) * HALF), S["hg_f_loaded"])

            def qv_load(hd, half):
                for j in range(2):
                    hg_load(QV[:, half, j, :], hd, 1 + j, slice(half * HALF, (half + 1) * HALF), hg_qv_loaded[half])

            f_load(0, 0)
            qv_load(0, 0)
            qv_load(0, 1)
            hg_load(G[:, :], 0, 3, slice(0, T), S["hg_g_loaded"])
            sp.wait_ge(S["hg_f"], 1)
            f_load(0, 1)
            with sp.Fori(1, HEADS) as hd:
                for half in range(2):
                    sp.wait_ge(S["hg_f"], hd * 2 + half)
                    f_load(hd, half)
                    sp.wait_ge(S["hg_lvl_done"], hd * NB + (half - 1) * NB // 2)
                    qv_load(hd, half)
                    if half == 0:
                        sp.wait_ge(S["hg_gate_made"], hd)
                        hg_load(G[:, :], hd, 3, slice(0, T), S["hg_g_loaded"])
            sp.wait_ge(S["hg_y_low"], 2 * HEADS)
            sp.wait_ge(S["h_spilled"], 16)
            sp.dma_start(H[:, :, :], h_dram.rearrange("(k p) t -> p k t", p=P)).then_inc(S["h_restored"], 16)
            with sp.Fori(1, 4) as i:
                for b in range(2):
                    load(b, i * 2 + (22 + b - 1), cols(w, bass.ds(i * 256 + b * P, P)))
            mlp(SLAB["mlp0"], 0)
            run(SLAB["gate0"], 8, a["w_ple_gate"][0])
            ple_up(SLAB["up0"], 0)
            run(SLAB["qkv"], 12, a["w_qkv_odd"][0])
            w = a["w_o_odd"][0]
            for b in range(2):
                load(b, SLAB["wo"] + b - 1, cols(w, slice(b * P, (b + 1) * P)))
            for b in range(2):
                sp.wait_ge(spilled[b], 16 * 16)
            for g in range(KVH):
                par = g % 2
                if g >= 2:
                    sp.wait_ge(S["at_vt_done"], g - 1 + CREDIT)
                    sp.wait_ge(S["at_qk_done"], (g - 1) * NB + CREDIT)
                q = qkv_dram[g * 256:(g + 1) * 256, :].rearrange("(j p) t -> p j t", p=P)
                sp.dma_start(AQ[:, par, :, :], q).then_inc(at_loaded[par], 16)
                for r in range(2):
                    k = qkv_dram[1024 + g * HD:1024 + (g + 1) * HD, :]
                    sp.dma_start(AK[r * HD:(r + 1) * HD, par, :], k).then_inc(at_loaded[par], 16)
                sp.dma_start(AV[:, par, :], qkv_dram[1280 + g * HD:1280 + (g + 1) * HD, :]).then_inc(at_loaded[par], 16)
            with sp.Fori(1, 4) as i:
                for b in range(2):
                    load(b, i * 2 + (SLAB["wo"] + b - 1), cols(w, bass.ds(i * 256 + b * P, P)))
            mlp(SLAB["mlp1"], 1)
            run(SLAB["gate1"], 8, a["w_ple_gate"][1])
            ple_up(SLAB["up1"], 1)
            for n in range(NB):
                sp.wait_ge(S[("scaled_dve", "scaled_act")[n % 2]], n // 2 + 1)
                sp.dma_start(out[0, n * P:(n + 1) * P, :], OT[:, n, :]).then_inc(out_stored[n % 2], 16)
            for b in range(2):
                sp.wait_ge(out_stored[b], 16 * NB // 2)

        @block.gpsimd
        def _(pool):
            own = Own(pool, S["pool_step"])

            own(pool.memset(ident[:, :], 1.0))
            own(pool.affine_select(out=ident[:, :], in_=ident[:, :], compare_op=ALU.is_equal, fill=0.0,
                                   base=0, pattern=[[-1, P]], channel_multiplier=1))
            pool.memset(ones[:, :], 1.0).then_inc(S["consts_ready"], 1)
            own(pool.iota(dist[:, :], [[-1, 2 * P]], base=P, channel_multiplier=1, allow_small_or_imprecise_dtypes=True))
            own(pool.affine_select(out=dist[:, :], in_=dist[:, :], compare_op=ALU.is_ge, fill=FAR,
                                   base=P, pattern=[[-1, 2 * P]], channel_multiplier=1))
            pool.affine_select(out=dist[:, :], in_=dist[:, :], compare_op=ALU.is_ge, fill=FAR,
                               base=-1, pattern=[[1, 2 * P]], channel_multiplier=-1).then_inc(S["dist_ready"], 1)
            for h in range(QH):
                ins = pool.memset(slope[:, h:h + 1], -2.0 ** (-8.0 * (h + 1) / QH))
            ins.then_inc(S["slopes_ready"], 1)

            def split(b, s, visit, used):
                pool.wait_ge(w_loaded[b], visit)
                if used is not None:
                    pool.wait_ge(S["acc_done"], used)
                pool.nop().then_inc(S["pool_passed"], 1)
                pool.tensor_copy(WH[:, b, :], RAW[:, b, :]).then_inc(S["w_hi_done"], 1)
                pool.wait_ge(S["w_hi_done"], s)
                pool.tensor_tensor(WL[:, b, :], RAW[:, b, :], WH[:, b, :].bitcast(F32), ALU.subtract).then_inc(S["w_ready"], 1)

            def one(s, used):
                split(s % 2, s + 1, 16 * (s // 2 + 1), used)

            def run(s0, u0, n):
                with pool.Fori(0, n // 2) as i:
                    for b in range(2):
                        split(b, i * 2 + (s0 + b + 1), i * 16 + 16 * (s0 // 2 + 1), i * 2 + (u0 + b - 1))

            for s in range(2):
                one(s, None)
            for s in range(2, 4):
                one(s, s - 1)
            run(4, 4, 16)
            one(20, 19)
            one(21, 20)
            pool.wait_ge(S["s5_y_done"], 8)
            own(pool.memset(MASK[:, :, :], 1.0))
            for l, w in enumerate(LEVELS):
                m = MASK[:, l, :]
                n = P // (2 * w)
                own(pool.affine_select(out=m, in_=m, compare_op=ALU.is_ge, fill=0.0, base=0,
                                       pattern=[[-2 * w, n], [0, 2 * w]], channel_multiplier=1))
                own(pool.affine_select(out=m, in_=m, compare_op=ALU.is_ge, fill=0.0, base=w - 1,
                                       pattern=[[2 * w, n], [0, 2 * w]], channel_multiplier=-1))
                own(pool.affine_select(out=m, in_=m, compare_op=ALU.is_ge, fill=0.0, base=-w,
                                       pattern=[[0, n], [1, 2 * w]], channel_multiplier=0))
            pool.affine_select(out=MASK[:, 7, :], in_=MASK[:, 7, :], compare_op=ALU.is_equal, fill=0.0,
                               base=0, pattern=[[-1, P]], channel_multiplier=1).then_inc(S["masks_ready"], 1)
            def keys_and_queries(hd, half, first=False):
                un = hd * 2 + half
                pool.wait_ge(hg_qv_loaded[half], hd * 32 + 32)
                for j in range(2):
                    ins = pool.tensor_tensor(QV[:, half, j, :], QV[:, half, j, :], RSTD[:, half * HALF:(half + 1) * HALF], ALU.mult)
                ins.then_inc(S["hg_qv_scaled"], 1)
                pool.wait_ge(S["hg_exp_b"], un + 1)
                pool.wait_ge(S["hg_qv_scaled"], un + 1)
                if not first:
                    pool.wait_ge(S["hg_o_done"], un * 4 + (CREDIT - 4))
                pool.tensor_tensor(QB[:, half, :], QV[:, half, 0, :], TC[:, :], ALU.mult)
                pool.wait_ge(S["hg_exp_end"], un + 1)
                pool.tensor_tensor(KD[:, half, :], KK[:, half, :], TD[:, :], ALU.mult).then_inc(S["hg_decayed"], 1)

            def levels(hd, half):
                for l, w in enumerate(LEVELS):
                    v, k, q = (ap.rearrange("p (n two w) -> p n two w", two=2, w=w)
                               for ap in (LVL[:, half, l, :], KK[:, half, :], QV[:, half, 0, :]))
                    pool.wait_ge(S["hg_level_exp"], hd * 14 + (7 * half + l + 1))
                    pool.tensor_tensor(v[:, :, 0, :], v[:, :, 0, :], k[:, :, 0, :], ALU.mult)
                    ins = pool.tensor_tensor(v[:, :, 1, :], v[:, :, 1, :], q[:, :, 1, :], ALU.mult)
                ins.then_inc(S["hg_levels"], 1)

            def heads_chunks(hd, last):
                keys_and_queries(hd, 1)
                levels(hd, 1)
                pool.wait_ge(S["hg_g_loaded"], hd * 16 + 16)
                pool.tensor_tensor(G[:, :], G[:, :], RSTD[:, :], ALU.mult).then_inc(S["hg_g_scaled"], 1)
                if not last:
                    keys_and_queries(hd + 1, 0)
                pool.wait_ge(S["hg_sigmoid_g"], hd + 1)
                pool.tensor_tensor(PC[:, :], PC[:, :], G[:, :], ALU.mult).then_inc(S["hg_gate_made"], 1)
                if not last:
                    levels(hd + 1, 0)

            keys_and_queries(0, 0, first=True)
            levels(0, 0)
            one(22, 22)
            one(23, 24)
            with pool.Fori(0, HEADS - 1) as hd:
                heads_chunks(hd, False)
            heads_chunks(HEADS - 1, True)
            with pool.Fori(0, 3) as i:
                for b in range(2):
                    split(b, i * 2 + (24 + b + 1), i * 16 + 16 * 13, i * 2 + (26 + b - 1))
            run(SLAB["mlp0"], UNIT["mlp0"], 64)
            run(SLAB["gate0"], UNIT["gate0"], 8)

            def ups(name, nxt, n_next):
                s, u = SLAB[name], UNIT[name]
                one(s, u - 1)
                one(s + 1, u)
                if nxt:
                    s, u = SLAB[nxt], UNIT[nxt]
                    one(s, u - 4)
                    one(s + 1, u)
                    with pool.Fori(1, n_next // 2) as i:
                        for b in range(2):
                            split(b, i * 2 + (s + b + 1), i * 16 + 16 * (s // 2 + 1), i * 2 + (u + b - 1))

            ups("up0", "qkv", 12)
            for s in range(SLAB["wo"], SLAB["wo"] + 2):
                one(s, s - SLAB["wo"] + UNIT["wo"] - 1)
            with pool.Fori(0, KVH // 2) as gp:
                for i in range(BODY):
                    lo = P if i % NB == 0 else 0
                    pr = SC[:, i % RING, :, lo:]
                    den = sm[:, 2, i % RING, :].unsqueeze(2).to_broadcast([P, 4, 2 * P - lo])
                    pool.wait_ge(S["at_den"], gp * BODY + (i + 1))
                    pool.tensor_tensor(pr, pr, den, ALU.mult).then_inc(S["at_norm"], 1)
            with pool.Fori(1, 4) as i:
                for b in range(2):
                    split(b, i * 2 + (SLAB["wo"] + b + 1), i * 16 + 16 * (SLAB["wo"] // 2 + 1), i * 2 + (UNIT["wo"] + b - 1))
            run(SLAB["mlp1"], UNIT["mlp1"], 64)
            run(SLAB["gate1"], UNIT["gate1"], 8)
            ups("up1", None, 0)

        @block.tensor
        def _(pe):
            for name in "hg_o_done at_vt_done at_qk_done at_pt_done".split():
                pe.nop().then_inc(S[name], CREDIT)
            def unit(acc, wh, wl, xh, xl, kts=KT, k0=0, ready=None):
                for k in range(kts):
                    if ready is not None:
                        pe.wait_ge(*ready(k))
                    for w, x in ((wh, xh), (wh, xl), (wl, xh)):
                        for h in range(2):
                            ins = pe.matmul(acc[:, h, :], w[:, k, :], x[:, k0 + k, h * HALF:(h + 1) * HALF],
                                            start=(k == 0 and w is wh and x is xh), stop=(k == kts - 1 and w is wl))
                ins.then_inc(S["acc_done"], 1)

            whs = [WH[:, b, :].rearrange("p (k n) -> p k n", n=P) for b in range(2)]
            wls = [WL[:, b, :].rearrange("p (k n) -> p k n", n=P) for b in range(2)]

            def one(s, u, x, **kw):
                pe.wait_ge(S["w_ready"], s + 1)
                if u >= 2:
                    pe.wait_ge(*free_of(u - 2))
                unit(ACC[u % 2], whs[s % 2], wls[s % 2], *x, **kw)

            def run(s0, u0, n, x):
                with pe.Fori(0, n // 2) as i:
                    for b in range(2):
                        pe.wait_ge(S["w_ready"], i * 2 + (s0 + b + 1))
                        pe.wait_ge(free_of(u0)[0], i * 2 + (free_of(u0)[1] + b - 2))
                        unit(ACC[b], whs[b], wls[b], *x)

            XA, XB = (XAh, XAl), (XBh, XBl)

            def x_ready(norm):
                return lambda k: (S["x_ready"], 8 * norm + k + 1)

            def sum_squares(n):
                pe.wait_ge(S["sumsq_ready"], n + 1)
                for h in range(2):
                    ins = pe.matmul(PS[:, 4 + h, :], ones[:, :], SUMSQ[:, h * HALF:(h + 1) * HALF], start=True, stop=True)
                ins.then_inc(S["ss_done"], 1)

            def first_two(s, u, norm):
                one(s, u, XA, ready=x_ready(norm))
                sum_squares(norm)
                one(s + 1, u + 1, XA)

            pe.wait_ge(S["consts_ready"], 1)
            pe.wait_ge(S["pool_step"], 2)
            pe.wait_ge(S["gains_loaded"], 16)
            pe.transpose(PS[:, 0, 0:16], ROWS[0:16, :], ident[0:16, 0:16]).then_inc(S["cols_done"], 1)

            def x_tile(k):
                pe.wait_ge(x_loaded[k], 16)
                if k >= 2:
                    pe.wait_ge(S["x_tr_dve"], k - 1)
                    pe.wait_ge(S["x_tr_act"], k - 1)
                for n in range(NB):
                    ins = pe.transpose(PS[:, 4 + 2 * (k % 2) + n // 4, (n % 4) * P:(n % 4 + 1) * P], XS[:, k, n, :], ident[:, :])
                ins.then_inc(S["x_tr_done"], 1)

            x_tile(0)
            x_tile(1)
            pe.wait_ge(S["cols_ready"], 1)
            for k in range(KT):
                if k + 2 < KT:
                    x_tile(k + 2)
                pe.wait_ge(*x_ready(0)(k))
                for u in range(2):
                    if k == 0:
                        pe.wait_ge(S["w_ready"], u + 1)
                    for w, x in ((whs[u], XAh), (whs[u], XAl), (wls[u], XAh)):
                        for h in range(2):
                            ins = pe.matmul(ACC[u][:, h, :], w[:, k, :], x[:, k, h * HALF:(h + 1) * HALF],
                                            start=(k == 0 and w is whs[u] and x is XAh), stop=(k == KT - 1 and w is wls[u]))
                    if k == KT - 1:
                        ins.then_inc(S["acc_done"], 1)
            sum_squares(0)
            pe.wait_ge(S["rows_loaded"], 16 * 9)
            pe.transpose(PS[:, 6, 0:N_ROWS], ROWS[:, :], ident[0:N_ROWS, 0:N_ROWS]).then_inc(S["cols_done"], 1)
            for s in range(2, 4):
                one(s, s, XA)
            one(4, 4, XA)
            one(5, 5, XA)
            pe.wait_ge(S["ss_read"], 1)
            pe.wait_ge(S["s5_raw_loaded"], 16 * 13)
            for h in range(2):
                for r in range(2):
                    j = 2 * h + r
                    ins = pe.transpose(PS[:, 4, j * P:(j + 1) * P], CROW[:, h, r, :], ident[:, :])
            ins.then_inc(S["s5_c_tr"], 1)
            for s in range(6, 11):
                one(s, s, XA)
            pe.wait_ge(S["s5_ba_ready"], 1)
            for n in range(8):
                if n == 0:
                    pe.wait_ge(S["s5_ca_ready"], 1)
                if n >= 4:
                    pe.wait_ge(S["s5_ew_copied"], n - 3)
                for j in range(4):
                    q, r = 2 * n + j // 2, j % 2
                    ins = pe.transpose(PS[:, 4 + n % 4, j * P:(j + 1) * P],
                                       BA[:, r, q, :, :].rearrange("p j h -> p (j h)"), ident[:, :])
                ins.then_inc(S["s5_ew_tr"], 1)
            def group(n, j):
                return 8 * (n // 2) + n % 2 + 2 * j

            for n in range(8):
                if n < 4:
                    pe.wait_ge(S["s5_ew_copied"], n + 5)
                else:
                    pe.wait_ge(S["s5_g_copied"], n - 3)
                for j in range(4):
                    g = group(n, j)
                    q, rows = g // 2, slice(STATES * (g % 2), STATES * (g % 2 + 1))
                    o = PS[0:GRP, 4 + n % 4, j * P:(j + 1) * P]
                    for r in range(2):
                        pe.matmul(o[:, 0:GRP], BB[rows, r, q, :], C0[rows, r, q, :], start=(r == 0), stop=(r == 1))
                    for r in range(2):
                        ins = pe.matmul(o[:, GRP:P], BB[rows, r, q, :],
                                        CA[rows, r, q, 0:L - 1, :].rearrange("p j h -> p (j h)"), start=(r == 0), stop=(r == 1))
                ins.then_inc(S["s5_g_done"], 1)
            one(11, 11, XA)
            one(12, 12, XA)
            pe.wait_ge(S["s5_u_loaded"], 16 * 8)
            pe.wait_ge(S["s5_g_copied"], 8)
            for half in range(2):
                if half:
                    one(13, 13, XA)
                    one(14, 14, XA)
                    pe.wait_ge(S["s5_end_read"], 1)
                for qq in range(8):
                    q = 8 * half + qq
                    for two in range(2):
                        for r in range(2):
                            o = PS[STATES * two:STATES * (two + 1), 4 + 2 * r + qq // 4, (qq % 4) * P:(qq % 4 + 1) * P]
                            ins = pe.matmul(o, EW[:, q, r, STATES * two:STATES * (two + 1)], U[:, 2 * q + two, :], start=True, stop=True)
                ins.then_inc(S["s5_end_done"], 1)
            for s in range(15, 18):
                one(s, s, XA)
            pe.wait_ge(S["s5_t_loaded"], 16 * 8)
            pe.wait_ge(S["s5_states_ready"], 1)
            pe.wait_ge(S["s5_end_read"], 2)
            for n in range(8):
                if n >= 4:
                    pe.wait_ge(S["s5_y_copied"], n - 3)
                for j in range(4):
                    g = group(n, j)
                    q, rows = g // 2, slice(STATES * (g % 2), STATES * (g % 2 + 1))
                    o = PS[:, 4 + n % 4, j * P:(j + 1) * P]
                    pe.matmul(o, TOEP[:, g, :], U[:, g, :], start=True, stop=False)
                    for r in range(2):
                        ins = pe.matmul(o[:, 1:CH], CA[rows, r, q, :, :].rearrange("p j h -> p (j h)"),
                                        CR[rows, r, q, 0:CH - 1], start=False, stop=(r == 1))
                ins.then_inc(S["s5_y_done"], 1)
            for s in range(18, 20):
                one(s, s, XA)
            for s in range(2):
                pe.wait_ge(S["w_ready"], 21 + s)
                wh = WH[:, s, :].rearrange("p (k n) -> p k n", n=256)
                wl = WL[:, s, :].rearrange("p (k n) -> p k n", n=256)
                for j in range(2):
                    u = 20 + 2 * s + j
                    pe.wait_ge(*free_of(u - 2))
                    unit(ACC[j], wh[:, :, j * P:(j + 1) * P], wl[:, :, j * P:(j + 1) * P], XBh, XBl, kts=4, k0=4,
                         ready=(lambda k: (S["mid_ready"], k + 1)) if u == 20 else None)
            for u in (22, 23):
                pe.wait_ge(*free_of(u))
            pe.wait_ge(S["s5_y_copied"], 8)
            pe.wait_ge(S["masks_ready"], 1)

            def head(hd):
                for c in range(NB + 1):
                    half, t, b = c // 4, slice(c % 4 * P, (c % 4 + 1) * P), c % 2
                    if c < NB:
                        if c % 4 == 0:
                            pe.wait_ge(S["hg_decayed"], hd * 2 + (half + 1))
                        pe.wait_ge(S["hg_tr_copied"], hd * NB + (c + CREDIT))
                        pe.transpose(PS[:, 3, 0:P], QV[:, half, 1, t], ident[:, :])
                        pe.transpose(PS[:, 3, P:2 * P], KD[:, half, t], ident[:, :]).then_inc(S["hg_tr"], 1)
                        if c % 4 == 0:
                            pe.wait_ge(S["hg_levels"], hd * 2 + (half + 1))
                        pe.wait_ge(S["hg_lvl_read"], hd * NB + (max(c - 1, 0) + CREDIT))
                        for l in range(8):
                            o = PS[:, 4 + 2 * b + l // 4, (l % 4) * P:(l % 4 + 1) * P]
                            if l < 7:
                                ins = pe.matmul(o, LVL[:, half, l, t], LVL[:, half, l, t], start=True, stop=True)
                            else:
                                ins = pe.matmul(o, KK[:, half, t], QV[:, half, 0, t], start=True, stop=True)
                        ins.then_inc(S["hg_lvl_done"], 1)
                    if c == 0:
                        continue
                    c, b = c - 1, 1 - b
                    half, t = c // 4, slice(c % 4 * P, (c % 4 + 1) * P)
                    pe.wait_ge(S["hg_tr_copied"], hd * NB + (c + 1 + CREDIT))
                    pe.wait_ge(S["hg_state"], hd * (NB - 1) + (c + CREDIT))
                    if c < NB - 1:
                        ins = pe.matmul(PS[:, 2, 0:P], VK[:, b, 1, :], VK[:, b, 0, :], start=True, stop=True)
                        if c == 0:
                            ins.then_inc(S["hg_ds_done"], 1)
                    pe.wait_ge(S["hg_o_copied"], hd * NB + (max(c - 1, 0) + CREDIT))
                    if c in (1, 5):
                        pe.wait_ge(S["hg_ss_read"], hd * 2 + (c // 4 + CREDIT))
                    if c:
                        ins = pe.matmul(PS[:, b, 0:P], SS[:, :], QB[:, half, t], start=True, stop=False)
                        if c < NB - 1:
                            ins.then_inc(S["hg_ds_done"], 1)
                    pe.wait_ge(S["hg_att"], hd * NB + (c + 1))
                    pe.matmul(PS[:, b, 0:P], VK[:, b, 0, :], AT[:, b, :], start=(c == 0), stop=True).then_inc(S["hg_o_done"], 1)
                    if c in (4, 7):
                        pe.wait_ge(S["hg_squares_made"], hd * 2 + (c // 4 if c == 4 else 2))
                        pe.matmul(PS[:, 1, :], ones[:, :], PA[:, :], start=True, stop=True).then_inc(S["hg_ss"], 1)

            with pe.Fori(0, HEADS) as hd:
                head(hd)
            pe.wait_ge(S["hg_y_low"], 2 * HEADS)
            pe.wait_ge(S["mid_ready"], 8)
            one(22, 24, XB)
            one(23, 25, XB)
            run(24, 26, 6, XB)

            def mlp(name, norm, mid0):
                s, u = SLAB[name], UNIT[name]
                first_two(s, u, norm)
                run(s + 2, u + 2, 6, XA)

                def down_two(c):
                    for b in range(2):
                        pe.wait_ge(S["w_ready"], c * 16 + (s + 8 + b + 1))
                        pe.wait_ge(S["acc_free"], c * 16 + (free_of(u + 8)[1] + b - 2))
                        ready = (lambda k: (S["mid_ready"], c * 8 + (mid0 + k + 1))) if b == 0 else None
                        unit(ACC[b], whs[b], wls[b], *XB, ready=ready)

                def two(off, x):
                    for b in range(2):
                        pe.wait_ge(S["w_ready"], off + (s + b + 1))
                        pe.wait_ge(S["acc_free"], off + (free_of(u)[1] + b - 2))
                        unit(ACC[b], whs[b], wls[b], *x)

                with pe.Fori(0, 3) as c:
                    down_two(c)
                    with pe.Fori(0, 3) as m:
                        two(c * 16 + m * 2 + 10, XB)
                    with pe.Fori(0, 4) as m:
                        two(c * 16 + m * 2 + 16, XA)
                for b in range(2):
                    ready = (lambda k: (S["mid_ready"], mid0 + 24 + k + 1)) if b == 0 else None
                    one(s + 56 + b, u + 56 + b, XB, ready=ready)
                run(s + 58, u + 58, 6, XB)

            def last_embed(s):
                pe.wait_ge(S["w_ready"], s + 2)
                pe.wait_ge(S["p_ready"], 4)
                pe.wait_ge(S["p_hi"], 4)
                for v in (202, 203):
                    pe.wait_ge(*free_of(v))

                def transposes(e):
                    half, m = e // KT, e % KT
                    pe.wait_ge(S["last_gain"], e + 1)
                    if e >= 3:
                        pe.wait_ge(S["last_copied"], e - 2)
                    for j in range(4):
                        n = 4 * half + j
                        ins = pe.transpose(PS[:, 4 + e % 3, j * P:(j + 1) * P], HG[:, m, n * P:(n + 1) * P], ident[:, :])
                    ins.then_inc(S["last_tr"], 1)

                def sum_of_tokens(half):
                    pe.wait_ge(S["last_sq_used"], KT * (half + 1))
                    for j in range(4):
                        n = 4 * half + j
                        ins = pe.matmul(PS[:, 7, n * 4:(n + 1) * 4], SUMSQ[:, n * P:(n + 1) * P], ones[:, 0:4], start=True, stop=True)
                    ins.then_inc(S["last_ss"], 1)

                for e in range(2 * KT):
                    half, m = e // KT, e % KT
                    if e >= 4:
                        pe.wait_ge(S["last_free"], e - 3)
                    ws = [w[:, m // 4, :].rearrange("p (k n) -> p k n", n=HALF)[:, :, m % 4 * P:(m % 4 + 1) * P] for w in (WH, WL)]
                    t = slice(half * HALF, (half + 1) * HALF)
                    for k in range(2):
                        for w, x in ((ws[0], PTh), (ws[0], PTl), (ws[1], PTh)):
                            ins = pe.matmul(PS[:, e % 4, :], w[:, k, :], x[:, k, t],
                                            start=(k == 0 and w is ws[0] and x is PTh), stop=(k == 1 and w is ws[1]))
                    ins.then_inc(S["last_done"], 1)
                    if e >= 2:
                        transposes(e - 2)
                    if e == KT + 2:
                        sum_of_tokens(0)
                for e in (14, 15):
                    transposes(e)
                sum_of_tokens(1)

            def embed(i, norm):
                s, u = SLAB[f"gate{i}"], UNIT[f"gate{i}"]
                first_two(s, u, norm)
                pe.wait_ge(S["p_loaded"], 16 * (i + 1))
                pe.wait_ge(S["ss_read"], norm + 1)
                for k in range(2):
                    for t in range(NB):
                        ins = pe.transpose(PS[:, 4 + 2 * k + t // 4, (t % 4) * P:(t % 4 + 1) * P],
                                           PIN[:, t, k * P:(k + 1) * P], ident[:, :])
                    ins.then_inc(S["p_tr"], 1)
                run(s + 2, u + 2, 6, XA)
                s, u = SLAB[f"up{i}"], UNIT[f"up{i}"]
                if i == 1:
                    return last_embed(s)
                for n in range(2):
                    pe.wait_ge(S["w_ready"], s + n + 1)
                    wh = WH[:, n, :].rearrange("p (k n) -> p k n", n=HALF)
                    wl = WL[:, n, :].rearrange("p (k n) -> p k n", n=HALF)
                    if n == 0:
                        pe.wait_ge(S["p_ready"], 2 * (i + 1))
                    for j in range(4):
                        v = u + 4 * n + j
                        pe.wait_ge(*free_of(v - 2))
                        unit(ACC[v % 2], wh[:, :, j * P:(j + 1) * P], wl[:, :, j * P:(j + 1) * P], PTh, PTl, kts=2)

            mlp("mlp0", 1, 8)
            embed(0, 2)
            first_two(SLAB["qkv"], UNIT["qkv"], 3)
            run(SLAB["qkv"] + 2, UNIT["qkv"] + 2, 10, XA)
            for u in (122, 123):
                pe.wait_ge(*free_of(u))
            pe.wait_ge(S["ss_read"], 4)
            with pe.Fori(0, KVH // 2) as gp:

                def after(name, i):
                    pe.wait_ge(S[name], gp * BODY + (max(i + 1, 0) + CREDIT))

                def v_tokens(i):
                    par = i // NB
                    pe.wait_ge(at_loaded[par], gp * 64 + 64)
                    after("at_o_done_lo", i - AHEAD - 2)
                    pe.nop().then_inc(S["pe_passed"], 1)
                    for n in range(NB):
                        ins = pe.transpose(PS[:, 3, n * HD:(n + 1) * HD], AV[:, par, n * P:(n + 1) * P], ident[0:HD, 0:HD])
                    ins.then_inc(S["at_vt_done"], 1)

                def scores(i):
                    par, n, b = i // NB, i % NB, i % 2
                    lo = P if n == 0 else 0
                    if n == 0:
                        pe.wait_ge(at_loaded[par], gp * 64 + 64)
                    after("at_scored", i - 2)
                    for j in range(4):
                        rows = slice(HD * (j % 2), HD * (j % 2 + 1))
                        o = PS[:, 4 + 2 * b + j % 2, (j // 2) * 256 + lo:(j // 2 + 1) * 256]
                        ins = pe.matmul(o, AQ[rows, par, j // 2, n * P:(n + 1) * P],
                                        AK[rows, par, (n - 1) * P + lo:(n + 1) * P], start=True, stop=True)
                    ins.then_inc(S["at_qk_done"], 1)

                def transposes(i):
                    pe.wait_ge(S["at_norm"], gp * BODY + (i + 1))
                    after("at_pt_copied", i - 1)
                    for h in ((1,) if i % NB == 0 else (0, 1)):
                        for j in range(4):
                            ins = pe.transpose(PS[:, h, j * P:(j + 1) * P], SC[:, i % RING, j, h * P:(h + 1) * P], ident[:, :])
                    ins.then_inc(S["at_pt_done"], 1)

                def outputs(i):
                    par, n, b = i // NB, i % NB, i % 2
                    after("at_pt_copied", i)
                    after("at_o_done_lo", i - 2)
                    for r in range(2):
                        for h in ((1,) if n == 0 else (0, 1)):
                            ins = pe.matmul(PS[HD * r:HD * (r + 1), 2 + b, 0:256], AVT[:, par, n - 1 + h, :],
                                            PT[:, h, 2 * r:2 * r + 2, :], start=(h == 0 or n == 0), stop=(h == 1))
                    ins.then_inc(S["at_o_done"], 1)

                v_tokens(0)
                scores(0)
                for i in range(BODY + AHEAD):
                    if i == NB:
                        v_tokens(i)
                    if i >= AHEAD:
                        transposes(i - AHEAD)
                    if i + 1 < BODY:
                        scores(i + 1)
                    if i in (0, NB):
                        pe.wait_ge(S["at_vt_copied"], gp * 2 + (1 if i == 0 else 2))
                    if i >= AHEAD:
                        outputs(i - AHEAD)
            pe.wait_ge(S["at_o_done_lo"], KVH * NB + CREDIT)
            one(SLAB["wo"], UNIT["wo"], XB)
            one(SLAB["wo"] + 1, UNIT["wo"] + 1, XB)
            run(SLAB["wo"] + 2, UNIT["wo"] + 2, 6, XB)
            mlp("mlp1", 4, 40)
            embed(1, 5)

        @block.scalar
        def _(act):
            for name in "hg_tr_copied hg_o_copied at_pt_copied".split():
                act.nop().then_inc(S[name], CREDIT)
            own = Own(act, S["act_step"])

            def fn(o, i, f, **kw):
                return act.activation(o, i, f, **kw)

            def wait(s, n):
                act.wait_ge(S[s], n)
                settle()

            def settle():
                act.nop().then_inc(S["act_passed"], 1)

            def finish(norm, gain, g0):
                with act.Fori(0, KT) as m:
                    hm = H[:, bass.ds(m, 1), :].rearrange("p a t -> p (a t)")
                    wait("h_ready", m + (8 * norm + 1))
                    fn(XAh[:, bass.ds(m, 1), :].rearrange("p a t -> p (a t)"), hm, ACT.Identity,
                       scale=COLS[:, bass.ds(m + (ROW[gain] + g0), 1)]).then_inc(S["x_hi_done"], 1)
                    wait("sq_used", m + 8 * norm + CREDIT)
                    fn(SQ[:, :], hm, ACT.Square).then_inc(S["sq_done"], 1)

            def root(n):
                act.wait_ge(S["rcp_done"], n + 1)
                fn(RSTD[:, :], ST[1][:, :], ACT.Sqrt).then_inc(S["rstd_done"], 1)

            def x_copy(k):
                act.wait_ge(S["x_tr_done"], k + 1)
                fn(H[:, k, HALF:], PS[:, 5 + 2 * (k % 2), :], ACT.Copy).then_inc(S["x_tr_act"], 1)

            x_copy(0)
            for k in range(KT):
                if k + 1 < KT:
                    x_copy(k + 1)
                act.wait_ge(S["cols_ready"], 1)
                act.wait_ge(S["x_tr_act"], k + 1)
                act.wait_ge(S["x_tr_dve"], k + 1)
                fn(XAh[:, k, :], H[:, k, :], ACT.Identity, scale=col("mix", k)).then_inc(S["x_hi_done"], 1)
                act.wait_ge(S["sq_used"], k + CREDIT)
                fn(SQ[:, :], H[:, k, :], ACT.Square).then_inc(S["sq_done"], 1)
            act.dma_start(h_dram.rearrange("(k p) t -> p k t", p=P), H[:, :, :]).then_inc(S["h_spilled"], 16)
            root(0)
            for u in range(4):
                act.wait_ge(S["acc_free"], u + 1)
                act.dma_start(u_dram[u * P:(u + 1) * P, :], ST[u % 2][:, :]).then_inc(spilled[u % 2], 16)
            act.wait_ge(S["lb_in"], 1)
            fn(floor_[:, :], floor_[:, :], ACT.Exp).then_inc(S["lb_exp"], 1)
            p = lambda i: PR[:, i, :]
            act.wait_ge(S["cols_ready"], 2)
            act.wait_ge(S["s5_dve"], 1)
            act.wait_ge(S["s5_raw_loaded"], 16 * 13)
            for two in range(2):
                half = slice(two * STATES, (two + 1) * STATES)
                own(fn(PR[half, 1, :], log_dt[half, two::2], ACT.Exp))
            act.nop().then_inc(S["s5_act"], 1)
            act.wait_ge(S["s5_dve"], 2)
            fn(p(3), p(2), ACT.Exp)
            fn(p(4), p(2), ACT.Exp, scale=float(L)).then_inc(S["s5_act"], 1)
            act.wait_ge(S["s5_dve"], 3)
            fn(p(6), p(5), ACT.Sin)
            fn(p(7), p(5), ACT.Sin, scale=0.5).then_inc(S["s5_act"], 1)

            def head_unit(u):
                b = u % 2
                act.wait_ge(S["acc_done"], u + 1)
                act.wait_ge(spilled[b], 16 * (u // 2))
                fn(ST[b][:, :], flat(ACC[b]), ACT.Copy).then_inc(S["acc_free_act"], 1)
                act.wait_ge(S["acc_free_act"], u - 3)
                act.dma_start(fqig_dram[(u - 4) * P:(u - 3) * P, :], ST[b][:, :]).then_inc(spilled[b], 16)

            for u in range(4, 9):
                head_unit(u)
            act.wait_ge(S["h_spilled"], 16)
            for b in range(2):
                act.wait_ge(spilled[b], 16 * 2)
            for j in range(L):
                act.dma_start(U[j * GRP:(j + 1) * GRP, :, :],
                              u_dram[:, j * CH:(j + 1) * CH].rearrange("(g h) c -> h g c", h=GRP)).then_inc(S["s5_u_loaded"], 16)
            for u in range(9, 11):
                head_unit(u)
            for n in range(8):
                act.wait_ge(S["s5_ew_tr"], n + 1)
                fn(EW[:, 2 * n:2 * n + 2, :, :].rearrange("p q r m -> p (q r m)"), PS[:, 4 + n % 4, :], ACT.Copy)\
                    .then_inc(S["s5_ew_copied"], 1)

            def four(n):
                g0 = 8 * (n // 2) + n % 2
                return slice(g0, g0 + 7, 2)

            for n in range(8):
                act.wait_ge(S["s5_g_done"], n + 1)
                if n == 0:
                    act.wait_ge(S["s5_ew_tr"], 8)
                fn(GK[:, four(n), :], PS[0:GRP, 4 + n % 4, :].rearrange("p (g m) -> p g m", m=P), ACT.Copy)\
                    .then_inc(S["s5_g_copied"], 1)
            act.wait_ge(S["s5_g_copied"], 8)
            act.wait_ge(S["s5_t_zeroed"], 1)
            for j in range(L):
                act.dma_start(TOEP[j * GRP:(j + 1) * GRP, :, j * GRP:P], GK[:, :, 0:P - j * GRP]).then_inc(S["s5_t_loaded"], 16)
            for u in range(11, 18):
                head_unit(u)
            act.wait_ge(S["s5_states_ready"], 1)
            act.dma_start(UT[:, :, :], u_dram.rearrange("(k p) t -> p k t", p=P)).then_inc(S["s5_ut_loaded"], 16)
            def tiles_back(h):
                act.wait_ge(S["s5_y_stored"], 16 * L * (h + 1))
                for k in (2 * h, 2 * h + 1):
                    act.dma_start(YT[:, k, :], y_dram[k * P:(k + 1) * P, :]).then_inc(yt_loaded[k], 16)

            for half in range(2):
                for n in range(4 * half, 4 * half + 4):
                    act.wait_ge(S["s5_y_done"], n + 1)
                    fn(YS[:, four(n), :], PS[:, 4 + n % 4, :].rearrange("p (g m) -> p g m", m=P), ACT.Copy)\
                        .then_inc(S["s5_y_copied"], 1)
                act.wait_ge(S["s5_y_copied"], 4 * half + 4)
                if half == 1:
                    tiles_back(0)
                for j in range(L):
                    act.dma_start(y_dram[half * 256:(half + 1) * 256, j * CH:(j + 1) * CH].rearrange("(g h) c -> h g c", h=GRP),
                                  YS[j * GRP:(j + 1) * GRP, 16 * half:16 * half + 16, :]).then_inc(S["s5_y_stored"], 16)
            tiles_back(1)
            for k in range(4):
                act.wait_ge(S["glu_tanh_in"], k + 1)
                fn(ST[3][:, :], ST[2][:, :], ACT.Tanh).then_inc(S["glu_tanh"], 1)
                act.wait_ge(S["glu_zz"], k + 1)
                fn(XBh[:, 4 + k, :].rearrange("p (c j) -> p j c", j=L), YT[:, k, :].rearrange("p (j c) -> p j c", j=L),
                   ACT.Copy, scale=0.5).then_inc(S["mid_hi_done"], 1)
                if k < 2:
                    head_unit(18 + k)
            def told(ins, name):
                ins.then_inc(S[name], 1)

            def sigmoid(o, tmp, i, name):
                own(fn(tmp, i, ACT.Exp, scale=-1.0))
                own(fn(o, tmp, ACT.Ln, bias=1.0))
                told(fn(o, o, ACT.Exp, scale=-1.0), name)

            def decay(hd, half, first=False):
                un = hd * 2 + half
                act.wait_ge(S["hg_f"], un + 1)
                if not first:
                    act.wait_ge(S["hg_decayed"], un)
                sigmoid(TC[:, :], TB[:, :], TA[:, :], "hg_sigmoid_f")
                act.wait_ge(S["hg_sigmoid_f"], un + 1)
                settle()
                told(fn(TD[:, :], TC[:, :], ACT.Ln, scale=keep[:, bass.ds(hd, 1)], bias=floor_[:, bass.ds(hd, 1)]), "hg_log_f")

            def cumulated(hd, half):
                act.wait_ge(S["hg_cumulated"], hd * 2 + (half + 1))
                act.wait_ge(S["hg_k_made"], hd * 2 + (half + 1))
                fn(TC[:, :], BC[:, :], ACT.Exp)
                told(fn(ENDS[:, half, :], BC[:, P - 1::P], ACT.Exp), "hg_exp_b")
                act.wait_ge(S["hg_to_end"], hd * 2 + (half + 1))
                told(fn(TD[:, :], TD[:, :], ACT.Exp, scale=-1.0), "hg_exp_end")

            def level_exps(hd, half, some):
                for l in some:
                    act.wait_ge(S["hg_level"], hd * 14 + (7 * half + l + 1))
                    told(fn(LVL[:, half, l, :], LVL[:, half, l, :], ACT.Exp, scale=-1.0), "hg_level_exp")

            def rstd_head(hd, half):
                act.wait_ge(S["hg_ss_read"], hd * 2 + (half + 1 + CREDIT))
                own(fn(PD[:, :], PD[:, :], ACT.Ln))
                told(fn(PD[:, :], PD[:, :], ACT.Exp, scale=-0.5), "hg_rstd")

            def squares(hd, half):
                act.wait_ge(S["hg_o_copied"], hd * NB + (4 * half + 4 + CREDIT))
                told(fn(PA[:, :], OUTH[:, half, :], ACT.Square), "hg_squares_made")

            def y_high(hd, half):
                act.wait_ge(S["hg_y_ready"], hd * 2 + (half + 1))
                settle()
                told(fn(XBh[:, bass.ds(hd + 4, 1), half * HALF:(half + 1) * HALF].rearrange("p a t -> p (a t)"), PD[:, :], ACT.Copy),
                     "hg_y_high")

            def head(hd, last):
                for c in range(NB + 1):
                    half, b = c // 4, c % 2
                    if c < NB:
                        act.wait_ge(S["hg_tr"], hd * NB + (c + 1))
                        fn(VK[:, b, :, :].rearrange("p a t -> p (a t)"), PS[:, 3, 0:2 * P], ACT.Copy).then_inc(S["hg_tr_copied"], 1)
                    unit = (hd + half, 1 - half)
                    if c < NB and not (last and half == 1):
                        if c % 4 == 1:
                            cumulated(*unit)
                        if c % 4 == 2:
                            level_exps(*unit, range(4))
                        if c % 4 == 3:
                            level_exps(*unit, range(4, 7))
                            if not last:
                                decay(hd + 1, half)
                    if c:
                        act.wait_ge(S["hg_o_done"], hd * NB + (c + CREDIT))
                        o = (c - 1) % 4 * P
                        fn(OUTH[:, (c - 1) // 4, o:o + P], PS[:, 1 - b, 0:P], ACT.Copy).then_inc(S["hg_o_copied"], 1)
                    if c == 4:
                        squares(hd, 0)
                        act.wait_ge(S["hg_g_scaled"], hd + 1)
                        sigmoid(PC[:, :], PC[:, :], G[:, :], "hg_sigmoid_g")
                    if c == 6:
                        rstd_head(hd, 0)
                squares(hd, 1)
                y_high(hd, 0)
                rstd_head(hd, 1)
                y_high(hd, 1)

            for m in range(4):
                if m == 0:
                    decay(0, 0, first=True)
                if m == 1:
                    cumulated(0, 0)
                if m >= 2:
                    level_exps(0, 0, (range(4), range(4, 7))[m - 2])
                act.wait_ge(S["acc_done"], 21 + m)
                if m:
                    act.wait_ge(S["mid_ready"], 4 + m)
                fn(ST[2][:, :], flat(ACC[m % 2]), ACT.Sigmoid, bias=col("b_glu", m)).then_inc(S["glu_sig"], 1)
                act.wait_ge(S["glu_zz"], 5 + m)
                fn(XBh[:, m, :], ST[3][:, :], ACT.Copy).then_inc(S["mid_hi_done"], 1)
            decay(0, 1)
            with own.loop(HEADS - 1, 8) as hd:
                head(hd, False)
            head(HEADS - 1, True)
            finish(1, "mlp", 0)

            def hidden(u, m):
                act.wait_ge(S["acc_free"], u)
                own(fn(ST[1][:, :], ST[0][:, :], ACT.Square))
                settle()
                fn(XBh[:, bass.ds(m, 1), :].rearrange("p a t -> p (a t)"), ST[1][:, :], ACT.Copy).then_inc(S["mid_hi_done"], 1)

            def mlp(name, norm_after, gain, g0):
                f0 = free_of(UNIT[name])[1]
                start = own.n
                with act.Fori(0, 4) as c:
                    with act.Fori(0, 8) as m:
                        own.n = c * 8 + m + start
                        hidden(c * 16 + m + f0, m)
                own.n = start + 32
                finish(norm_after, gain, g0)

            def embed(i, norm, nroot, after):
                u0 = UNIT[f"gate{i}"]
                act.wait_ge(S["acc_done"], u0)
                act.dma_start(PIN[:, :, :], a["p"][i, 0].rearrange("(t p) e -> p t e", p=P)).then_inc(S["p_loaded"], 16)
                root(nroot)
                for m in range(KT):
                    act.wait_ge(S["acc_free"], free_of(u0)[1] + m)
                    fn(GATE[:, m, :], ST[m % 2][:, :], ACT.Sigmoid).then_inc(S["gate_done"], 1)
                    if m in (2, 3):
                        k = m - 2
                        act.wait_ge(S["p_tr"], 2 * i + k + 1)
                        fn(PTh[:, k, :], flat(PS[:, 4 + 2 * k:6 + 2 * k, :]), ACT.Copy).then_inc(S["p_hi"], 1)
                if after:
                    finish(*after)

            mlp("mlp0", 2, "ple", 0)
            embed(0, 2, 1, (3, "mix", 8))
            root(2)
            for u in range(12):
                act.wait_ge(S["acc_free"], free_of(UNIT["qkv"])[1] + u)
                act.dma_start(qkv_dram[u * P:(u + 1) * P, :], ST[u % 2][:, :]).then_inc(spilled[u % 2], 16)
            with act.Fori(0, KVH // 2) as gp:

                def v_copy(par):
                    act.wait_ge(S["at_vt_done"], gp * 2 + (par + 1 + CREDIT))
                    fn(AVT[:, par, :, :].rearrange("p n d -> p (n d)"), PS[:, 3, :], ACT.Copy).then_inc(S["at_vt_copied"], 1)

                def exps(i):
                    s, lo = i % RING, (P if i % NB == 0 else 0)
                    act.wait_ge(S["at_max"], gp * BODY + (i + 1))
                    for j in range(4):
                        fn(SC[:, s, j, lo:], SC[:, s, j, lo:], ACT.Exp, bias=sm[:, 0, s, j:j + 1], accum_out=sm[:, 1, s, j:j + 1])
                    fn(sm[:, 3, s, :], sm[:, 3, s, :], ACT.Exp).then_inc(S["at_exp"], 1)

                def probs(i):
                    halves = slice(1, 2) if i % NB == 0 else slice(0, 2)
                    act.wait_ge(S["at_pt_done"], gp * BODY + (i + 1 + CREDIT))
                    fn(PT[:, halves, :, :].rearrange("p h j t -> p (h j t)"),
                       PS[:, halves, :].rearrange("p h t -> p (h t)"), ACT.Copy).then_inc(S["at_pt_copied"], 1)

                def out_high(i):
                    n = i % NB
                    act.wait_ge(S["at_o_done"], gp * BODY + (i + 1))
                    settle()
                    fn(XBh[:, bass.ds(gp * 4 + 2 * (i // NB), 2), n * P:(n + 1) * P],
                       PS[:, 2 + i % 2, 0:256].rearrange("p (j t) -> p j t", t=P), ACT.Copy).then_inc(S["at_o_hi"], 1)

                v_copy(0)
                for i in range(BODY + AHEAD + 1):
                    if i == NB:
                        v_copy(1)
                    if AHEAD <= i < BODY + AHEAD:
                        probs(i - AHEAD)
                    if i < BODY:
                        exps(i)
                    if i > AHEAD:
                        out_high(i - AHEAD - 1)
            finish(4, "mlp", 8)
            mlp("mlp1", 5, "ple", 8)
            embed(1, 5, 3, None)
            for e in range(2 * KT + 3):
                if e < 2 * KT:
                    half, m = e // KT, e % KT
                    t = slice(half * HALF, (half + 1) * HALF)
                    act.wait_ge(S["last_h"], e + 1)
                    if e >= 2:
                        act.wait_ge(S["last_sq_used"], e - 1)
                    fn(SQ[:, e % 2 * HALF:(e % 2 + 1) * HALF], H[:, m, t], ACT.Square).then_inc(S["last_sq"], 1)
                    fn(HG[:, m, t], H[:, m, t], ACT.Identity, scale=col("final", m)).then_inc(S["last_gain"], 1)
                if e >= 3:
                    half, m = (e - 3) // KT, (e - 3) % KT
                    act.wait_ge(S["last_tr"], e - 2)
                    fn(OT[:, 4 * half:4 * half + 4, m * P:(m + 1) * P], PS[:, 4 + (e - 3) % 3, :].rearrange("p (n f) -> p n f", f=P), ACT.Copy)\
                        .then_inc(S["last_copied"], 1)
                for half in range(2):
                    if e == (KT + 4, 2 * KT + 2)[half]:
                        act.wait_ge(S["last_var"], half + 1)
                        fn(root_mean[:, half, :], root_mean[:, half, :], ACT.Sqrt).then_inc(S["last_root"], 1)
                        act.wait_ge(S["last_root"], half + 1)
                        act.wait_ge(S["last_copied"], KT * (half + 1))
                        for j in (1, 3):
                            o = OT[:, 4 * half + j, :]
                            fn(o, o, ACT.Identity, scale=root_mean[:, half, j:j + 1]).then_inc(S["scaled_act"], 1)

        @block.vector
        def _(dve):
            for name in "hg_lvl_read hg_state hg_ss_read at_o_done_lo at_scored sq_used".split():
                dve.nop().then_inc(S[name], CREDIT)
            own = Own(dve, S["dve_step"])
            tt = dve.tensor_tensor

            def tile(buf, m):
                return buf[:, m, :] if isinstance(m, int) else buf[:, bass.ds(m, 1), :].rearrange("p a t -> p (a t)")

            def add_squares(norm, m):
                dve.wait_ge(S["sq_done"], m + (8 * norm + 1))
                tt(SUMSQ[:, :], SUMSQ[:, :], SQ[:, :], ALU.add).then_inc(S["sq_used"], 1)
                dve.wait_ge(S["sq_used"], m + (8 * norm + 1 + CREDIT))

            def low(norm, m, g):
                dve.wait_ge(S["x_hi_done"], m + (8 * norm + 1))
                dve.scalar_tensor_tensor(tile(XAl, m), tile(H, m), COLS[:, bass.ds(m + g, 1)], tile(XAh, m).bitcast(F32),
                                         ALU.mult, ALU.subtract).then_inc(S["x_ready"], 1)
                add_squares(norm, m)

            def start_norm():
                own(dve.memset(SUMSQ[:, :], 0.0))

            def end_norm():
                dve.nop().then_inc(S["sumsq_ready"], 1)

            def variance(norm):
                dve.wait_ge(S["ss_done"], norm + 1)
                dve.tensor_scalar(ST[0][:, :], flat(PS[:, 4:6, :]), 1.0 / D, EPS, ALU.mult, ALU.add).then_inc(S["ss_read"], 1)
                dve.wait_ge(S["ss_read"], norm + 1)

            def rstd(norm, n):
                variance(norm)
                dve.reciprocal(ST[1][:, :], ST[0][:, :]).then_inc(S["rcp_done"], 1)
                dve.wait_ge(S["rstd_done"], n + 1)

            def rstd_squared(norm):
                variance(norm)
                own(dve.reciprocal(RSTD[:, :], ST[0][:, :]))

            def x_copy(k):
                dve.wait_ge(S["x_tr_done"], k + 1)
                dve.tensor_copy(H[:, k, 0:HALF], PS[:, 4 + 2 * (k % 2), :]).then_inc(S["x_tr_dve"], 1)
                dve.nop().then_inc(S["h_ready"], 1)

            start_norm()
            dve.wait_ge(S["cols_done"], 1)
            dve.tensor_copy(COLS[:, 0:16], PS[:, 0, 0:16]).then_inc(S["cols_ready"], 1)
            x_copy(0)
            for k in range(KT):
                if k + 1 < KT:
                    x_copy(k + 1)
                dve.wait_ge(S["x_hi_done"], k + 1)
                dve.scalar_tensor_tensor(XAl[:, k, :], H[:, k, :], col("mix", k), XAh[:, k, :].bitcast(F32),
                                         ALU.mult, ALU.subtract).then_inc(S["x_ready"], 1)
                add_squares(0, k)
            end_norm()
            dve.wait_ge(S["cols_done"], 2)
            dve.tensor_copy(COLS[:, 16:N_ROWS], PS[:, 6, 16:N_ROWS]).then_inc(S["cols_ready"], 1)
            dve.wait_ge(S["cols_ready"], 2)
            x4 = COLS[:, ROW["lb"]:ROW["lb"] + HEADS]
            tt(floor_[:, :], x4, x4, ALU.subtract).then_inc(S["lb_in"], 1)
            rstd(0, 0)
            for u in range(4):
                dve.wait_ge(S["acc_done"], u + 1)
                if u >= 2:
                    dve.wait_ge(spilled[u % 2], 16)
                tt(ST[u % 2][:, :].rearrange("p (j c) -> p j c", j=L), flat(ACC[u % 2]).rearrange("p (c j) -> p j c", j=L),
                   RSTD[:, :].rearrange("p (c j) -> p j c", j=L), ALU.mult).then_inc(S["acc_free"], 1)
            dve.wait_ge(S["s5_raw_loaded"], 16 * 13)
            p = lambda i: PR[:, i, :]
            ph = lambda i: phase[:, i, :]
            colp = lambda name: COLS[:, ROW[name]:ROW[name] + PAIRS]

            def t2(o, x, y, op):
                own(tt(o, x, y, op))

            def ts(o, x, c, op, c2=None, op2=None):
                own(dve.tensor_scalar(o, x, c, c2, op) if op2 is None else dve.tensor_scalar(o, x, c, c2, op, op2))

            def cmul(or_, oi, ar, ai, br, bi, tmp):
                t2(tmp, ai, bi, ALU.mult)
                t2(or_, ar, br, ALU.mult)
                t2(or_, or_, tmp, ALU.subtract)
                t2(tmp, ai, br, ALU.mult)
                t2(oi, ar, bi, ALU.mult)
                t2(oi, oi, tmp, ALU.add)

            lr, li = p(0), colp("lam_im")
            ts(lr, colp("lam_re"), -1e-4, ALU.min)
            dve.nop().then_inc(S["s5_dve"], 1)
            dve.wait_ge(S["s5_act"], 1)
            t2(p(8), li, p(1), ALU.mult)
            t2(p(2), lr, p(1), ALU.mult)
            dve.nop().then_inc(S["s5_dve"], 1)
            ts(p(9), p(8), 1.0 / TWO_PI, ALU.mult, MAGIC, ALU.add)
            ts(p(9), p(9), MAGIC, ALU.subtract)
            c1 = 6.28125
            c2 = float(np.float32(TWO_PI - c1))
            c3 = float(TWO_PI - c1 - c2)
            own(dve.scalar_tensor_tensor(p(5), p(9), -c1, p(8), ALU.mult, ALU.add))
            own(dve.scalar_tensor_tensor(p(5), p(9), -c2, p(5), ALU.mult, ALU.add))
            own(dve.scalar_tensor_tensor(p(5), p(9), -c3, p(5), ALU.mult, ALU.add))
            ts(p(5), p(5), 3.14159, ALU.min, -3.14159, ALU.max)
            dve.nop().then_inc(S["s5_dve"], 1)
            dve.wait_ge(S["s5_act"], 3)
            sn, cs, ar, ai = p(6), p(10), p(11), p(12)
            t2(cs, p(7), p(7), ALU.mult)
            ts(cs, cs, -2.0, ALU.mult, 1.0, ALU.add)
            t2(ar, p(3), cs, ALU.mult)
            t2(ai, p(3), sn, ALU.mult)
            xr, den, zr, zi, tmp = p(13), p(14), p(15), p(16), p(17)
            ts(xr, ar, -1.0, ALU.add)
            t2(den, lr, lr, ALU.mult)
            t2(tmp, li, li, ALU.mult)
            t2(den, den, tmp, ALU.add)
            own(dve.reciprocal(den, den))
            t2(zr, xr, lr, ALU.mult)
            t2(tmp, ai, li, ALU.mult)
            t2(zr, zr, tmp, ALU.add)
            t2(zr, zr, den, ALU.mult)
            t2(zi, ai, lr, ALU.mult)
            t2(tmp, xr, li, ALU.mult)
            t2(zi, zi, tmp, ALU.subtract)
            t2(zi, zi, den, ALU.mult)
            own(dve.memset(PW[:, 0, :, 0:1], 1.0))
            own(dve.memset(PW[:, 1, :, 0:1], 0.0))
            for j in range(L):
                cmul(PW[:, 0, :, j + 1], PW[:, 1, :, j + 1], PW[:, 0, :, j], PW[:, 1, :, j], ar, ai, tmp)

            def wide(ap, n):
                return ap.unsqueeze(2).to_broadcast([P, PAIRS, n])

            tq = PT1[:, 0:PAIRS * GRP].rearrange("p (q h) -> p q h", h=GRP)
            cmul(BB[:, 0], BB[:, 1], BRAW[:, 0], BRAW[:, 1], wide(zr, GRP), wide(zi, GRP), tq)
            for j in range(L):
                pw = [wide(PW[:, r, :, L - 1 - j], GRP) for r in range(2)]
                cmul(BA[:, 0, :, j, :], BA[:, 1, :, j, :], BB[:, 0], BB[:, 1], pw[0], pw[1], tq)
            dve.nop().then_inc(S["s5_ba_ready"], 1)
            dve.wait_ge(S["s5_c_tr"], 1)
            for h in range(2):
                src = PS[:, 4, h * 256:(h + 1) * 256].rearrange("p (r q h) -> p r q h", r=2, h=GRP)
                own(dve.tensor_copy(C0[:, 0, 8 * h:8 * h + 8, :], src[:, 0]))
                ts(C0[:, 1, 8 * h:8 * h + 8, :], src[:, 1], -1.0, ALU.mult)
            for j in range(L):
                pr_, pi_ = (wide(PW[:, r, :, j + 1], GRP) for r in range(2))
                t2(tq, C0[:, 1], pi_, ALU.mult)
                t2(CA[:, 0, :, j, :], C0[:, 0], pr_, ALU.mult)
                t2(CA[:, 0, :, j, :], CA[:, 0, :, j, :], tq, ALU.add)
                t2(tq, C0[:, 0], pi_, ALU.mult)
                t2(CA[:, 1, :, j, :], C0[:, 1], pr_, ALU.mult)
                t2(CA[:, 1, :, j, :], CA[:, 1, :, j, :], tq, ALU.subtract)
            dve.nop().then_inc(S["s5_ca_ready"], 1)
            dve.wait_ge(S["h_spilled"], 16)
            own(dve.memset(TOEP[:, :, :], 0.0))
            dve.nop().then_inc(S["s5_t_zeroed"], 1)
            w8r, w8i = ph(0), ph(1)
            ur, ui, vr, vi = p(18), p(19), p(20), p(21)
            cmul(ur, ui, cs, sn, cs, sn, tmp)
            cmul(vr, vi, ur, ui, ur, ui, tmp)
            cmul(w8r, w8i, vr, vi, vr, vi, tmp)
            own(dve.tensor_copy(ph(2), p(4)))
            dve.wait_ge(S["s5_g_copied"], 8)
            own(dve.memset(ROT[:, 0, :, 0:1], 1.0))
            own(dve.memset(ROT[:, 1, :, 0:1], 0.0))
            n = 1
            while n < CH:
                wr, wi = (wide(ph(r), n) for r in range(2))
                tr = ST[2][:, 0:PAIRS * n].rearrange("p (q c) -> p q c", c=n)
                cmul(ROT[:, 0, :, n:2 * n], ROT[:, 1, :, n:2 * n], ROT[:, 0, :, 0:n], ROT[:, 1, :, 0:n], wr, wi, tr)
                if 2 * n < CH:
                    cmul(ph(3), ph(4), ph(0), ph(1), ph(0), ph(1), ph(5))
                    own(dve.tensor_copy(ph(0), ph(3)))
                    own(dve.tensor_copy(ph(1), ph(4)))
                n *= 2
            dve.wait_ge(S["s5_t_loaded"], 16 * 8)
            t1 = ST[2][:, :].rearrange("p (q c) -> p q c", c=CH)
            t2_ = ST[3][:, :].rearrange("p (q c) -> p q c", c=CH)
            for half in range(2):
                q = slice(8 * half, 8 * half + 8)
                er, ei = (flat(PS[:, 4 + 2 * r:6 + 2 * r, :]).rearrange("p (q c) -> p q c", c=CH) for r in range(2))
                dve.wait_ge(S["s5_end_done"], half + 1)
                t2(t1, ei, ROT[:, 1, q, :], ALU.mult)
                t2(CR[:, 0, q, :], er, ROT[:, 0, q, :], ALU.mult)
                t2(CR[:, 0, q, :], CR[:, 0, q, :], t1, ALU.add)
                t2(t1, er, ROT[:, 1, q, :], ALU.mult)
                t2(CR[:, 1, q, :], ei, ROT[:, 0, q, :], ALU.mult)
                dve.nop().then_inc(S["s5_end_read"], 1)
                t2(CR[:, 1, q, :], CR[:, 1, q, :], t1, ALU.subtract)
            for r in range(2):
                for q in range(PAIRS):
                    ins = dve.tensor_tensor_scan(CR[:, r, q, :], ph(2)[:, q:q + 1].to_broadcast([P, CH]), CR[:, r, q, :],
                                                 0.0, ALU.mult, ALU.add)
                    own(ins)
            for half in range(2):
                q = slice(8 * half, 8 * half + 8)
                t2(t1, CR[:, 1, q, :], ROT[:, 1, q, :], ALU.mult)
                t2(t2_, CR[:, 0, q, :], ROT[:, 1, q, :], ALU.mult)
                t2(CR[:, 0, q, :], CR[:, 0, q, :], ROT[:, 0, q, :], ALU.mult)
                t2(CR[:, 0, q, :], CR[:, 0, q, :], t1, ALU.subtract)
                t2(CR[:, 1, q, :], CR[:, 1, q, :], ROT[:, 0, q, :], ALU.mult)
                t2(CR[:, 1, q, :], CR[:, 1, q, :], t2_, ALU.add)
            dve.nop().then_inc(S["s5_states_ready"], 1)
            dve.wait_ge(S["lb_exp"], 1)
            own(dve.reciprocal(keep[:, :], floor_[:, :]))
            t2(keep[:, :], keep[:, :], floor_[:, :], ALU.mult)
            t2(floor_[:, :], keep[:, :], keep[:, :], ALU.subtract)
            ts(keep[:, :], floor_[:, :], -1.0, ALU.mult, 1.0, ALU.add)
            ts(floor_[:, :], floor_[:, :], 1e-30, ALU.max)
            dve.wait_ge(S["s5_ut_loaded"], 16)

            def gelu_in(k):
                y = YT[:, k, :]
                c = float(np.sqrt(2.0 / np.pi))
                dve.wait_ge(yt_loaded[k], 16)
                own(dve.scalar_tensor_tensor(y, UT[:, k, :], col("d", k), y, ALU.mult, ALU.add))
                if k:
                    dve.wait_ge(S["glu_tanh"], k)
                t2(ST[2][:, :], y, y, ALU.mult)
                ts(ST[2][:, :], ST[2][:, :], c * 0.044715, ALU.mult, c, ALU.add)
                tt(ST[2][:, :], ST[2][:, :], y, ALU.mult).then_inc(S["glu_tanh_in"], 1)

            def gelu_out(k):
                y = YT[:, k, :]
                dve.wait_ge(S["glu_tanh"], k + 1)
                dve.scalar_tensor_tensor(y, ST[3][:, :], 1.0, y, ALU.add, ALU.mult).then_inc(S["glu_zz"], 1)

            def z_low(k):
                dve.wait_ge(S["mid_hi_done"], k + 1)
                dve.scalar_tensor_tensor(XBl[:, 4 + k, :].rearrange("p (c j) -> p j c", j=L), YT[:, k, :].rearrange("p (j c) -> p j c", j=L),
                                         0.5, XBh[:, 4 + k, :].bitcast(F32).rearrange("p (c j) -> p j c", j=L),
                                         ALU.mult, ALU.subtract).then_inc(S["mid_ready"], 1)

            gelu_in(0)
            for k in range(4):
                if k < 3:
                    gelu_in(k + 1)
                gelu_out(k)
                if k:
                    z_low(k - 1)
            z_low(3)

            def told(ins, name):
                ins.then_inc(S[name], 1)

            def clamp_f(hd, half):
                dve.wait_ge(S["hg_f_loaded"], hd * 32 + (16 * half + 16))
                t2(TA[:, :], F[:, :], RSTD[:, half * HALF:(half + 1) * HALF], ALU.mult)
                told(dve.tensor_scalar(TA[:, :], TA[:, :], -80.0, None, ALU.max), "hg_f")

            def cumulate(hd, half):
                un = hd * 2 + half
                dve.wait_ge(S["hg_sigmoid_f"], un + 1)
                told(dve.scalar_tensor_tensor(KK[:, half, :], TB[:, :], keep[:, bass.ds(hd, 1)], TC[:, :], ALU.mult, ALU.mult), "hg_k_made")
                dve.wait_ge(S["hg_log_f"], un + 1)
                for c in range(4):
                    t = slice(c * P, (c + 1) * P)
                    ins = dve.tensor_tensor_scan(BC[:, t], ones[:, :], TD[:, t], 0.0, ALU.mult, ALU.add)
                told(ins, "hg_cumulated")
                dve.wait_ge(S["hg_cumulated"], un + 1)
                bc = BC[:, :].rearrange("p (c t) -> p c t", t=P)
                told(tt(TD[:, :].rearrange("p (c t) -> p c t", t=P), bc, bc[:, :, P - 1:P].to_broadcast([P, 4, P]), ALU.subtract), "hg_to_end")

            def level_exponents(half, some):
                for l in some:
                    w = LEVELS[l]
                    b4, lv = (ap.rearrange("p (n two w) -> p n two w", two=2, w=w) for ap in (BC[:, :], LVL[:, half, l, :]))
                    ref = b4[:, :, 0, w - 1:w].to_broadcast([P, HALF // (2 * w), w])
                    tt(lv[:, :, 0, :], b4[:, :, 0, :], ref, ALU.subtract)
                    told(tt(lv[:, :, 1, :], ref, b4[:, :, 1, :], ALU.subtract), "hg_level")

            def mean_square(hd, half):
                dve.wait_ge(S["hg_ss"], hd * 2 + (half + 1))
                if half == 1:
                    dve.wait_ge(S["hg_y_low"], hd * 2 + 1)
                told(dve.tensor_scalar(PD[:, :], PS[:, 1, :], 1.0 / P, EPS, ALU.mult, ALU.add), "hg_ss_read")

            def product(hd, half):
                o = OUTH[:, half, :]
                dve.wait_ge(S["hg_rstd"], hd * 2 + (half + 1))
                if half == 0:
                    dve.wait_ge(S["hg_gate_made"], hd + 1)
                t2(o, o, PD[:, :], ALU.mult)
                told(dve.scalar_tensor_tensor(PD[:, :], o, COLS[:, bass.ds(hd + ROW["head_norm"], 1)], PC[:, half * HALF:(half + 1) * HALF],
                                              ALU.mult, ALU.mult), "hg_y_ready")

            def y_low(hd, half):
                dve.wait_ge(S["hg_y_high"], hd * 2 + (half + 1))
                t = slice(half * HALF, (half + 1) * HALF)
                hi, lo = (x[:, bass.ds(hd + 4, 1), t].rearrange("p a t -> p (a t)") for x in (XBh, XBl))
                told(tt(lo, PD[:, :], hi.bitcast(F32), ALU.subtract), "hg_y_low")

            def head(hd, last):
                for c in range(NB):
                    half, b = c // 4, c % 2
                    dve.wait_ge(S["hg_lvl_done"], hd * NB + (c + 1))
                    told(tt(MP[:, b, :, :].rearrange("p l t -> p (l t)"), flat(PS[:, 4 + 2 * b:6 + 2 * b, :]),
                            MASK[:, :, :].rearrange("p l t -> p (l t)"), ALU.mult), "hg_lvl_read")
                    dve.wait_ge(S["hg_lvl_read"], hd * NB + (c + 1 + CREDIT))
                    told(dve.tensor_reduce(AT[:, b, :], MP[:, b, :, :].rearrange("p l t -> p t l"), X, ALU.add), "hg_att")
                    if c:
                        dve.wait_ge(S["hg_ds_done"], hd * (NB - 1) + c)
                        if c == 1:
                            told(dve.tensor_copy(SS[:, :], PS[:, 2, 0:P]), "hg_state")
                        else:
                            end = ENDS[:, (c - 1) // 4, (c - 1) % 4:(c - 1) % 4 + 1]
                            dve.wait_ge(S["hg_state"], hd * (NB - 1) + (c - 1 + CREDIT))
                            told(dve.scalar_tensor_tensor(SS[:, :], SS[:, :], end, PS[:, 2, 0:P], ALU.mult, ALU.add), "hg_state")
                    if c == 5:
                        mean_square(hd, 0)
                    if c == 7:
                        product(hd, 0)
                    if not (last and half == 1):
                        if c % 4 == 0:
                            cumulate(hd + half, 1 - half)
                        if c % 4 == 1:
                            level_exponents(1 - half, range(4))
                        if c % 4 == 2:
                            level_exponents(1 - half, range(4, 7))
                            if not last:
                                clamp_f(hd + 1, half)
                y_low(hd, 0)
                mean_square(hd, 1)
                product(hd, 1)
                y_low(hd, 1)

            for m in range(4):
                if m == 0:
                    clamp_f(0, 0)
                if m == 1:
                    cumulate(0, 0)
                if m >= 2:
                    level_exponents(0, (range(4), range(4, 7))[m - 2])
                dve.wait_ge(S["glu_sig"], m + 1)
                dve.nop().then_inc(S["acc_free"], 1)
                dve.scalar_tensor_tensor(ST[3][:, :].rearrange("p (c j) -> p c j", j=L), YT[:, m, :].rearrange("p (j c) -> p c j", j=L),
                                         0.5, ST[2][:, :].rearrange("p (c j) -> p c j", j=L), ALU.mult, ALU.mult).then_inc(S["glu_zz"], 1)
                dve.wait_ge(S["mid_hi_done"], 5 + m)
                tt(XBl[:, m, :], ST[3][:, :], XBh[:, m, :].bitcast(F32), ALU.subtract).then_inc(S["mid_ready"], 1)
            clamp_f(0, 1)
            dve.wait_ge(S["mid_ready"], 8)
            dve.wait_ge(S["masks_ready"], 1)
            with own.loop(HEADS - 1, 4) as hd:
                head(hd, False)
            head(HEADS - 1, True)

            def residual(u0, norm, gain, factor):
                start_norm()
                with dve.Fori(0, KT // 2) as i:
                    for b in range(2):
                        m = i * 2 + b
                        dve.wait_ge(S["acc_done"], i * 2 + (u0 + b + 1))
                        h = tile(H, m)
                        if factor is None:
                            tt(h, flat(ACC[b]), h, ALU.add).then_inc(S["acc_free"], 1)
                            dve.wait_ge(S["acc_free"], i * 2 + (free_of(u0)[1] + b))
                        else:
                            tt(ST[0][:, :], flat(ACC[b]), factor, ALU.mult).then_inc(S["acc_free"], 1)
                            dve.wait_ge(S["acc_free"], i * 2 + (free_of(u0)[1] + b))
                            tt(h, h, ST[0][:, :], ALU.add).then_inc(S["h_ready"], 1)
                        if factor is None:
                            dve.nop().then_inc(S["h_ready"], 1)
                        low(norm, m, ROW[gain[0]] + gain[1])
                end_norm()

            def mlp(name, norm, mid0, after):
                u0 = UNIT[name]
                f0 = free_of(u0)[1]

                def up(c):
                    with dve.Fori(0, 4) as i:
                        for b in range(2):
                            off = c * 16 + i * 2 + b
                            dve.wait_ge(S["acc_done"], off + (u0 + 1))
                            dve.tensor_scalar(ST[0][:, :], flat(ACC[b]), 0.0, None, ALU.max).then_inc(S["acc_free"], 1)
                            dve.wait_ge(S["mid_hi_done"], c * 8 + i * 2 + (mid0 + b + 1))
                            tt(tile(XBl, i * 2 + b), ST[1][:, :], tile(XBh, i * 2 + b).bitcast(F32), ALU.subtract).then_inc(S["mid_ready"], 1)

                def down(c):
                    base_ = own.n
                    with dve.Fori(0, 4) as i:
                        for b in range(2):
                            off = c * 16 + i * 2 + b
                            dve.wait_ge(S["acc_done"], off + (u0 + 9))
                            tt(ST[0][:, :], flat(ACC[b]), RSTD[:, :], ALU.mult).then_inc(S["acc_free"], 1)
                            dve.wait_ge(S["acc_free"], off + (f0 + 8))
                            h = tile(H, i * 2 + b)
                            own.n = c * 8 + i * 2 + (start + b)
                            own(tt(h, h, ST[0][:, :], ALU.add))

                with dve.Fori(0, 4) as i:
                    for b in range(2):
                        dve.wait_ge(S["acc_done"], i * 2 + (u0 + b + 1))
                        dve.tensor_scalar(ST[0][:, :], flat(ACC[b]), 0.0, None, ALU.max).then_inc(S["acc_free"], 1)
                        dve.wait_ge(S["mid_hi_done"], i * 2 + (mid0 + b + 1))
                        tt(tile(XBl, i * 2 + b), ST[1][:, :], tile(XBh, i * 2 + b).bitcast(F32), ALU.subtract).then_inc(S["mid_ready"], 1)
                dve.wait_ge(S["mid_ready"], mid0 + 8)
                rstd_squared(norm)
                start = own.n
                with dve.Fori(0, 3) as c:
                    down(c)
                    up(c + 1)
                own.n = start + 24
                residual(u0 + 56, *after, RSTD[:, :])

            def embed(i, norm, nroot, after, gain):
                u0 = UNIT[f"gate{i}"]
                rstd(norm, nroot)
                for m in range(KT):
                    dve.wait_ge(S["acc_done"], u0 + m + 1)
                    if m >= 2:
                        dve.wait_ge(S["gate_done"], 8 * i + m - 1)
                    tt(ST[m % 2][:, :], flat(ACC[m % 2]), RSTD[:, :], ALU.mult).then_inc(S["acc_free"], 1)
                    dve.wait_ge(S["acc_free"], free_of(u0)[1] + m)
                    if m in (2, 3):
                        k = m - 2
                        dve.wait_ge(S["p_hi"], 2 * i + k + 1)
                        tt(PTl[:, k, :], flat(PS[:, 4 + 2 * k:6 + 2 * k, :]), PTh[:, k, :].bitcast(F32), ALU.subtract).then_inc(S["p_ready"], 1)
                dve.wait_ge(S["gate_done"], 8 * i + 8)
                if i == 1:
                    return
                u0 = UNIT[f"up{i}"]
                start_norm()
                for m in range(KT):
                    dve.wait_ge(S["acc_done"], u0 + m + 1)
                    tt(ST[0][:, :], flat(ACC[m % 2]), GATE[:, m, :], ALU.mult).then_inc(S["acc_free"], 1)
                    dve.wait_ge(S["acc_free"], free_of(u0)[1] + m)
                    tt(H[:, m, :], H[:, m, :], ST[0][:, :], ALU.add).then_inc(S["h_ready"], 1)
                    low(after, m, ROW[gain[0]] + gain[1])
                end_norm()

            dve.wait_ge(S["h_restored"], 16)
            residual(UNIT["out"], 1, ("mlp", 0), None)
            mlp("mlp0", 1, 8, (2, ("ple", 0)))
            embed(0, 2, 1, 3, ("mix", 8))
            rstd(3, 2)
            for u in range(12):
                dve.wait_ge(S["acc_done"], UNIT["qkv"] + u + 1)
                dve.wait_ge(spilled[u % 2], 16 * (10 + u // 2))
                tt(ST[u % 2][:, :], flat(ACC[u % 2]), RSTD[:, :], ALU.mult).then_inc(S["acc_free"], 1)
            dve.wait_ge(S["dist_ready"], 1)
            dve.wait_ge(S["slopes_ready"], 1)
            dve.wait_ge(S["sinks_loaded"], 16)
            ts(neg_sink[:, :], sink[:, :], -1.0, ALU.mult)
            with own.loop(KVH // 2, AT_STEPS) as gp:

                def bias(par):
                    dve.wait_ge(at_loaded[par], gp * 64 + 64)
                    for s, j in enumerate((0, 2, 1, 3)):
                        own(dve.tensor_scalar(BIAS[:, par, s, :], dist[:, :], slope[:, bass.ds(gp * 8 + (4 * par + j), 1)], None, ALU.mult))

                def score(i):
                    par, s, lo = i // NB, i % RING, (P if i % NB == 0 else 0)
                    sc = SC[:, s, :, lo:]
                    dve.wait_ge(S["at_qk_done"], gp * BODY + (i + 1 + CREDIT))
                    dve.wait_ge(S["at_pt_done"], gp * BODY + (max(i - RING + 1, 0) + CREDIT))
                    b = i % 2
                    ps = PS[:, 4 + 2 * b:6 + 2 * b, :].rearrange("p a (j s) -> p (a j) s", j=2)[:, :, lo:]
                    dve.scalar_tensor_tensor(sc, ps, HD ** -0.5, BIAS[:, par, :, lo:], ALU.mult, ALU.add).then_inc(S["at_scored"], 1)
                    dve.wait_ge(S["at_scored"], gp * BODY + (i + 1 + CREDIT))
                    own(dve.tensor_reduce(sm[:, 0, s, :], sc, X, ALU.max))
                    sk, neg = (x[:, bass.ds(gp * 8 + 4 * par, 4)].rearrange("p (j r) -> p r j", r=2) for x in (sink, neg_sink))
                    mx, ex = (sm[:, k, s, :].rearrange("p (r j) -> p r j", r=2) for k in (0, 3))
                    own(dve.scalar_tensor_tensor(mx, mx, -1.0, neg, ALU.mult, ALU.min))
                    tt(ex, sk, mx, ALU.add).then_inc(S["at_max"], 1)

                def denominators(i):
                    s = i % RING
                    dve.wait_ge(S["at_exp"], gp * BODY + (i + 1))
                    own(tt(sm[:, 2, s, :], sm[:, 1, s, :], sm[:, 3, s, :], ALU.add))
                    dve.reciprocal(sm[:, 2, s, :], sm[:, 2, s, :]).then_inc(S["at_den"], 1)

                def out_low(i):
                    n = i % NB
                    dve.wait_ge(S["at_o_hi"], gp * BODY + (i + 1))
                    t, heads = slice(n * P, (n + 1) * P), bass.ds(gp * 4 + 2 * (i // NB), 2)
                    tt(XBl[:, heads, t], PS[:, 2 + i % 2, 0:256].rearrange("p (j t) -> p j t", t=P),
                       XBh[:, heads, t].bitcast(F32), ALU.subtract).then_inc(S["at_o_done_lo"], 1)

                for i in range(BODY + AHEAD + 1):
                    if i < BODY:
                        if i % NB == 0:
                            bias(i // NB)
                        score(i)
                    if i > AHEAD:
                        out_low(i - AHEAD - 1)
                    if 1 <= i <= BODY:
                        denominators(i - 1)
            residual(UNIT["wo"], 4, ("mlp", 8), None)
            mlp("mlp1", 4, 40, (5, ("ple", 8)))
            embed(1, 5, 3, None, None)
            start_norm()

            def sum_squares(e):
                half = e // KT
                t = slice(half * HALF, (half + 1) * HALF)
                dve.wait_ge(S["last_sq"], e + 1)
                if e >= 1:
                    dve.wait_ge(S["last_sq_used"], e)
                tt(SUMSQ[:, t], SUMSQ[:, t], SQ[:, e % 2 * HALF:(e % 2 + 1) * HALF], ALU.add).then_inc(S["last_sq_used"], 1)

            def scale(half):
                rm = root_mean[:, half, :]
                dve.wait_ge(S["last_ss"], half + 1)
                own(dve.tensor_scalar(rm, PS[:, 7, half * 16:(half + 1) * 16:4], 1.0 / D, EPS, ALU.mult, ALU.add))
                dve.reciprocal(rm, rm).then_inc(S["last_var"], 1)
                dve.wait_ge(S["last_root"], half + 1)
                dve.wait_ge(S["last_copied"], KT * (half + 1))
                for j in (0, 2):
                    o = OT[:, 4 * half + j, :]
                    dve.tensor_scalar(o, o, rm[:, j:j + 1], None, ALU.mult).then_inc(S["scaled_dve"], 1)

            for e in range(2 * KT):
                half, m = e // KT, e % KT
                t = slice(half * HALF, (half + 1) * HALF)
                part = ST[0][:, e % 2 * HALF:(e % 2 + 1) * HALF]
                dve.wait_ge(S["last_done"], e + 1)
                tt(part, PS[:, e % 4, :], GATE[:, m, t], ALU.mult).then_inc(S["last_free"], 1)
                dve.wait_ge(S["last_free"], e + 1)
                tt(H[:, m, t], H[:, m, t], part, ALU.add).then_inc(S["last_h"], 1)
                if e:
                    sum_squares(e - 1)
                if e == KT + 4:
                    scale(0)
            sum_squares(2 * KT - 1)
            scale(1)


_SHAPES = dict(
    x=(1, T, D), p=(2, 1, T, PLE), mix_norm=(2, D), mlp_norm=(2, D), ple_norm=(2, D), final_norm=(D,),
    w_in_even=(1, D, 5 * S5W), w_out_even=(1, D, D), s5_lam_re=(1, GROUPS, STATES), s5_lam_im=(1, GROUPS, STATES),
    s5_log_dt=(1, GROUPS), s5_b_re=(1, GROUPS, STATES, GRP), s5_b_im=(1, GROUPS, STATES, GRP),
    s5_c_re=(1, GROUPS, GRP, STATES), s5_c_im=(1, GROUPS, GRP, STATES), s5_d=(1, GROUPS, GRP),
    s5_w_glu=(1, S5W, S5W), s5_b_glu=(1, S5W), hgrn_lb_logits=(1, S5W), hgrn_norm=(1, HEADS, P),
    w_qkv_odd=(1, D, 12 * P), w_o_odd=(1, D, D), attn_sinks=(1, QH), w_mlp_in=(2, D, FF), w_mlp_out=(2, FF, D),
    w_ple_up=(2, PLE, D), w_ple_gate=(2, D, D))


def kernel(**inputs):
    import concourse.bacc as bacc
    from concourse.bass_utils import run_bass_kernel_spmd

    nc = bacc.Bacc("TRN2", target_bir_lowering=False, num_devices=1)
    arrays = {f"{n}_in": np.ascontiguousarray(inputs[n]) for n in _SHAPES}
    a = {n: nc.dram_tensor(f"{n}_in", shape, F32, kind="ExternalInput").ap() for n, shape in _SHAPES.items()}
    out = nc.dram_tensor("out", (1, T, D), F32, kind="ExternalOutput").ap()
    build(nc, a, out)
    return run_bass_kernel_spmd(nc, [arrays], core_ids=[0]).results[0]["out"]
```
